# Optimizing a Trainium2 kernel written in Bass

```python
import math
import jax
import jax.numpy as jnp
from jax import lax
import numpy as np

D_MODEL = 1024
BATCH = 1
SEQ = 512
DEPTH = 2

GRID_W = 64
CTX_LEN = 256
N_MIXERS = 2
N_MLA_LAYERS = (DEPTH + 1) // 2
N_GDN_LAYERS = DEPTH // 2
DEEPNORM_ALPHA = (2.0 * DEPTH) ** 0.25
DEEPNORM_BETA = (8.0 * DEPTH) ** -0.25
N_MOD = 6
LN_EPS = 1e-5
RMS_EPS = 1e-6

MLA_HEADS = D_MODEL // 128
MLA_Q_RANK = D_MODEL // 2
MLA_KV_RANK = D_MODEL // 4
MLA_NOPE = 128
MLA_ROPE = 64
MLA_V = 128
MLA_IN_W = MLA_Q_RANK + MLA_KV_RANK + MLA_ROPE
MLA_SCALE = (MLA_NOPE + MLA_ROPE) ** -0.5
Q_BLOCK = 128
ROPE_THETA = 10000.0

GDN_K_HEADS = D_MODEL // 128
GDN_V_HEADS = 2 * GDN_K_HEADS
GDN_DK = 128
GDN_DV = 128
GDN_KW = GDN_K_HEADS * GDN_DK
GDN_VW = GDN_V_HEADS * GDN_DV
GDN_QKV_W = 2 * GDN_KW + GDN_VW
GDN_IN_W = GDN_QKV_W + GDN_VW + 4 * GDN_V_HEADS
GDN_CONV = 5
CHUNK = 64

D_FF = int(math.ceil(8 * D_MODEL / 3 / 256)) * 256


def layer_norm(x, g, b):
    xf = x.astype(jnp.float32)
    mu = jnp.mean(xf, axis=-1, keepdims=True)
    var = jnp.mean(jnp.square(xf - mu), axis=-1, keepdims=True)
    return ((xf - mu) * lax.rsqrt(var + LN_EPS) * g + b).astype(x.dtype)

def rms_norm(x, g):
    xf = x.astype(jnp.float32)
    y = xf * lax.rsqrt(jnp.mean(jnp.square(xf), axis=-1, keepdims=True) + RMS_EPS) * g
    return y.astype(x.dtype)

def l2_norm(x):
    xf = x.astype(jnp.float32)
    return (xf * lax.rsqrt(jnp.sum(jnp.square(xf), axis=-1, keepdims=True) + RMS_EPS)).astype(x.dtype)

def modulate(h, shift, scale):
    return h * (1 + scale) + shift

def axial_rope_tables(n_tokens):
    rows = n_tokens // GRID_W
    row = jnp.broadcast_to(jnp.arange(rows)[:, None], (rows, GRID_W)).reshape(-1).astype(jnp.float32)
    col = jnp.broadcast_to(jnp.arange(GRID_W)[None, :], (rows, GRID_W)).reshape(-1).astype(jnp.float32)
    n_freq = MLA_ROPE // 4
    axis_dim = MLA_ROPE // 2
    inv_freq = ROPE_THETA ** (-(2.0 * jnp.arange(n_freq, dtype=jnp.float32)) / axis_dim)
    ang = jnp.concatenate([row[:, None] * inv_freq, col[:, None] * inv_freq], axis=-1)
    return jnp.cos(ang), jnp.sin(ang)

def apply_axial_rope(u, cos, sin):
    B, T, H, _ = u.shape
    f = MLA_ROPE // 4
    u = u.reshape(B, T, H, 2, 2, f)
    u1, u2 = u[..., 0, :], u[..., 1, :]
    cs = cos.reshape(1, T, 1, 2, f).astype(u.dtype)
    sn = sin.reshape(1, T, 1, 2, f).astype(u.dtype)
    out = jnp.stack([u1 * cs - u2 * sn, u2 * cs + u1 * sn], axis=-2)
    return out.reshape(B, T, H, MLA_ROPE)

def softmax_attend(q, k, v):
    s = jnp.einsum('bqhd,bkhd->bhqk', q, k).astype(jnp.float32) * MLA_SCALE
    p = jax.nn.softmax(s, axis=-1).astype(v.dtype)
    return jnp.einsum('bhqk,bkhd->bqhd', p, v)

def blockwise_attend(q, k, v):
    B, T, H, dq = q.shape
    qb = jnp.moveaxis(q.reshape(B, T // Q_BLOCK, Q_BLOCK, H, dq), 1, 0)
    o = lax.map(lambda blk: softmax_attend(blk, k, v), qb)
    return jnp.moveaxis(o, 0, 1).reshape(B, T, H, v.shape[-1])

def mla_project(h, w_in, q_norm, kv_norm, w_q_up, w_kv_up, rope):
    B, T, _ = h.shape
    lat = h @ w_in
    cq = rms_norm(lat[..., :MLA_Q_RANK], q_norm)
    ckv = rms_norm(lat[..., MLA_Q_RANK:MLA_Q_RANK + MLA_KV_RANK], kv_norm)
    k_rope = lat[..., MLA_Q_RANK + MLA_KV_RANK:][:, :, None, :]
    q = (cq @ w_q_up).reshape(B, T, MLA_HEADS, MLA_NOPE + MLA_ROPE)
    kv = (ckv @ w_kv_up).reshape(B, T, MLA_HEADS, MLA_NOPE + MLA_V)
    q_nope, q_rope = q[..., :MLA_NOPE], q[..., MLA_NOPE:]
    k_nope, v = kv[..., :MLA_NOPE], kv[..., MLA_NOPE:]
    if rope is not None:
        cos, sin = rope
        q_rope = apply_axial_rope(q_rope, cos, sin)
        k_rope = apply_axial_rope(k_rope, cos, sin)
    k_rope = jnp.broadcast_to(k_rope, (B, T, MLA_HEADS, MLA_ROPE))
    q = jnp.concatenate([q_nope, q_rope], axis=-1)
    k = jnp.concatenate([k_nope, k_rope], axis=-1)
    return q, k, v

def mla_mixer(h_ctx, h_lat, w_in, q_norm, kv_norm, w_q_up, w_kv_up, w_out, rope):
    q_c, k_c, v_c = mla_project(h_ctx, w_in, q_norm, kv_norm, w_q_up, w_kv_up, None)
    q_l, k_l, v_l = mla_project(h_lat, w_in, q_norm, kv_norm, w_q_up, w_kv_up, rope)
    o_c = softmax_attend(q_c, k_c, v_c)
    o_l = blockwise_attend(q_l, jnp.concatenate([k_c, k_l], axis=1), jnp.concatenate([v_c, v_l], axis=1))

    def out(o):
        B, T = o.shape[:2]
        return o.reshape(B, T, MLA_HEADS * MLA_V) @ w_out

    return out(o_c), out(o_l)

def short_conv(u, w):
    out = lax.conv_general_dilated(u, w[:, None, :], window_strides=(1,),
                                   padding=[(GDN_CONV // 2, GDN_CONV // 2)],
                                   dimension_numbers=('NWC', 'WIO', 'NWC'),
                                   feature_group_count=u.shape[-1])
    return jax.nn.silu(out)

def gated_delta_chunked(q, k, v, beta, g, s0):
    B, T, H, dk = q.shape
    dv = v.shape[-1]
    n = T // CHUNK
    f32 = jnp.float32

    def chunks(a):
        return jnp.moveaxis(a.astype(f32).reshape((B, n, CHUNK) + a.shape[2:]), 3, 1)

    qc, kc, vc, bc, gc = chunks(q), chunks(k), chunks(v), chunks(beta), chunks(g)
    gcum = jnp.cumsum(gc, axis=-1)
    idx = jnp.arange(CHUNK)
    incl = idx[:, None] >= idx[None, :]
    strict = idx[:, None] > idx[None, :]
    diff = gcum[..., :, None] - gcum[..., None, :]
    decay = jnp.where(incl, jnp.exp(jnp.where(incl, diff, 0.0)), 0.0)
    kb = kc * bc[..., None]
    lmat = jnp.where(strict, jnp.einsum('bhnid,bhnjd->bhnij', kb, kc) * decay, 0.0)
    a = lmat + jnp.eye(CHUNK, dtype=f32)
    rhs = jnp.concatenate([vc * bc[..., None], kb * jnp.exp(gcum)[..., None]], axis=-1)
    sol = lax.linalg.triangular_solve(a, rhs, left_side=True, lower=True, unit_diagonal=True)
    u, w = sol[..., :dv], sol[..., dv:]
    attn = jnp.einsum('bhnid,bhnjd->bhnij', qc, kc) * decay
    q_dec = qc * jnp.exp(gcum)[..., None]
    k_dec = kc * jnp.exp(gcum[..., -1:] - gcum)[..., None]
    g_last = jnp.exp(gcum[..., -1])
    xs = tuple(jnp.moveaxis(t, 2, 0) for t in (w, u, q_dec, k_dec, attn, g_last))

    def step(S, inp):
        w_i, u_i, qd_i, kd_i, a_i, gl_i = inp
        v_new = u_i - jnp.einsum('bhck,bhkv->bhcv', w_i, S)
        o_i = jnp.einsum('bhck,bhkv->bhcv', qd_i, S) + jnp.einsum('bhij,bhjv->bhiv', a_i, v_new)
        S = S * gl_i[..., None, None] + jnp.einsum('bhck,bhcv->bhkv', kd_i, v_new)
        return S, o_i

    s_final, o = lax.scan(step, s0, xs)
    o = jnp.transpose(o, (1, 0, 3, 2, 4)).reshape(B, T, H, dv)
    return o.astype(v.dtype), s_final

def gdn_project(h, w_in, conv_w, a_log, dt_bias):
    B, T, _ = h.shape
    proj = h @ w_in
    qkv = short_conv(proj[..., :GDN_QKV_W], conv_w)
    rep = GDN_V_HEADS // GDN_K_HEADS
    q = l2_norm(qkv[..., :GDN_KW].reshape(B, T, GDN_K_HEADS, GDN_DK)) * (GDN_DK ** -0.5)
    k = l2_norm(qkv[..., GDN_KW:2 * GDN_KW].reshape(B, T, GDN_K_HEADS, GDN_DK))
    q = jnp.repeat(q, rep, axis=2)
    k = jnp.repeat(k, rep, axis=2)
    v = qkv[..., 2 * GDN_KW:].reshape(B, T, GDN_V_HEADS, GDN_DV)
    z = proj[..., GDN_QKV_W:GDN_QKV_W + GDN_VW].reshape(B, T, GDN_V_HEADS, GDN_DV)
    ba = proj[..., GDN_QKV_W + GDN_VW:].astype(jnp.float32).reshape(B, T, 2, 2, GDN_V_HEADS)
    beta = jax.nn.sigmoid(ba[..., 0, :])
    g = -jnp.exp(a_log.astype(jnp.float32)) * jax.nn.softplus(ba[..., 1, :] + dt_bias.astype(jnp.float32))
    return q, k, v, z, beta, g

def gdn_mixer(h_ctx, h_lat, w_in, conv_w, a_log, dt_bias, norm_w, w_out):
    ctx_t = gdn_project(h_ctx, w_in, conv_w, a_log, dt_bias)
    lat_t = gdn_project(h_lat, w_in, conv_w, a_log, dt_bias)
    s0 = jnp.zeros((h_lat.shape[0], GDN_V_HEADS, GDN_DK, GDN_DV), jnp.float32)

    def one_direction(d):
        flip = (lambda a: jnp.flip(a, axis=1)) if d == 1 else (lambda a: a)

        def run(t, s_init):
            q, k, v, _, beta, g = t
            o, s_fin = gated_delta_chunked(flip(q), flip(k), flip(v), flip(beta[:, :, d]), flip(g[:, :, d]), s_init)
            return flip(o), s_fin

        o_ctx, s_ctx = run(ctx_t, s0)
        o_lat, _ = run(lat_t, s_ctx)
        return o_ctx, o_lat

    oc_f, ol_f = one_direction(0)
    oc_b, ol_b = one_direction(1)

    def finish(o, z):
        B, T = o.shape[:2]
        y = rms_norm(o, norm_w) * jax.nn.silu(z)
        return y.reshape(B, T, GDN_VW) @ w_out

    return finish(oc_f + oc_b, ctx_t[3]), finish(ol_f + ol_b, lat_t[3])

def swiglu(h, w_in, w_out):
    gate, up = jnp.split(h @ w_in, 2, axis=-1)
    return (jax.nn.silu(gate) * up) @ w_out

def first_inputs(seed: int = 0) -> dict:
    key = jax.random.key(seed)
    ks = jax.random.split(key, 24)
    f32 = jnp.float32

    def nrm(i, shape, std=1.0):
        return std * jax.random.normal(ks[i], shape, f32)

    D = D_MODEL
    nA, nB = N_MLA_LAYERS, N_GDN_LAYERS
    a_log = jnp.log(jax.random.uniform(ks[20], (nB, 2, GDN_V_HEADS), f32, 1.0, 16.0))
    dt = jnp.exp(jax.random.uniform(ks[21], (nB, 2, GDN_V_HEADS), f32, math.log(1e-3), math.log(1e-1)))
    dt_bias = dt + jnp.log(-jnp.expm1(-dt))
    return {
        'x': nrm(0, (BATCH, SEQ, D)),
        'c': nrm(1, (BATCH, D)),
        'ctx': nrm(2, (BATCH, CTX_LEN, D)),
        'c_ctx': nrm(3, (D,)),
        'w_mod': nrm(4, (DEPTH, D, N_MOD * D), D ** -0.5),
        'b_mod': nrm(5, (DEPTH, N_MOD * D), 0.01),
        'ln1_g': 1.0 + nrm(6, (DEPTH, D), 0.02),
        'ln1_b': nrm(7, (DEPTH, D), 0.01),
        'ln2_g': 1.0 + nrm(8, (DEPTH, D), 0.02),
        'ln2_b': nrm(9, (DEPTH, D), 0.01),
        'w_ffn_in': nrm(10, (DEPTH, D, 2 * D_FF), D ** -0.5),
        'w_ffn_out': nrm(11, (DEPTH, D_FF, D), DEEPNORM_BETA * D_FF ** -0.5),
        'mla_w_in': nrm(12, (nA, D, MLA_IN_W), D ** -0.5),
        'mla_q_norm': 1.0 + nrm(13, (nA, MLA_Q_RANK), 0.02),
        'mla_kv_norm': 1.0 + nrm(14, (nA, MLA_KV_RANK), 0.02),
        'mla_w_q_up': nrm(15, (nA, MLA_Q_RANK, MLA_HEADS * (MLA_NOPE + MLA_ROPE)), MLA_Q_RANK ** -0.5),
        'mla_w_kv_up': nrm(16, (nA, MLA_KV_RANK, MLA_HEADS * (MLA_NOPE + MLA_V)), MLA_KV_RANK ** -0.5),
        'mla_w_out': nrm(17, (nA, MLA_HEADS * MLA_V, D), DEEPNORM_BETA * (MLA_HEADS * MLA_V) ** -0.5),
        'gdn_w_in': nrm(18, (nB, D, GDN_IN_W), D ** -0.5),
        'gdn_conv': nrm(19, (nB, GDN_CONV, GDN_QKV_W), GDN_CONV ** -0.5),
        'gdn_a_log': a_log,
        'gdn_dt_bias': dt_bias,
        'gdn_norm': 1.0 + nrm(22, (nB, GDN_DV), 0.02),
        'gdn_w_out': nrm(23, (nB, GDN_VW, D), DEEPNORM_BETA * GDN_VW ** -0.5),
    }

def first_block(x, c, ctx, c_ctx, w_mod, b_mod, ln1_g, ln1_b, ln2_g, ln2_b, w_ffn_in, w_ffn_out,
              mla_w_in, mla_q_norm, mla_kv_norm, mla_w_q_up, mla_w_kv_up, mla_w_out,
              gdn_w_in, gdn_conv, gdn_a_log, gdn_dt_bias, gdn_norm, gdn_w_out):
    rope = axial_rope_tables(x.shape[1])
    h_lat, h_ctx = x, ctx
    for i in range(DEPTH):
        last = i == DEPTH - 1
        mod_lat = jnp.split((jax.nn.silu(c) @ w_mod[i] + b_mod[i])[:, None, :], N_MOD, axis=-1)
        mod_ctx = jnp.split(jax.nn.silu(c_ctx) @ w_mod[i] + b_mod[i], N_MOD, axis=-1)
        u_ctx = modulate(h_ctx, mod_ctx[0], mod_ctx[1])
        u_lat = modulate(h_lat, mod_lat[0], mod_lat[1])
        j = i // N_MIXERS
        if i % N_MIXERS == 0:
            y_ctx, y_lat = mla_mixer(u_ctx, u_lat, mla_w_in[j], mla_q_norm[j], mla_kv_norm[j],
                                     mla_w_q_up[j], mla_w_kv_up[j], mla_w_out[j], rope)
        else:
            y_ctx, y_lat = gdn_mixer(u_ctx, u_lat, gdn_w_in[j], gdn_conv[j], gdn_a_log[j],
                                     gdn_dt_bias[j], gdn_norm[j], gdn_w_out[j])
        h_lat = layer_norm(DEEPNORM_ALPHA * h_lat + mod_lat[2] * y_lat, ln1_g[i], ln1_b[i])
        f_lat = swiglu(modulate(h_lat, mod_lat[3], mod_lat[4]), w_ffn_in[i], w_ffn_out[i])
        h_lat = layer_norm(DEEPNORM_ALPHA * h_lat + mod_lat[5] * f_lat, ln2_g[i], ln2_b[i])
        if not last:
            h_ctx = layer_norm(DEEPNORM_ALPHA * h_ctx + mod_ctx[2] * y_ctx, ln1_g[i], ln1_b[i])
            f_ctx = swiglu(modulate(h_ctx, mod_ctx[3], mod_ctx[4]), w_ffn_in[i], w_ffn_out[i])
            h_ctx = layer_norm(DEEPNORM_ALPHA * h_ctx + mod_ctx[5] * f_ctx, ln2_g[i], ln2_b[i])
    return h_lat


N_MIXERS_2 = 3
EXPAND = 2
E_WIDTH = EXPAND * D_MODEL
HEAD_DIM = 128
N_Q_HEADS = E_WIDTH // HEAD_DIM
N_KV_HEADS = max(1, N_Q_HEADS // 4)
Q_PER_KV = N_Q_HEADS // N_KV_HEADS
KV_WIDTH = N_KV_HEADS * HEAD_DIM
WINDOW = 128
ATTN_BLOCK = 128
S5_GROUP = 16
S5_GROUPS = E_WIDTH // S5_GROUP
S5_STATE = 64
S5_CHUNK = 128
HG_HEAD_DIM = 128
HG_HEADS = E_WIDTH // HG_HEAD_DIM
HG_CHUNK = 64
ATTN_IN = 2 * E_WIDTH + 2 * KV_WIDTH
S5_IN = 2 * E_WIDTH
HG_IN = 5 * E_WIDTH
NORM_EPS = 1e-5
NEG_INF = -1e30


def layer_norm_2(x, g, b):
    xf = x.astype(jnp.float32)
    mu = jnp.mean(xf, -1, keepdims=True)
    var = jnp.mean(jnp.square(xf - mu), -1, keepdims=True)
    y = (xf - mu) * lax.rsqrt(var + NORM_EPS) * g.astype(jnp.float32) + b.astype(jnp.float32)
    return y.astype(x.dtype)

def grid_positions(n_tokens):
    rows = n_tokens // GRID_W
    row = jnp.repeat(jnp.arange(rows, dtype=jnp.float32), GRID_W)
    col = jnp.tile(jnp.arange(GRID_W, dtype=jnp.float32), rows)
    return row, col

def rope_2d(x, row, col):
    half = x.shape[-1] // 2
    nf = half // 2
    inv_freq = jnp.power(ROPE_THETA, -jnp.arange(nf, dtype=jnp.float32) / nf)
    xf = x.astype(jnp.float32)

    def rotate(xp, pos):
        ang = pos[:, None] * inv_freq[None, :]
        cos = jnp.cos(ang)[None, :, None, :]
        sin = jnp.sin(ang)[None, :, None, :]
        x1, x2 = xp[..., :nf], xp[..., nf:]
        return jnp.concatenate([x1 * cos - x2 * sin, x2 * cos + x1 * sin], -1)

    return jnp.concatenate([rotate(xf[..., :half], row), rotate(xf[..., half:], col)], -1).astype(x.dtype)

def softmax_with_sink(s, sink):
    sk = jnp.broadcast_to(sink[None, :, :, None, None], s.shape[:-1] + (1,))
    return jax.nn.softmax(jnp.concatenate([s, sk], -1), axis=-1)[..., :-1]

def attention_mixer(p, pc, sink, row, col, ctx_out):
    bsz, n_lat, _ = p.shape
    n_ctx = pc.shape[1]

    def split(t):
        b_, l_ = t.shape[0], t.shape[1]
        q = t[..., :E_WIDTH].reshape(b_, l_, N_Q_HEADS, HEAD_DIM)
        k = t[..., E_WIDTH:E_WIDTH + KV_WIDTH].reshape(b_, l_, N_KV_HEADS, HEAD_DIM)
        v = t[..., E_WIDTH + KV_WIDTH:].reshape(b_, l_, N_KV_HEADS, HEAD_DIM)
        return q, k, v

    q, k, v = split(p)
    qc, kc, vc = split(pc)
    q = rope_2d(q, row, col).reshape(bsz, n_lat, N_KV_HEADS, Q_PER_KV, HEAD_DIM)
    k = rope_2d(k, row, col)
    qc = qc.reshape(bsz, n_ctx, N_KV_HEADS, Q_PER_KV, HEAD_DIM)
    scale = HEAD_DIM ** -0.5
    sink_r = sink.astype(jnp.float32).reshape(N_KV_HEADS, Q_PER_KV)

    n_blk = n_lat // ATTN_BLOCK
    n_key = ATTN_BLOCK + 2 * WINDOW
    qb = q.reshape(bsz, n_blk, ATTN_BLOCK, N_KV_HEADS, Q_PER_KV, HEAD_DIM).swapaxes(0, 1)
    pad = ((0, 0), (WINDOW, WINDOW), (0, 0), (0, 0))
    kp = jnp.pad(k, pad)
    vp = jnp.pad(v, pad)
    q_off = jnp.arange(ATTN_BLOCK)
    k_off = jnp.arange(n_key) - WINDOW

    def block(args):
        j, qj = args
        start = j * ATTN_BLOCK
        kj = lax.dynamic_slice_in_dim(kp, start, n_key, axis=1)
        vj = lax.dynamic_slice_in_dim(vp, start, n_key, axis=1)
        qpos = start + q_off
        kpos = start + k_off
        valid = ((jnp.abs(qpos[:, None] - kpos[None, :]) <= WINDOW)
                 & (kpos >= 0)[None, :] & (kpos < n_lat)[None, :])
        s_win = jnp.einsum('bqhgd,bkhd->bhgqk', qj, kj, preferred_element_type=jnp.float32) * scale
        s_win = jnp.where(valid, s_win, NEG_INF)
        s_ctx = jnp.einsum('bqhgd,bchd->bhgqc', qj, kc, preferred_element_type=jnp.float32) * scale
        pr = softmax_with_sink(jnp.concatenate([s_win, s_ctx], -1), sink_r).astype(vj.dtype)
        return (jnp.einsum('bhgqk,bkhd->bqhgd', pr[..., :n_key], vj)
                + jnp.einsum('bhgqc,bchd->bqhgd', pr[..., n_key:], vc))

    o = lax.map(block, (jnp.arange(n_blk), qb)).swapaxes(0, 1).reshape(bsz, n_lat, E_WIDTH)
    if not ctx_out:
        return o, None
    sc = jnp.einsum('bqhgd,bkhd->bhgqk', qc, kc, preferred_element_type=jnp.float32) * scale
    prc = softmax_with_sink(sc, sink_r).astype(vc.dtype)
    oc = jnp.einsum('bhgqk,bkhd->bqhgd', prc, vc).reshape(bsz, n_ctx, E_WIDTH)
    return o, oc

def flip_seq(t, rev):
    return jnp.flip(t, axis=1) if rev else t

def _linrec_combine(e1, e2):
    a1, b1 = e1
    a2, b2 = e2
    return a1 * a2, a2 * b1 + b2

def s5_discretise(lam_re, lam_im, log_step, b_re, b_im, c_re, c_im):
    lam = lax.complex(lam_re.astype(jnp.float32), lam_im.astype(jnp.float32))
    dt = jnp.exp(log_step.astype(jnp.float32))[:, None]
    abar = jnp.exp(lam * dt)
    bmat = lax.complex(b_re.astype(jnp.float32), b_im.astype(jnp.float32))
    bbar = ((abar - 1.0) / lam)[..., None] * bmat
    cmat = lax.complex(c_re.astype(jnp.float32), c_im.astype(jnp.float32))
    return abar, bbar, cmat

def s5_scan(u, abar, bbar, cmat, h0):
    bsz, n_tok, n_g, n_c = u.shape
    n_chunk = n_tok // S5_CHUNK
    uc = u.reshape(bsz, n_chunk, S5_CHUNK, n_g, n_c).swapaxes(0, 1)

    def step(h, u_blk):
        bu = jnp.einsum('btgn,gpn->btgp', u_blk.astype(jnp.complex64), bbar)
        bu = bu.at[:, 0].add(abar[None] * h)
        a = jnp.broadcast_to(abar, bu.shape)
        _, hs = lax.associative_scan(_linrec_combine, (a, bu), axis=1)
        y = jnp.einsum('btgp,gnp->btgn', hs, cmat).real
        return hs[:, -1], y

    h_last, ys = lax.scan(step, h0, uc)
    return ys.swapaxes(0, 1).reshape(bsz, n_tok, n_g, n_c), h_last

def s5_mixer(p, pc, lam_re, lam_im, log_step, b_re, b_im, c_re, c_im, d_skip, glu_w, glu_b):
    bsz, n_lat, _ = p.shape
    n_ctx = pc.shape[1]
    u = p.astype(jnp.float32).reshape(bsz, n_lat, S5_GROUPS, S5_GROUP)
    uc = pc.astype(jnp.float32).reshape(bsz, n_ctx, S5_GROUPS, S5_GROUP)
    d = d_skip.astype(jnp.float32).reshape(S5_GROUPS, S5_GROUP)
    y = d * u
    yc = d * uc
    for rev in (0, 1):
        abar, bbar, cmat = s5_discretise(lam_re[rev], lam_im[rev], log_step[rev],
                                         b_re[rev], b_im[rev], c_re[rev], c_im[rev])
        h0 = jnp.zeros((bsz, S5_GROUPS, S5_STATE), jnp.complex64)
        yc_dir, h_ctx = s5_scan(flip_seq(uc, rev), abar, bbar, cmat, h0)
        y_dir, _ = s5_scan(flip_seq(u, rev), abar, bbar, cmat, h_ctx)
        y = y + flip_seq(y_dir, rev)
        yc = yc + flip_seq(yc_dir, rev)
    w = glu_w.astype(jnp.float32)
    bias = glu_b.astype(jnp.float32)

    def glu(t, n):
        g = jax.nn.gelu(t.reshape(bsz, n, E_WIDTH))
        return (g * jax.nn.sigmoid(g @ w + bias)).astype(p.dtype)

    return glu(y, n_lat), glu(yc, n_ctx)

def hgrn2_scan(q, k, v, logf, s0):
    bsz, n_tok, n_h, _ = q.shape
    n_chunk = n_tok // HG_CHUNK
    mid = HG_CHUNK // 2
    order_mask = jnp.tril(jnp.ones((HG_CHUNK, HG_CHUNK), dtype=bool))

    def blocks(t):
        return t.reshape(bsz, n_chunk, HG_CHUNK, n_h, t.shape[-1]).transpose(1, 0, 3, 2, 4)

    def step(s, blk):
        qb, kb, vb, gb = blk
        b = jnp.cumsum(gb, axis=2)
        ref = b[:, :, mid:mid + 1]
        att = jnp.einsum('bhtk,bhsk->bhts', qb * jnp.exp(b - ref), kb * jnp.exp(ref - b))
        att = jnp.where(order_mask, att, 0.0)
        o = (jnp.einsum('bhts,bhsv->bhtv', att, vb)
             + jnp.einsum('bhtk,bhkv->bhtv', qb * jnp.exp(b), s))
        b_last = b[:, :, -1:]
        s = (jnp.exp(b_last[:, :, 0])[..., None] * s
             + jnp.einsum('bhsk,bhsv->bhkv', kb * jnp.exp(b_last - b), vb))
        return s, o

    s_last, outs = lax.scan(step, s0, (blocks(q), blocks(k), blocks(v), blocks(logf)))
    return outs.transpose(1, 0, 3, 2, 4).reshape(bsz, n_tok, n_h, v.shape[-1]), s_last

def hgrn2_mixer(p, pc, lb, norm_g):
    bsz, n_lat, _ = p.shape
    n_ctx = pc.shape[1]
    lbh = lb.astype(jnp.float32).reshape(HG_HEADS, HG_HEAD_DIM)

    def heads(t):
        t = t.astype(jnp.float32).reshape(t.shape[0], t.shape[1], 4, HG_HEADS, HG_HEAD_DIM)
        return t[:, :, 0], t[:, :, 1], t[:, :, 2], t[:, :, 3]

    q, f_fw, f_bw, v = heads(p)
    qc, fc_fw, fc_bw, vc = heads(pc)
    outs, outs_c = [], []
    for rev, (fl, flc) in enumerate(((f_fw, fc_fw), (f_bw, fc_bw))):
        f = lbh + (1.0 - lbh) * jax.nn.sigmoid(fl)
        fc = lbh + (1.0 - lbh) * jax.nn.sigmoid(flc)
        s0 = jnp.zeros((bsz, HG_HEADS, HG_HEAD_DIM, HG_HEAD_DIM), jnp.float32)
        oc_dir, s_ctx = hgrn2_scan(flip_seq(qc, rev), flip_seq(1.0 - fc, rev),
                                   flip_seq(vc, rev), flip_seq(jnp.log(fc), rev), s0)
        o_dir, _ = hgrn2_scan(flip_seq(q, rev), flip_seq(1.0 - f, rev),
                              flip_seq(v, rev), flip_seq(jnp.log(f), rev), s_ctx)
        outs.append(flip_seq(o_dir, rev))
        outs_c.append(flip_seq(oc_dir, rev))
    g = norm_g.astype(jnp.float32).reshape(HG_HEADS, HG_HEAD_DIM)

    def head_norm(t, n):
        t = t * lax.rsqrt(jnp.mean(jnp.square(t), -1, keepdims=True) + NORM_EPS) * g
        return t.reshape(bsz, n, E_WIDTH).astype(p.dtype)

    return head_norm(outs[0] + outs[1], n_lat), head_norm(outs_c[0] + outs_c[1], n_ctx)

def second_inputs(seed: int = 0) -> dict:
    key = jax.random.key(seed)
    ks = jax.random.split(key, 25)
    f32 = jnp.float32
    n_attn = len(range(0, DEPTH, N_MIXERS_2))
    n_s5 = len(range(1, DEPTH, N_MIXERS_2))
    n_hg = len(range(2, DEPTH, N_MIXERS_2))
    beta = (8.0 * DEPTH) ** -0.25

    def nrm(k, shape, std):
        return std * jax.random.normal(k, shape, f32)

    s5_shape = (n_s5, 2, S5_GROUPS, S5_STATE)
    lam_im_init = math.pi * jnp.arange(S5_STATE, dtype=f32)
    return {
        'x': nrm(ks[0], (BATCH, SEQ, D_MODEL), 1.0),
        'c': nrm(ks[1], (BATCH, D_MODEL), 1.0),
        'ctx': nrm(ks[2], (BATCH, CTX_LEN, D_MODEL), 1.0),
        'c_ctx': nrm(ks[3], (D_MODEL,), 1.0),
        'ada_w': nrm(ks[4], (DEPTH, D_MODEL, 3 * D_MODEL), 0.5 * D_MODEL ** -0.5),
        'ada_b': nrm(ks[5], (DEPTH, 3 * D_MODEL), 0.02),
        'ln_g': 1.0 + nrm(ks[6], (DEPTH, D_MODEL), 0.02),
        'ln_b': nrm(ks[7], (DEPTH, D_MODEL), 0.02),
        'w_out': nrm(ks[8], (DEPTH, E_WIDTH, D_MODEL), beta * E_WIDTH ** -0.5),
        'attn_w_in': nrm(ks[9], (n_attn, D_MODEL, ATTN_IN), D_MODEL ** -0.5),
        'attn_sink': nrm(ks[10], (n_attn, N_Q_HEADS), 0.5),
        's5_w_in': nrm(ks[11], (n_s5, D_MODEL, S5_IN), D_MODEL ** -0.5),
        's5_lam_re': -0.5 + nrm(ks[12], s5_shape, 0.01),
        's5_lam_im': lam_im_init + nrm(ks[13], s5_shape, 0.01),
        's5_log_step': jax.random.uniform(ks[14], (n_s5, 2, S5_GROUPS), f32, math.log(1e-3), math.log(1e-1)),
        's5_b_re': nrm(ks[15], (n_s5, 2, S5_GROUPS, S5_STATE, S5_GROUP), (2 * S5_GROUP) ** -0.5),
        's5_b_im': nrm(ks[16], (n_s5, 2, S5_GROUPS, S5_STATE, S5_GROUP), (2 * S5_GROUP) ** -0.5),
        's5_c_re': nrm(ks[17], (n_s5, 2, S5_GROUPS, S5_GROUP, S5_STATE), S5_STATE ** -0.5),
        's5_c_im': nrm(ks[18], (n_s5, 2, S5_GROUPS, S5_GROUP, S5_STATE), S5_STATE ** -0.5),
        's5_d': nrm(ks[19], (n_s5, E_WIDTH), 0.5),
        's5_glu_w': nrm(ks[20], (n_s5, E_WIDTH, E_WIDTH), E_WIDTH ** -0.5),
        's5_glu_b': nrm(ks[21], (n_s5, E_WIDTH), 0.02),
        'hg_w_in': nrm(ks[22], (n_hg, D_MODEL, HG_IN), D_MODEL ** -0.5),
        'hg_lb': nrm(ks[23], (DEPTH, E_WIDTH), 0.1),
        'hg_norm_g': 1.0 + nrm(ks[24], (n_hg, E_WIDTH), 0.02),
    }

def second_block(x, c, ctx, c_ctx, ada_w, ada_b, ln_g, ln_b, w_out, attn_w_in, attn_sink,
              s5_w_in, s5_lam_re, s5_lam_im, s5_log_step, s5_b_re, s5_b_im, s5_c_re, s5_c_im,
              s5_d, s5_glu_w, s5_glu_b, hg_w_in, hg_lb, hg_norm_g):
    n_lat = x.shape[1]
    row, col = grid_positions(n_lat)
    alpha = (2.0 * DEPTH) ** 0.25
    lb_w = jax.nn.softmax(hg_lb.astype(jnp.float32), axis=0)
    lb_all = jnp.cumsum(lb_w, axis=0) - lb_w[0:1]
    xc = ctx
    for i in range(DEPTH):
        kind, j = i % N_MIXERS_2, i // N_MIXERS_2
        last = i == DEPTH - 1
        mod = jax.nn.silu(c) @ ada_w[i] + ada_b[i]
        mod_c = jax.nn.silu(c_ctx) @ ada_w[i] + ada_b[i]
        shift, scale, gate = jnp.split(mod[:, None, :], 3, axis=-1)
        shift_c, scale_c, gate_c = jnp.split(mod_c, 3, axis=-1)
        h = x * (1.0 + scale) + shift
        hc = xc * (1.0 + scale_c) + shift_c
        w_in = (attn_w_in, s5_w_in, hg_w_in)[kind][j]
        pz = h @ w_in
        pzc = hc @ w_in
        p, z = pz[..., :-E_WIDTH], pz[..., -E_WIDTH:]
        pc, zc = pzc[..., :-E_WIDTH], pzc[..., -E_WIDTH:]
        if kind == 0:
            y, yc = attention_mixer(p, pc, attn_sink[j], row, col, not last)
        elif kind == 1:
            y, yc = s5_mixer(p, pc, s5_lam_re[j], s5_lam_im[j], s5_log_step[j], s5_b_re[j], s5_b_im[j],
                             s5_c_re[j], s5_c_im[j], s5_d[j], s5_glu_w[j], s5_glu_b[j])
        else:
            y, yc = hgrn2_mixer(p, pc, lb_all[i], hg_norm_g[j])
        x = layer_norm_2(alpha * x + gate * ((y * jax.nn.silu(z)) @ w_out[i]), ln_g[i], ln_b[i])
        if not last:
            xc = layer_norm_2(alpha * xc + gate_c * ((yc * jax.nn.silu(zc)) @ w_out[i]), ln_g[i], ln_b[i])
    return x


def setup_inputs(seed=0):
    out = dict(first_inputs(seed))
    for name, value in second_inputs(seed + 1).items():
        if name != "x":
            out[name + "_2"] = value
    return out


def reference(
    x, c, ctx, c_ctx, w_mod, b_mod, ln1_g, ln1_b, ln2_g, ln2_b, w_ffn_in, w_ffn_out, mla_w_in,
    mla_q_norm, mla_kv_norm, mla_w_q_up, mla_w_kv_up, mla_w_out, gdn_w_in, gdn_conv, gdn_a_log,
    gdn_dt_bias, gdn_norm, gdn_w_out, c_2, ctx_2, c_ctx_2, ada_w_2, ada_b_2, ln_g_2, ln_b_2,
    w_out_2, attn_w_in_2, attn_sink_2, s5_w_in_2, s5_lam_re_2, s5_lam_im_2, s5_log_step_2,
    s5_b_re_2, s5_b_im_2, s5_c_re_2, s5_c_im_2, s5_d_2, s5_glu_w_2, s5_glu_b_2, hg_w_in_2,
    hg_lb_2, hg_norm_g_2,
):
    x = first_block(
        x, c, ctx, c_ctx, w_mod, b_mod, ln1_g, ln1_b, ln2_g, ln2_b, w_ffn_in, w_ffn_out,
        mla_w_in, mla_q_norm, mla_kv_norm, mla_w_q_up, mla_w_kv_up, mla_w_out, gdn_w_in,
        gdn_conv, gdn_a_log, gdn_dt_bias, gdn_norm, gdn_w_out,
    )
    return second_block(
        x, c_2, ctx_2, c_ctx_2, ada_w_2, ada_b_2, ln_g_2, ln_b_2, w_out_2, attn_w_in_2,
        attn_sink_2, s5_w_in_2, s5_lam_re_2, s5_lam_im_2, s5_log_step_2, s5_b_re_2, s5_b_im_2,
        s5_c_re_2, s5_c_im_2, s5_d_2, s5_glu_w_2, s5_glu_b_2, hg_w_in_2, hg_lb_2, hg_norm_g_2,
    )


_drawn_inputs = setup_inputs


def setup_inputs(seed=0):
    import zlib

    import numpy as np

    out = dict(_drawn_inputs(seed))
    spreads = {}
    factors = {'ctx': 3.332,
     'b_mod': 6.288,
     'ln1_b': 4.061,
     'ln2_b': 3.774,
     'mla_q_norm': 8.0,
     'mla_kv_norm': 8.0,
     'gdn_norm': 8.0,
     'ctx_2': 8.0,
     'c_ctx_2': 5.061,
     'ada_b_2': 8.0,
     'attn_w_in_2': 2.947,
     'attn_sink_2': 8.0,
     's5_w_in_2': 4.284,
     's5_lam_re_2': 64.0,
     's5_lam_im_2': 64.0,
     's5_log_step_2': 64.0,
     's5_b_re_2': 64.0,
     's5_b_im_2': 64.0,
     's5_c_re_2': 64.0,
     's5_c_im_2': 64.0,
     's5_d_2': 4.739,
     's5_glu_w_2': 8.0,
     's5_glu_b_2': 64.0}
    for name, (base, spread) in spreads.items():
        noise = np.random.default_rng([zlib.crc32(name.encode()), seed]).standard_normal(out[name].shape)
        drawn = base * np.exp(spread * noise) if base else spread * noise
        out[name] = jnp.asarray(drawn.astype(out[name].dtype))
    for name, factor in factors.items():
        out[name] = (out[name] * factor).astype(out[name].dtype)
    return out
```

```python
import numpy as np
import concourse.bass as bass
from concourse import mybir

F32 = mybir.dt.float32
ACT = mybir.ActivationFunctionType
ALU = mybir.AluOpType
AX = mybir.AxisListType

D = 1024
LAT, CTX = 512, 256
T = LAT + CTX
KD = D // 128
GRID_W = 64
ALPHA = 4.0 ** 0.25
FF = 2816
KF = FF // 128
SLOT = KF * 128
HEADS = 8
MLA_SCALE = 192 ** -0.5
ATT_SCALE = 128 ** -0.5
BOTH = ((0, 512), (512, 768))
LATS = ((0, 512),)
LEVELS = 7


def pairs(eng, groups, body):
    for g in range(min(2, groups)):
        body(g, g, True)
    if groups > 3:
        with eng.Fori(1, groups // 2) as p:
            for s in range(2):
                body(p * 2 + s, s, False)
    if groups > 2 and groups % 2:
        body(groups - 1, 0, False)


def one(g):
    return bass.ds(g, 1)


def rows_of(dram, g):
    return dram[one(g), :, :].rearrange("o p n -> (o p) n")


PRODUCTS = [
    ("mod", 8, 2), ("mla_in", 8, 1), ("q_up", 4, 2), ("k_up", 2, 2), ("v_up", 2, 2), ("mla_out", 8, 2),
    ("ffn_in0", 8, 2), ("ffn_out0", KF, 1),
    ("gdn_qkv", 8, 2), ("gdn_ba", 8, 1), ("gdn_z", 8, 2), ("gdn_out", 16, 1), ("ffn_in1", 8, 2), ("ffn_out1", KF, 1),
    ("att_qk", 8, 2), ("att_v", 8, 2), ("att_z", 8, 2), ("att_out", 16, 1),
    ("s5_in", 8, 2), ("s5_glu", 16, 1), ("s5_z", 8, 2), ("s5_out", 16, 1),
]


class Core:

    def __init__(self, nc, ins):
        self.nc, self.ins = nc, ins
        self.sems, self.live = 0, []
        f = lambda name, *shape: nc.alloc_sbuf_tensor(name, [128, *shape], F32)
        self.h = f("h", KD, T)
        self.u = f("u", KD, T)
        self.ring = f("ring", 2, SLOT)
        self.tmp = f("tmp", 2, 2, T)
        self.mod = f("mod", 144, 4)
        self.vec = f("vec", ins["vecs"].shape[1])
        self.ones = f("ones", 128)
        self.ident = f("ident", 128)
        self.stat = f("stat", 2, T)
        self.area_size = (nc.sbuf_bytes_remaining // 4) - 64
        self.area = f("area", self.area_size)
        self.P = nc.alloc_psum_tensor("P", [128, 4, 1024], F32)
        self.ring_ready = [self.sem(f"ring_ready{s}") for s in range(2)]
        self.mm_done = self.sem("mm_done")
        self.live = []
        self.first = {}
        n = 0
        for name, _, _ in PRODUCTS:
            self.first[name] = n
            n += ins["w_" + name].shape[0]
        self.total = n

    def sem(self, name):
        self.sems += 1
        got = self.nc.alloc_semaphore(f"{name}_{self.sems}")
        self.live.append(got)
        return got

    def clear_sems(self):
        self.nc.clear_and_free_semaphores(self.live)
        self.nc.all_engine_barrier()
        self.live = []

    def view(self, at, *shape):
        n = int(np.prod(shape))
        assert at + n <= self.area_size, (at, shape, self.area_size)
        v = self.area[:, at:at + n]
        names = "abcd"[:len(shape)]
        if len(shape) > 1:
            v = v.rearrange(f"p ({' '.join(names)}) -> p {' '.join(names)}", **dict(zip(names[1:], shape[1:])))
        return v

    def load_slot(self, sp, name, g, slot):
        w = self.ins["w_" + name]
        n = w.shape[2]
        sp.dma_start(self.ring[:, slot, 0:n], rows_of(w, g)).then_inc(self.ring_ready[slot], 16)

    def prefetch(self, sp, name):
        order = [p[0] for p in PRODUCTS]
        i = order.index(name) + 1
        if i == len(order):
            return
        at = self.first[order[i]]
        for g in range(min(2, self.ins["w_" + order[i]].shape[0])):
            sp.wait_ge(self.mm_done, at + g - 1)
            self.load_slot(sp, order[i], g, (at + g) % 2)

    def shape_of(self, name):
        return next((kt, per) for n, kt, per in PRODUCTS if n == name)


def stream(c, sp, name):
    at, groups = c.first[name], c.ins["w_" + name].shape[0]

    def body(g, s, first):
        if not first:
            sp.wait_ge(c.mm_done, g + (at - 1))
            c.load_slot(sp, name, g, (at + s) % 2)
    pairs(sp, groups, body)
    c.prefetch(sp, name)


def dense(c, name, x, segs, act, vec=None, act_frees=True):
    nc = c.nc
    kt, per = c.shape_of(name)
    at, groups = c.first[name], c.ins["w_" + name].shape[0]
    act_done, vec_done = c.sem(name + "_act_done"), c.sem(name + "_vec_done")
    freed = act_done if act_frees else vec_done
    with nc.Block() as block:
        @block.sync
        def _(sp):
            stream(c, sp, name)

        @block.tensor
        def _(pe):
            def body(g, s, first):
                slot = (at + s) % 2
                pe.wait_ge(c.ring_ready[slot], (g - s) * 8 + 16 * ((at + s) // 2 + 1))
                if not first:
                    pe.wait_ge(freed, g - 1)
                for j in range(per):
                    for a, b in segs:
                        for k in range(kt):
                            last = nc.tensor.matmul(
                                c.P[:, 2 * s + j, a:b], c.ring[:, slot, (j * kt + k) * 128:(j * kt + k + 1) * 128],
                                x[:, k, a:b], start=k == 0, stop=k == kt - 1)
                last.then_inc(c.mm_done, 1)
            pairs(pe, groups, body)

        @block.scalar
        def _(eng):
            def body(g, s, first):
                eng.wait_ge(c.mm_done, g + (at + 1))
                if vec and not first:
                    eng.wait_ge(vec_done, g - 1)
                for j in range(per):
                    last = act(g, j, c.P[:, 2 * s + j, :], c.tmp[:, s, j, :])
                last.then_inc(act_done, 1)
            pairs(eng, groups, body)

        if vec:
            @block.vector
            def _(eng):
                def body(g, s, first):
                    eng.wait_ge(act_done, g + 1)
                    for j in range(per):
                        last = vec(g, j, c.P[:, 2 * s + j, :], c.tmp[:, s, j, :])
                    last.then_inc(vec_done, 1)
                pairs(eng, groups, body)


def dense_tokens(c, name, x, width, out):
    nc = c.nc
    kt, _ = c.shape_of(name)
    at, groups = c.first[name], c.ins["w_" + name].shape[0]
    copied = c.sem(name + "_copied")
    psum = c.P[:, :, :].rearrange("p a b -> p (a b)")
    with nc.Block() as block:
        @block.sync
        def _(sp):
            stream(c, sp, name)

        @block.tensor
        def _(pe):
            def body(g, s, first):
                slot = (at + s) % 2
                pe.wait_ge(c.ring_ready[slot], (g - s) * 8 + 16 * ((at + s) // 2 + 1))
                if not first:
                    pe.wait_ge(copied, g - 1)
                for t in range(T // 128):
                    for k in range(kt):
                        last = nc.tensor.matmul(
                            psum[:, 2048 * s + t * width:2048 * s + (t + 1) * width], x[:, k, t * 128:(t + 1) * 128],
                            c.ring[:, slot, k * width:(k + 1) * width], start=k == 0, stop=k == kt - 1)
                last.then_inc(c.mm_done, 1)
            pairs(pe, groups, body)

        @block.scalar
        def _(eng):
            def body(g, s, first):
                eng.wait_ge(c.mm_done, g + (at + 1))
                nc.scalar.activation(out[:, :, bass.ds(g * width, width)],
                                     psum[:, 2048 * s:2048 * s + T // 128 * width].rearrange("p (t n) -> p t n", n=width),
                                     ACT.Copy).then_inc(copied, 1)
            pairs(eng, groups, body)


def spread(ap, n, axis=1):
    return ap.unsqueeze(axis).broadcast_to([ap.shape[0], n, ap.shape[1]]) if axis == 1 else None


def normalise(c, name, src, kt, width, segs, eps, gain, shift=None, after=None):
    nc = c.nc
    inv = 1.0 / (kt * 128)
    s = {n: c.sem(f"{name}_{n}") for n in ("mean", "centred", "sq", "sq_used", "var", "sd", "rs", "unit", "affine")}
    ps_mean, ps_var = c.P[:, 0, 0:width], c.P[:, 1, 0:width]
    sq = [c.tmp[:, 0, 0, 0:width], c.tmp[:, 1, 0, 0:width]]
    sd, rs = c.stat[:, 0, 0:width], c.stat[:, 1, 0:width]
    x = src[:, 0:kt, 0:width]
    with nc.Block() as block:
        @block.tensor
        def _(pe):
            if shift is not None:
                for a, b in segs:
                    for k in range(kt):
                        last = nc.tensor.matmul(ps_mean[:, a:b], c.ones[:, :], src[:, k, a:b], start=k == 0, stop=k == kt - 1)
                last.then_inc(s["mean"], 1)
            for k in range(kt):
                pe.wait_ge(s["sq"], k + 1)
                for a, b in segs:
                    last = nc.tensor.matmul(ps_var[:, a:b], c.ones[:, :], sq[k % 2][:, a:b], start=k == 0, stop=k == kt - 1)
                last.then_inc(s["sq_used"], 1)

        @block.scalar
        def _(act):
            if shift is not None:
                act.wait_ge(s["centred"], 1)
            for k in range(kt):
                if k >= 2:
                    act.wait_ge(s["sq_used"], k - 1)
                nc.scalar.activation(sq[k % 2], src[:, k, 0:width], ACT.Square).then_inc(s["sq"], 1)
            act.wait_ge(s["var"], 1)
            nc.scalar.activation(sd, sd, ACT.Sqrt).then_inc(s["sd"], 1)
            if after:
                out, parts = after
                for k in range(kt):
                    act.wait_ge(s["affine"], k + 1)
                    for scale, add, a, b in parts:
                        nc.scalar.activation(out[:, k, a:b], src[:, k, a:b], ACT.Identity, scale=scale(k), bias=add(k))

        @block.vector
        def _(dve):
            if shift is not None:
                dve.wait_ge(s["mean"], 1)
                nc.vector.scalar_tensor_tensor(out=x, in0=spread(ps_mean, kt), scalar=-inv, in1=x,
                                               op0=ALU.mult, op1=ALU.add).then_inc(s["centred"], 1)
            dve.wait_ge(s["sq_used"], kt)
            nc.vector.tensor_scalar(sd, ps_var, inv, eps, ALU.mult, ALU.add).then_inc(s["var"], 1)
            dve.wait_ge(s["sd"], 1)
            nc.vector.reciprocal(rs, sd).then_inc(s["rs"], 1)
            dve.wait_ge(s["rs"], 1)
            nc.vector.tensor_tensor(x, x, spread(rs, kt), ALU.mult).then_inc(s["unit"], 1)
            dve.wait_ge(s["unit"], 1)
            for k in range(kt):
                if shift is not None:
                    nc.vector.tensor_scalar(src[:, k, 0:width], src[:, k, 0:width], gain(k), shift(k),
                                            ALU.mult, ALU.add).then_inc(s["affine"], 1)
                else:
                    nc.vector.tensor_scalar(src[:, k, 0:width], src[:, k, 0:width], gain(k), None,
                                            ALU.mult).then_inc(s["affine"], 1)


def turn(c, name, x, blocks, tables, perm):
    nc = c.nc
    landed, partner, turned, kept, done = (c.sem(f"{name}_{n}") for n in ("landed", "partner", "turned", "kept", "done"))
    cos, sin, perm_sb = tables[:, 0, :], tables[:, 1, :], tables[:, 2, 0:128]
    with nc.Block() as block:
        @block.sync
        def _(sp):
            sp.dma_start(tables[:, 0:2, :].rearrange("p a b -> p (a b)"), c.ins[perm[0]]).then_inc(landed, 16)
            sp.dma_start(perm_sb, c.ins[perm[1]]).then_inc(landed, 16)

        @block.tensor
        def _(pe):
            pe.wait_ge(landed, 32)
            for n in range(blocks):
                if n >= 4:
                    pe.wait_ge(turned, n - 3)
                nc.tensor.matmul(c.P[:, n % 4, 0:LAT], perm_sb, x[:, n, 0:LAT], start=True, stop=True).then_inc(partner, 1)

        @block.vector
        def _(dve):
            dve.wait_ge(landed, 32)
            for n in range(blocks):
                dve.wait_ge(partner, n + 1)
                if n >= 2:
                    dve.wait_ge(done, n - 1)
                nc.vector.tensor_tensor(c.tmp[:, n % 2, 0, 0:LAT], c.P[:, n % 4, 0:LAT], sin, ALU.mult).then_inc(turned, 1)
                nc.vector.tensor_tensor(x[:, n, 0:LAT], x[:, n, 0:LAT], cos, ALU.mult).then_inc(kept, 1)
                dve.wait_ge(turned, n + 1)
                dve.wait_ge(kept, n + 1)
                nc.vector.tensor_tensor(x[:, n, 0:LAT], x[:, n, 0:LAT], c.tmp[:, n % 2, 0, 0:LAT], ALU.add).then_inc(done, 1)


def attention(c, name, rounds, per, window, q, k, v, out, at, scale, rope=None, sink=None):
    nc = c.nc
    qs, vs = c.view(at, per, T), c.view(at + per * T, per, T // 128, 128)
    at += 2 * per * T
    if rope:
        rs = c.view(at, T)
        at += T
    prob, probT = c.tmp[:, 0, :, :], c.tmp[:, 1, :, :]
    small = c.stat[:, 0, 0:16].rearrange("p (a b) -> p a b", a=2)
    mask = None
    if window:
        mask = c.view(at, 3 * 128)
    units = []
    for j in range(per):
        for t in range(T // 128):
            if t >= LAT // 128:
                tiles = [4, 5]
            elif window:
                tiles = list(range(max(0, t - 1), min(4, t + 2))) + [4, 5]
            else:
                tiles = list(range(6))
            units.append((j, t, tiles))
    U = len(units)
    S = [c.P[:, 0, :], c.P[:, 1, :]]
    TP = c.P[:, 2, :]
    O = [c.P[:, 3, 0:128], c.P[:, 3, 512:640]]
    sem = {n: c.sem(f"{name}_{n}") for n in
           ("const", "staged", "head", "score", "masked", "top", "peak", "negpeak", "prob", "sinkexp", "total", "inv",
            "unit", "turned", "probT", "o", "ocopied")}
    with nc.Block() as block:
        if window:
            @block.sync
            def _(sp):
                sp.dma_start(mask, c.ins["window_mask"]).then_inc(sem["const"], 16)

        @block.gpsimd
        def _(pool):
            def body(i, s, first):
                for j in range(per):
                    if not first:
                        pool.wait_ge(sem["o"], (i - 1) * U + (j + 1) * (U // per))
                    elif i:
                        pool.wait_ge(sem["o"], (i - 1) * U + (j + 1) * (U // per))
                    if rope and j == 0:
                        if not (first and i == 0):
                            pool.wait_ge(sem["o"], i * U)
                        nc.gpsimd.tensor_copy(rs[:, :].unsqueeze(1), rope[0](i))
                    nc.gpsimd.tensor_copy(qs[:, j, :].unsqueeze(1), q(i, j))
                    nc.gpsimd.tensor_copy(vs[:, j, :, :], v(i, j)).then_inc(sem["staged"], 1)
            body(0, 0, True)
            with pool.Fori(1, rounds) as i:
                body(i, 0, False)

        @block.tensor
        def _(pe):
            def body(i, first):
                def score(n):
                    j, t, tiles = units[n]
                    w = 128 * (len(tiles) - 2)
                    if t == 0:
                        pe.wait_ge(sem["staged"], i * per + (j + 1))
                    if not (first and n < 2):
                        pe.wait_ge(sem["prob"], i * U + (n - 1))
                    segs = ([(512 - w, 512, tiles[0] * 128)] if w else []) + [(512, 768, 512)]
                    for a, b, key in segs:
                        last = nc.tensor.matmul(S[n % 2][:, a:b], qs[:, j, t * 128:t * 128 + 128],
                                                k(i, j, key, key + b - a), start=True, stop=rope is None)
                        if rope:
                            last = nc.tensor.matmul(S[n % 2][:, a:b], rs[64 * j:64 * j + 64, t * 128:t * 128 + 128],
                                                    rope[1](j, key, key + b - a), start=False, stop=True)
                    last.then_inc(sem["score"], 1)

                def flip(n):
                    pe.wait_ge(sem["unit"], i * U + (n + 1))
                    if not (first and n == 0):
                        pe.wait_ge(sem["probT"], i * U + n)
                    nb = len(units[n][2])
                    for b in range(nb):
                        a = 768 - 128 * nb + 128 * b
                        last = nc.tensor.transpose(TP[:, b * 128:b * 128 + 128], prob[:, n % 2, a:a + 128], c.ident[:, :])
                    last.then_inc(sem["turned"], 1)

                def value(n):
                    j, t, tiles = units[n]
                    pe.wait_ge(sem["probT"], i * U + (n + 1))
                    if not (first and n < 2):
                        pe.wait_ge(sem["ocopied"], i * U + (n - 1))
                    for b, key in enumerate(tiles):
                        last = nc.tensor.matmul(O[n % 2], vs[:, j, key, :], probT[:, n % 2, b * 128:b * 128 + 128],
                                                start=b == 0, stop=b == len(tiles) - 1)
                    last.then_inc(sem["o"], 1)
                for n in range(U + 2):
                    if n < U:
                        score(n)
                    if 1 <= n <= U:
                        flip(n - 1)
                    if n >= 2:
                        value(n - 2)
            body(0, True)
            with pe.Fori(1, rounds) as i:
                body(i, False)

        @block.scalar
        def _(act):
            def body(i, first):
                def exps(n):
                    a = 768 - 128 * len(units[n][2])
                    act.wait_ge(sem["negpeak"], i * U + (n + 1))
                    if not (first and n < 2):
                        act.wait_ge(sem["turned"], i * U + (n - 1))
                    nc.scalar.activation(prob[:, n % 2, a:768], prob[:, n % 2, a:768] if window else S[n % 2][:, a:768],
                                         ACT.Exp, bias=small[:, n % 2, 1:2], scale=scale,
                                         accum_out=small[:, n % 2, 2:3]).then_inc(sem["prob"], 1)
                    if sink:
                        nc.scalar.activation(small[:, n % 2, 3:4], sink(i, units[n][0]), ACT.Exp,
                                             bias=small[:, n % 2, 1:2]).then_inc(sem["sinkexp"], 1)

                def copy(n):
                    nb = len(units[n][2])
                    act.wait_ge(sem["turned"], i * U + (n + 1))
                    if not (first and n < 2):
                        act.wait_ge(sem["o"], i * U + (n - 1))
                    nc.scalar.activation(probT[:, n % 2, 0:nb * 128], TP[:, 0:nb * 128], ACT.Copy).then_inc(sem["probT"], 1)
                for n in range(U + 1):
                    if n < U:
                        exps(n)
                    if n >= 1:
                        copy(n - 1)
            body(0, True)
            with act.Fori(1, rounds) as i:
                body(i, False)

        @block.vector
        def _(dve):
            if window:
                dve.wait_ge(sem["const"], 16)

            def body(i, first):
                def peak(n):
                    j, t, tiles = units[n]
                    a = 768 - 128 * len(tiles)
                    dve.wait_ge(sem["score"], i * U + (n + 1))
                    seen = S[n % 2]
                    if window:
                        if not (first and n < 2):
                            dve.wait_ge(sem["turned"], i * U + (n - 1))
                        if t < 4:
                            m0 = 128 * (tiles[0] - t + 1)
                            nc.vector.tensor_tensor(prob[:, n % 2, a:512], seen[:, a:512], mask[:, m0:m0 + 512 - a], ALU.add)
                        nc.vector.tensor_copy(prob[:, n % 2, 512:768], seen[:, 512:768]).then_inc(sem["masked"], 1)
                        dve.wait_ge(sem["masked"], i * U + (n + 1))
                        seen = prob[:, n % 2, :]
                    nc.vector.reduce_max(small[:, n % 2, 0:1], seen[:, a:768], AX.X).then_inc(sem["top"], 1)
                    dve.wait_ge(sem["top"], i * U + (n + 1))
                    if sink:
                        nc.vector.tensor_scalar(small[:, n % 2, 4:5], small[:, n % 2, 0:1], scale, None, ALU.mult
                                                ).then_inc(sem["peak"], 1)
                        dve.wait_ge(sem["peak"], i * U + (n + 1))
                        nc.vector.tensor_scalar(small[:, n % 2, 1:2], small[:, n % 2, 4:5], sink(i, j), -1.0, ALU.max, ALU.mult
                                                ).then_inc(sem["negpeak"], 1)
                    else:
                        nc.vector.tensor_scalar(small[:, n % 2, 1:2], small[:, n % 2, 0:1], -scale, None, ALU.mult
                                                ).then_inc(sem["negpeak"], 1)

                def finish(n):
                    a = 768 - 128 * len(units[n][2])
                    dve.wait_ge(sem["prob"], i * U + (n + 1))
                    total = small[:, n % 2, 2:3]
                    if sink:
                        dve.wait_ge(sem["sinkexp"], i * U + (n + 1))
                        total = small[:, n % 2, 5:6]
                        nc.vector.tensor_tensor(total, small[:, n % 2, 2:3], small[:, n % 2, 3:4], ALU.add).then_inc(sem["total"], 1)
                        dve.wait_ge(sem["total"], i * U + (n + 1))
                    nc.vector.reciprocal(small[:, n % 2, 6:7], total).then_inc(sem["inv"], 1)
                    dve.wait_ge(sem["inv"], i * U + (n + 1))
                    nc.vector.tensor_scalar(prob[:, n % 2, a:768], prob[:, n % 2, a:768], small[:, n % 2, 6:7], None, ALU.mult
                                            ).then_inc(sem["unit"], 1)

                def keep(n):
                    j, t, _ = units[n]
                    dve.wait_ge(sem["o"], i * U + (n + 1))
                    nc.vector.tensor_copy(out(i, j, t), O[n % 2].unsqueeze(1)).then_inc(sem["ocopied"], 1)
                for n in range(U + 2):
                    if n < U:
                        peak(n)
                    if 1 <= n <= U:
                        finish(n - 1)
                    if n >= 2:
                        keep(n - 2)
            body(0, True)
            with dve.Fori(1, rounds) as i:
                body(i, False)


class Flag:

    def __init__(self, c, name, per):
        self.sem, self.per = c.sem(name), per

    def up(self, instruction):
        instruction.then_inc(self.sem, 1)

    def wait(self, eng, i, n):
        if isinstance(i, int) and i * self.per + n <= 0:
            return
        eng.wait_ge(self.sem, i * self.per + n)


def four(ap):
    return ap.rearrange("p (d v t) -> p d v t", d=2, v=2)


def over_heads(ap, d):
    return ap[:, d:d + 1, :].broadcast_to([128, 2, 128])


def gdn_gates(c, ba, cols, at):
    nc = c.nc
    N = 6 * 32
    tri = c.view(at, 2, 128)
    rows = c.view(at + 256, 2, 32)
    w = [c.view(at + 320 + N * n, 6, 32) for n in range(6)]
    names = "bcgv"
    b_in = ba.rearrange("p t (d k h) -> p t d k h", d=2, k=2)[:, :, :, 0, :]
    a_in = ba.rearrange("p t (d k h) -> p t d k h", d=2, k=2)[:, :, :, 1, :]
    tdh = lambda x: x.rearrange("p t (d h) -> p t d h", d=2)
    flat = lambda x: x.rearrange("p t h -> p (t h)")
    quantity = lambda q, d: cols[:, :, q, :, d, :].rearrange("p k t v -> p t k v")
    s = {n: c.sem("gates_" + n) for n in ("landed", "a", "act", "dve", "pe")}
    cum, tot = c.P[:, 0, 0:2 * 96], c.P[:, 1, 0:2 * 96]
    with nc.Block() as block:
        @block.sync
        def _(sp):
            sp.dma_start(tri[:, :, :].rearrange("p a b -> p (a b)"), c.ins["tri"]).then_inc(s["landed"], 16)
            sp.dma_start(rows[:, :, :].rearrange("p a b -> p (a b)"), c.ins["gdn_rows"]).then_inc(s["landed"], 16)

        @block.scalar
        def _(act):
            act.wait_ge(s["landed"], 32)
            nc.scalar.activation(rows[:, 0, :], rows[:, 0, :], ACT.Exp).then_inc(s["act"], 1)
            act.wait_ge(s["dve"], 3)
            nc.scalar.activation(flat(w[1]), flat(w[1]), ACT.Exp).then_inc(s["act"], 1)
            nc.scalar.activation(flat(w[5]), flat(w[5]), ACT.Exp).then_inc(s["act"], 1)
            act.wait_ge(s["dve"], 4)
            nc.scalar.activation(flat(w[1]), flat(w[1]), ACT.Ln).then_inc(s["act"], 1)
            act.wait_ge(s["dve"], 9)
            nc.scalar.activation(flat(w[1]), flat(w[2]), ACT.Exp).then_inc(s["act"], 1)
            nc.scalar.activation(flat(w[0]), flat(w[0]), ACT.Exp).then_inc(s["act"], 1)
            nc.scalar.activation(flat(w[3]), flat(w[3]), ACT.Exp).then_inc(s["act"], 1)

        @block.vector
        def _(dve):
            n = [0]

            def step(ins):
                ins.then_inc(s["dve"], 1)
                n[0] += 1
                dve.wait_ge(s["dve"], n[0])
            dve.wait_ge(s["landed"], 32)
            for d in range(2):
                last = nc.vector.tensor_tensor(tdh(w[0])[:, :, d, :], a_in[:, :, d, :],
                                               rows[:, 1, 16 * d:16 * d + 16].unsqueeze(1).broadcast_to([128, 6, 16]), ALU.add)
            step(last)
            nc.vector.tensor_scalar(flat(w[1]), flat(w[0]), -1.0, None, ALU.mult).then_inc(s["dve"], 1)
            n[0] += 1
            dve.wait_ge(s["dve"], n[0])
            for d in range(2):
                nc.vector.tensor_scalar(tdh(w[5])[:, :, d, :], b_in[:, :, d, :], -1.0, None, ALU.mult)
            step(nc.vector.tensor_tensor(flat(w[1]), flat(w[1]), flat(w[0]), ALU.min))
            dve.wait_ge(s["act"], 2)
            step(nc.vector.tensor_scalar(flat(w[1]), flat(w[1]), 1.0, None, ALU.add))
            dve.wait_ge(s["act"], 4)
            step(nc.vector.scalar_tensor_tensor(out=flat(w[0]), in0=flat(w[0]), scalar=0.0, in1=flat(w[1]), op0=ALU.max, op1=ALU.add))
            step(nc.vector.scalar_tensor_tensor(out=w[0], in0=w[0], scalar=-1.0,
                                                in1=rows[:, 0, :].unsqueeze(1).broadcast_to([128, 6, 32]), op0=ALU.mult, op1=ALU.mult))
            for d in range(2):
                for t in range(6):
                    last = nc.vector.tensor_copy(cols[:, :, 5, t, d, :], w[0][:, t, 16 * d:16 * d + 16].rearrange("p (k v) -> p k v", v=2))
            step(last)
            nc.vector.tensor_scalar(flat(w[5]), flat(w[5]), 1.0, None, ALU.add).then_inc(s["dve"], 1)
            n[0] += 1
            dve.wait_ge(s["pe"], 1)
            dve.wait_ge(s["dve"], n[0])
            nc.vector.reciprocal(flat(w[4]), flat(w[5]))
            for d in range(2):
                nc.vector.tensor_copy(tdh(w[2])[:, :, d, :], cum[:, 96 * d:96 * d + 96].rearrange("p (t h) -> p t h", h=16))
                last = nc.vector.tensor_copy(tdh(w[0])[:, :, d, :], tot[:, 96 * d:96 * d + 96].rearrange("p (t h) -> p t h", h=16))
            last.then_inc(s["a"], 1)
            dve.wait_ge(s["a"], 1)
            step(nc.vector.tensor_tensor(flat(w[3]), flat(w[0]), flat(w[2]), ALU.subtract))
            dve.wait_ge(s["act"], 7)
            nc.vector.scalar_tensor_tensor(out=flat(w[1]), in0=flat(w[1]), scalar=-1.0, in1=flat(w[4]), op0=ALU.mult, op1=ALU.mult)
            step(nc.vector.tensor_scalar(flat(w[5]), flat(w[2]), -1.0, None, ALU.mult))
            for q, x in ((0, w[4]), (1, w[1]), (2, w[5]), (3, w[3]), (4, w[0])):
                for d in range(2):
                    for t in range(6):
                        nc.vector.tensor_copy(cols[:, :, q, t, d, :], x[:, t, 16 * d:16 * d + 16].rearrange("p (k v) -> p k v", v=2))

        @block.tensor
        def _(pe):
            pe.wait_ge(s["dve"], 7)
            for d in range(2):
                g = tdh(w[0])[:, :, d, :]
                nc.tensor.matmul(cum[:, 96 * d:96 * d + 96], tri[:, d, :], g, start=True, stop=True)
                last = nc.tensor.matmul(tot[:, 96 * d:96 * d + 96], c.ones[:, :], g, start=True, stop=True)
            last.then_inc(s["pe"], 1)


def gdn_heads(c, qkv, cols, at):
    nc = c.nc
    u = c.u[:, :, :].rearrange("p a b -> p (a b)")
    tmp = c.tmp[:, :, :, :].rearrange("p a b c -> p (a b c)")
    stat = c.stat[:, :, :].rearrange("p a b -> p (a b)")
    masks = c.view(at, LEVELS, 2, 128)
    tri = c.view(at + LEVELS * 256, 2, 128)
    at += (LEVELS + 1) * 256
    col = c.view(at, 6, 6, 2, 2)
    taps_all = c.view(at + 144, 32, 5)
    taps = c.view(at + 304, 4, 5)
    Vt = [c.view(at + 324, 6, 128), tmp[:, 2048:2816].rearrange("p (t n) -> p t n", t=6)]
    GK = stat.rearrange("p (t k n) -> p t k n", t=6, k=2)
    Kt = c.ring[:, 0, 2048:2816].rearrange("p (t n) -> p t n", t=6)
    S = c.ring[:, 1, 2048:2560]
    row = u[:, 0:4 * T].rearrange("p (r t) -> p r t", r=4)
    raw = u[:, 4 * T:8 * T].rearrange("p (r t) -> p r t", r=4)
    DT, LT, QD, E0, E1, X = (u[:, 4 * T + 512 * n:4 * T + 512 * (n + 1)] for n in range(6))
    E = [E0, E1]
    XT, Y, VN, KD_ = (tmp[:, 512 * n:512 * (n + 1)] for n in range(4))
    R = Y
    o_sum = row[:, 2:4, 0:LAT]
    PF = c.P[:, :, :].rearrange("p a b -> p (a b)")
    PA, PB, PY, PZT, PZ, PKS, PVN, PO = (PF[:, 512 * n:512 * (n + 1)] for n in range(8))
    STEPS = 6
    chunk = [[4, 5, 0, 1, 2, 3], [5, 4, 3, 2, 1, 0]]
    L = LEVELS - 1
    F = lambda name, per: Flag(c, "gdn_" + name, per)
    landed = c.sem("gdn_landed")
    raws, colss, conv, tap, silu, sq, ss, sse, ssd, ssr, qk, vturn, vt, kturn, kt, gk = (
        F(n, p) for n, p in (("raw", 1), ("cols", 1), ("conv", 4), ("tap", 16), ("silu", 4), ("sq", 1), ("ss", 1), ("sse", 1), ("ssd", 1),
                             ("ssr", 1), ("qk", 1), ("vturn", 1), ("vt", 1), ("kturn", 1), ("kt", 1), ("gk", 1)))
    rows, dm, dt, dtm, lt0, lt, e0, x0, xturn, xcp = (
        F(n, STEPS) for n in ("rows", "dm", "dt", "dtm", "lt0", "lt", "e0", "x0", "xturn", "xcp"))
    er, attn, qd, o, oadd = (F(n, STEPS - 2) for n in ("er", "attn", "qd", "o", "oadd"))
    et, y, ycp, z, xl = (F(n, STEPS * L) for n in ("et", "y", "ycp", "z", "xl"))
    bv, kd, ks, r, vn, vncp, sn, st = (F(n, STEPS) for n in ("bv", "kd", "ks", "r", "vn", "vncp", "sn", "st"))
    out = F("out", 1)
    unit = [(d, v, 2 * d + v) for d in range(2) for v in range(2)]
    at_u = lambda x, n: x[:, 128 * n:128 * n + 128]
    scalar = lambda q, s, d, v: col[:, q, chunk[d][s], d, v:v + 1]
    with nc.Block() as block:
        @block.sync
        def _(sp):
            sp.dma_start(masks[:, :, :, :].rearrange("p a b c -> p (a b c)"), c.ins["level_masks"]).then_inc(landed, 16)
            sp.dma_start(tri[:, :, :].rearrange("p a b -> p (a b)"), c.ins["tri"]).then_inc(landed, 16)
            sp.dma_start(taps_all[:, :, :].rearrange("p a b -> p (a b)"), c.ins["gdn_taps"]).then_inc(landed, 16)

        @block.gpsimd
        def _(pool):
            pool.wait_ge(landed, 48)

            def body(i):
                out.wait(pool, i, 0)
                nc.gpsimd.tensor_copy(col.rearrange("p a b c d -> p (a b c d)").unsqueeze(1),
                                      cols[:, one(i), :, :, :, :].rearrange("p k a b c d -> p k (a b c d)"))
                nc.gpsimd.tensor_copy(taps[:, 0:1, :], taps_all[:, one(i), :])
                nc.gpsimd.tensor_copy(taps[:, 1:2, :], taps_all[:, one(i + 8), :])
                nc.gpsimd.tensor_copy(taps[:, 2:4, :], taps_all[:, bass.ds(i * 2 + 16, 2), :])
                colss.up(nc.gpsimd.memset(S, 0.0))
                for s in range(STEPS):
                    for l in range(1, LEVELS):
                        n = s * L + l
                        lt.wait(pool, i, s + 1)
                        y.wait(pool, i, n - 2)
                        for d in range(2):
                            ins = nc.gpsimd.tensor_tensor(four(E[l % 2])[:, d], four(LT)[:, d], over_heads(masks[:, l], d), ALU.mult)
                        et.up(ins)
                    if s:
                        sn.wait(pool, i, s)
                    for d, v, n in unit:
                        ins = nc.gpsimd.tensor_tensor(at_u(KD_, n), Kt[:, chunk[d][s], :], scalar(3, s, d, v).broadcast_to([128, 128]),
                                                      ALU.mult)
                    kd.up(ins)
            body(0)
            with pool.Fori(1, HEADS) as i:
                body(i)

        @block.scalar
        def _(act):
            def body(i):
                out.wait(act, i, 0)
                for r_, blk in enumerate((i, i + 8, i * 2 + 16, i * 2 + 17)):
                    ins = nc.scalar.activation(raw[:, r_:r_ + 1, :], qkv[:, one(blk), :], ACT.Copy)
                raws.up(ins)
                for r_ in (2, 3, 0, 1):
                    conv.wait(act, i, {2: 1, 3: 2, 0: 3, 1: 4}[r_])
                    silu.up(nc.scalar.activation(row[:, r_, :], row[:, r_, :], ACT.Silu))
                silu.wait(act, i, 4)
                nc.scalar.activation(raw[:, 0, :], row[:, 0, :], ACT.Square)
                sq.up(nc.scalar.activation(raw[:, 1, :], row[:, 1, :], ACT.Square))
                vturn.wait(act, i, 1)
                for v in range(2):
                    ins = nc.scalar.activation(Vt[v].rearrange("p t n -> p (t n)"), c.P[:, v, 0:T], ACT.Copy)
                vt.up(ins)
                sse.wait(act, i, 1)
                ssd.up(nc.scalar.activation(raw[:, 2:4, :].rearrange("p a b -> p (a b)"),
                                            raw[:, 2:4, :].rearrange("p a b -> p (a b)"), ACT.Sqrt))
                kturn.wait(act, i, 1)
                kt.up(nc.scalar.activation(Kt.rearrange("p t n -> p (t n)"), PF[:, 0:T], ACT.Copy))
                for s in range(STEPS):
                    dm.wait(act, i, s + 1)
                    if s >= 2:
                        if s > 2:
                            o.wait(act, i, s - 2)
                        er.up(nc.scalar.activation(QD, PA, ACT.Exp))
                    dt.up(nc.scalar.activation(DT, DT, ACT.Exp))
                    xturn.wait(act, i, s + 1)
                    xcp.up(nc.scalar.activation(X, PY, ACT.Copy))
                    for l in range(1, LEVELS):
                        n = s * L + l
                        y.wait(act, i, n)
                        if l == 1 and s:
                            vn.wait(act, i, s)
                        z.wait(act, i, n - 1)
                        ycp.up(nc.scalar.activation(Y, PY, ACT.Copy))
                    z.wait(act, i, (s + 1) * L)
                    for d, v, n in unit:
                        ins = nc.scalar.activation(at_u(R, n), Vt[v][:, chunk[d][s], :], ACT.Copy, scale=scalar(0, s, d, v))
                    bv.up(ins)
                    vn.wait(act, i, s + 1)
                    vncp.up(nc.scalar.activation(VN, PVN, ACT.Copy))
            body(0)
            with act.Fori(1, HEADS) as i:
                body(i)

        @block.vector
        def _(dve):
            dve.wait_ge(landed, 48)

            def body(i):
                raws.wait(dve, i, 1)
                colss.wait(dve, i, 1)
                k = 0
                for r_ in (2, 3, 0, 1):
                    ins = nc.vector.tensor_scalar(row[:, r_, :], raw[:, r_, :], taps[:, r_, 2:3], None, ALU.mult)
                    for sh in (-2, -1, 1, 2):
                        tap.up(ins)
                        k += 1
                        tap.wait(dve, i, k)
                        for a, b in ((0, LAT), (LAT, T)):
                            lo, hi = max(a, a - sh), min(b, b - sh)
                            ins = nc.vector.scalar_tensor_tensor(out=row[:, r_, lo:hi], in0=raw[:, r_, lo + sh:hi + sh],
                                                                 scalar=taps[:, r_, sh + 2:sh + 3], in1=row[:, r_, lo:hi],
                                                                 op0=ALU.mult, op1=ALU.add)
                    conv.up(ins)
                ss.wait(dve, i, 1)
                for n in range(2):
                    ins = nc.vector.tensor_scalar(raw[:, 2 + n, :], c.P[:, 2 + n, 0:T], 1.0, 1e-6, ALU.mult, ALU.add)
                sse.up(ins)
                ssd.wait(dve, i, 1)
                ssr.up(nc.vector.reciprocal(raw[:, 0:2, :].rearrange("p a b -> p (a b)"),
                                            raw[:, 2:4, :].rearrange("p a b -> p (a b)")))
                ssr.wait(dve, i, 1)
                nc.vector.scalar_tensor_tensor(out=row[:, 0, :], in0=row[:, 0, :], scalar=128 ** -0.5, in1=raw[:, 0, :],
                                               op0=ALU.mult, op1=ALU.mult)
                qk.up(nc.vector.tensor_tensor(row[:, 1, :], row[:, 1, :], raw[:, 1, :], ALU.mult))
                kturn.wait(dve, i, 1)
                gk.up(nc.vector.tensor_copy(GK.rearrange("p t k n -> p (t k n)"), PF[:, 1024:2560]))
                for s in range(STEPS):
                    rows.wait(dve, i, s + 1)
                    for d, v, n in unit:
                        ins = nc.vector.tensor_scalar(at_u(DT, n), at_u(PA, n), scalar(2, s, d, v), 0.0, ALU.add, ALU.min)
                    dm.up(ins)
                    for d in range(2):
                        ins = nc.vector.tensor_tensor(four(LT)[:, d], GK[:, chunk[d][s], 0:1, :].broadcast_to([128, 2, 128]),
                                                      four(PB)[:, d], ALU.mult)
                    lt0.up(ins)
                    dt.wait(dve, i, s + 1)
                    for d in range(2):
                        ins = nc.vector.tensor_tensor(four(DT)[:, d], four(DT)[:, d], over_heads(tri, d), ALU.mult)
                    dtm.up(ins)
                    lt0.wait(dve, i, s + 1)
                    dtm.wait(dve, i, s + 1)
                    lt.up(nc.vector.tensor_tensor(LT, LT, DT, ALU.mult))
                    lt.wait(dve, i, s + 1)
                    for d in range(2):
                        ins = nc.vector.tensor_tensor(four(VN)[:, d], four(LT)[:, d], over_heads(masks[:, 0], d), ALU.mult)
                    e0.up(ins)
                    e0.wait(dve, i, s + 1)
                    x0.up(nc.vector.tensor_tensor(XT.rearrange("p (n t) -> p n t", n=4),
                                                  c.ident[:, :].unsqueeze(1).broadcast_to([128, 4, 128]),
                                                  VN.rearrange("p (n t) -> p n t", n=4), ALU.subtract))
                    if s >= 2:
                        for d in range(2):
                            ins = nc.vector.tensor_tensor(four(DT)[:, d], four(DT)[:, d],
                                                          GK[:, chunk[d][s], 1:2, :].broadcast_to([128, 2, 128]), ALU.mult)
                        attn.up(ins)
                        er.wait(dve, i, s - 1)
                        for d in range(2):
                            t0 = chunk[d][s] * 128
                            ins = nc.vector.tensor_tensor(four(QD)[:, d], four(QD)[:, d],
                                                          row[:, 0:1, t0:t0 + 128].broadcast_to([128, 2, 128]), ALU.mult)
                        qd.up(ins)
                    for l in range(1, LEVELS):
                        z.wait(dve, i, s * L + l)
                        ins = nc.vector.tensor_tensor(XT, XT, PZT, ALU.subtract)
                        if l < L:
                            ins = nc.vector.tensor_tensor(X, X, PZ, ALU.subtract)
                        xl.up(ins)
                    ks.wait(dve, i, s + 1)
                    bv.wait(dve, i, s + 1)
                    for d, v, n in unit:
                        ins = nc.vector.scalar_tensor_tensor(out=at_u(R, n), in0=at_u(PKS, n), scalar=scalar(1, s, d, v),
                                                             in1=at_u(R, n), op0=ALU.mult, op1=ALU.add)
                    r.up(ins)
                    sn.wait(dve, i, s + 1)
                    for d, v, n in unit:
                        ins = nc.vector.scalar_tensor_tensor(out=at_u(S, n), in0=at_u(S, n), scalar=scalar(4, s, d, v),
                                                             in1=at_u(PKS, n), op0=ALU.mult, op1=ALU.add)
                    st.up(ins)
                    if s >= 2:
                        for d in range(2):
                            t0 = chunk[d][s] * 128
                            part = o_sum[:, :, t0:t0 + 128]
                            if s < 4:
                                ins = nc.vector.tensor_copy(part, four(PO)[:, d])
                            else:
                                ins = nc.vector.tensor_tensor(part, part, four(PO)[:, d], ALU.add)
                        oadd.up(ins)
                oadd.wait(dve, i, STEPS - 2)
                out.up(nc.vector.tensor_scalar(qkv[:, bass.ds(i * 2 + 16, 2), 0:LAT], o_sum, 1.0, None, ALU.mult))
            body(0)
            with dve.Fori(1, HEADS) as i:
                body(i)

        @block.tensor
        def _(pe):
            pe.wait_ge(landed, 48)

            def body(i):
                silu.wait(pe, i, 2)
                oadd.wait(pe, i, 0)
                for v in range(2):
                    for t in range(6):
                        ins = nc.tensor.transpose(c.P[:, v, 128 * t:128 * t + 128], row[:, 2 + v, 128 * t:128 * t + 128], c.ident[:, :])
                vturn.up(ins)
                sq.wait(pe, i, 1)
                for n in range(2):
                    for a, b in BOTH:
                        ins = nc.tensor.matmul(c.P[:, 2 + n, a:b], c.ones[:, :], raw[:, n, a:b], start=True, stop=True)
                ss.up(ins)
                qk.wait(pe, i, 1)
                vt.wait(pe, i, 1)
                for t in range(6):
                    k_t, q_t = row[:, 1, 128 * t:128 * t + 128], row[:, 0, 128 * t:128 * t + 128]
                    nc.tensor.transpose(PF[:, 128 * t:128 * t + 128], k_t, c.ident[:, :])
                    nc.tensor.matmul(PF[:, 1024 + 256 * t:1152 + 256 * t], k_t, k_t, start=True, stop=True)
                    ins = nc.tensor.matmul(PF[:, 1152 + 256 * t:1280 + 256 * t], k_t, q_t, start=True, stop=True)
                kturn.up(ins)
                kt.wait(pe, i, 1)
                gk.wait(pe, i, 1)
                for s in range(STEPS):
                    lt0.wait(pe, i, s)
                    for d, v, n in unit:
                        g, b = scalar(5, s, d, v), scalar(0, s, d, v)
                        nc.tensor.matmul(at_u(PA, n), g.broadcast_to([128, 128]), tri[:, d, :], start=True, stop=True)
                        ins = nc.tensor.matmul(at_u(PB, n), b.broadcast_to([128, 128]), c.ident[:, :], start=True, stop=True)
                    rows.up(ins)
                    st.wait(pe, i, s)
                    for d in range(2):
                        t0 = 128 * chunk[d][s]
                        ins = nc.tensor.matmul(PKS[:, 256 * d:256 * d + 256], row[:, 1, t0:t0 + 128], S[:, 256 * d:256 * d + 256],
                                               start=True, stop=True)
                    ks.up(ins)
                    x0.wait(pe, i, s + 1)
                    for d, v, n in unit:
                        ins = nc.tensor.transpose(at_u(PY, n), at_u(XT, n), c.ident[:, :])
                    xturn.up(ins)
                    xcp.wait(pe, i, s + 1)
                    for l in range(1, LEVELS):
                        m = s * L + l
                        et.wait(pe, i, m)
                        if l > 1:
                            xl.wait(pe, i, m - 1)
                        for d, v, n in unit:
                            ins = nc.tensor.matmul(at_u(PY, n), at_u(E[l % 2], n), at_u(X, n), start=True, stop=True)
                        y.up(ins)
                        ycp.wait(pe, i, m)
                        for d, v, n in unit:
                            ins = nc.tensor.matmul(at_u(PZT, n), at_u(Y, n), at_u(XT, n), start=True, stop=True)
                        if l < L:
                            for d, v, n in unit:
                                ins = nc.tensor.matmul(at_u(PZ, n), at_u(XT, n), at_u(Y, n), start=True, stop=True)
                        z.up(ins)
                    r.wait(pe, i, s + 1)
                    xl.wait(pe, i, (s + 1) * L)
                    for d, v, n in unit:
                        ins = nc.tensor.matmul(at_u(PVN, n), at_u(XT, n), at_u(R, n), start=True, stop=True)
                    vn.up(ins)
                    vncp.wait(pe, i, s + 1)
                    if s >= 2:
                        qd.wait(pe, i, s - 1)
                        oadd.wait(pe, i, s - 2)
                        for d, v, n in unit:
                            nc.tensor.matmul(at_u(PO, n), at_u(VN, n), at_u(DT, n), start=True, stop=False)
                            ins = nc.tensor.matmul(at_u(PO, n), at_u(S, n), at_u(QD, n), start=False, stop=True)
                        o.up(ins)
                    kd.wait(pe, i, s + 1)
                    for d, v, n in unit:
                        ins = nc.tensor.matmul(at_u(PKS, n), at_u(KD_, n), at_u(VN, n), start=True, stop=True)
                    sn.up(ins)
            body(0)
            with pe.Fori(1, HEADS) as i:
                body(i)


def head_norm(c, o, at, gain):
    nc = c.nc
    sq, rs = c.view(at, 4, LAT), c.view(at + 4 * LAT, 4, LAT)
    flat = lambda x: x.rearrange("p a b -> p (a b)")
    s = {n: c.sem("headnorm_" + n) for n in ("sq", "sum", "var", "sd", "rs", "out")}
    psum = c.P[:, 0:2, :].rearrange("p a b -> p (a b)")
    with nc.Block() as block:
        @block.scalar
        def _(act):
            for q in range(4):
                if q:
                    act.wait_ge(s["sum"], q)
                nc.scalar.activation(sq, o[:, 4 * q:4 * q + 4, 0:LAT], ACT.Square).then_inc(s["sq"], 1)
                act.wait_ge(s["var"], q + 1)
                nc.scalar.activation(flat(rs), flat(rs), ACT.Sqrt).then_inc(s["sd"], 1)

        @block.tensor
        def _(pe):
            for q in range(4):
                pe.wait_ge(s["sq"], q + 1)
                if q:
                    pe.wait_ge(s["var"], q)
                for n in range(4):
                    last = nc.tensor.matmul(psum[:, 512 * n:512 * n + 512], c.ones[:, :], sq[:, n, :], start=True, stop=True)
                last.then_inc(s["sum"], 1)

        @block.vector
        def _(dve):
            for q in range(4):
                dve.wait_ge(s["sum"], q + 1)
                if q:
                    dve.wait_ge(s["out"], q)
                nc.vector.tensor_scalar(flat(rs), psum, 1.0 / 128, 1e-6, ALU.mult, ALU.add).then_inc(s["var"], 1)
                dve.wait_ge(s["sd"], q + 1)
                nc.vector.reciprocal(flat(rs), flat(rs)).then_inc(s["rs"], 1)
                dve.wait_ge(s["rs"], q + 1)
                x = o[:, 4 * q:4 * q + 4, 0:LAT]
                nc.vector.scalar_tensor_tensor(out=x, in0=x, scalar=gain, in1=rs, op0=ALU.mult, op1=ALU.mult
                                               ).then_inc(s["out"], 1)


MAGIC = 1.5 * 2.0 ** 23
TURN = 6.283185307179586


def s5_params(c, par, at):
    nc = c.nc
    N = 128
    raw = c.view(at, 3, N)
    w = [c.view(at + 3 * N + N * n, N) for n in range(12)]
    out = lambda q: par[:, :, q, :]
    sq2 = lambda x: x.rearrange("p (b e) -> p b e", e=8)
    landed, dv, ac = (c.sem("s5par_" + n) for n in ("landed", "dve", "act"))
    re, im, ls = raw[:, 0, :], raw[:, 1, :], raw[:, 2, :]
    with nc.Block() as block:
        @block.sync
        def _(sp):
            sp.dma_start(raw.rearrange("p a b -> p (a b)"), c.ins["s5_lam"]).then_inc(landed, 16)

        @block.scalar
        def _(act):
            act.wait_ge(landed, 16)
            nc.scalar.activation(w[0], ls, ACT.Exp).then_inc(ac, 1)
            act.wait_ge(dv, 1)
            nc.scalar.activation(w[2], w[1], ACT.Exp).then_inc(ac, 1)
            act.wait_ge(dv, 9)
            nc.scalar.activation(w[5], w[4], ACT.Sin, scale=TURN).then_inc(ac, 1)
            nc.scalar.activation(w[7], w[6], ACT.Sin, scale=TURN).then_inc(ac, 1)

        @block.vector
        def _(dve):
            n = [0]

            def step(ins):
                ins.then_inc(dv, 1)
                n[0] += 1
                dve.wait_ge(dv, n[0])
            V = nc.vector
            dve.wait_ge(ac, 1)
            step(V.tensor_tensor(w[1], re, w[0], ALU.mult))
            step(V.tensor_tensor(w[3], im, w[0], ALU.mult))
            step(V.tensor_scalar(w[3], w[3], 1.0 / TURN, None, ALU.mult))
            step(V.tensor_scalar(w[4], w[3], MAGIC, -MAGIC, ALU.add, ALU.add))
            step(V.tensor_tensor(w[4], w[3], w[4], ALU.subtract))
            step(V.tensor_scalar(w[6], w[4], 0.25, None, ALU.add))
            step(V.tensor_scalar(w[8], w[6], MAGIC, -MAGIC, ALU.add, ALU.add))
            step(V.tensor_tensor(w[6], w[6], w[8], ALU.subtract))
            step(V.tensor_scalar(w[8], w[4], 3.0 * 2.0 ** 10, -3.0 * 2.0 ** 10, ALU.add, ALU.add))
            V.tensor_copy(out(1), sq2(w[8]))
            step(V.tensor_tensor(out(2), sq2(w[4]), sq2(w[8]), ALU.subtract))
            dve.wait_ge(ac, 4)
            V.tensor_copy(out(0), sq2(w[2]))
            step(V.tensor_tensor(w[9], w[2], w[7], ALU.mult))
            V.tensor_scalar(w[9], w[9], -1.0, None, ALU.add)
            step(V.tensor_tensor(w[10], w[2], w[5], ALU.mult))
            V.tensor_tensor(w[0], re, re, ALU.mult)
            step(V.tensor_tensor(w[1], im, im, ALU.mult))
            step(V.tensor_tensor(w[0], w[0], w[1], ALU.add))
            step(V.reciprocal(w[11], w[0]))
            V.tensor_tensor(w[0], w[9], re, ALU.mult)
            V.tensor_tensor(w[1], w[10], im, ALU.mult)
            V.tensor_tensor(w[2], w[10], re, ALU.mult)
            step(V.tensor_tensor(w[3], w[9], im, ALU.mult))
            V.tensor_tensor(w[0], w[0], w[1], ALU.add)
            step(V.tensor_tensor(w[2], w[2], w[3], ALU.subtract))
            V.tensor_tensor(out(3), sq2(w[0]), sq2(w[11]), ALU.mult)
            V.tensor_tensor(out(4), sq2(w[2]), sq2(w[11]), ALU.mult)


def s5_scan(c, p, par, at, skip):
    nc = c.nc
    steps = c.view(at, T)
    Bm, Cm = c.view(at + T, 2, 2, 128), c.view(at + T + 512, 2, 4, 2, 32)
    xs, col = c.view(at + T + 1024, T), c.view(at + 2 * T + 1024, 5, 8)
    w = [c.view(at + 2 * T + 1064 + T * n, T) for n in range(11)]
    A, N_, fs, fc = w[0:4]
    Tr, Ti, t1, t2 = w[0], w[1], w[4], w[5]
    t3, t4, gr, gi = w[6], w[7], w[8], w[9]
    hr, hi = w[10], w[6]
    landed, mats = c.sem("s5_landed"), c.sem("s5_mats")
    U = 8
    F = lambda name, per: Flag(c, "s5_" + name, per)
    staged, out, free = F("staged", 1), F("out", 1), None
    ph, trig, tab, bu, p4, add1, g, q4, add2, y = (F(n, U) for n in ("ph", "trig", "tab", "bu", "p4", "add1", "g", "q4", "add2", "y"))
    chain = F("chain", U * 13)
    PR, PI, PY = c.P[:, 0, 0:T], c.P[:, 1, 0:T], c.P[:, 2, 0:LAT]
    unit = [(d, q, 4 * d + q) for d in range(2) for q in range(4)]

    def order(d):
        if d == 0:
            return [(0, slice(LAT, T)), (256, slice(0, 256)), (512, slice(256, 512))]
        return [(0, slice(T - 1, LAT - 1, -1)), (256, slice(LAT - 1, 255, -1)), (512, slice(255, None, -1))]
    with nc.Block() as block:
        @block.sync
        def _(sp):
            sp.dma_start(steps, c.ins["s5_steps"]).then_inc(landed, 16)

            def body(i):
                out.wait(sp, i, 0)
                sp.dma_start(Bm.rearrange("p a b c -> p (a b c)"), rows_of(c.ins["s5_b"], i)).then_inc(mats, 16)
                sp.dma_start(Cm.rearrange("p a b c d -> p (a b c d)"), rows_of(c.ins["s5_c"], i)).then_inc(mats, 16)
            body(0)
            with sp.Fori(1, 16) as i:
                body(i)

        @block.gpsimd
        def _(pool):
            def body(i):
                out.wait(pool, i, 0)
                nc.gpsimd.tensor_copy(col.rearrange("p a b -> p (a b)").unsqueeze(1),
                                      par[:, one(i), :, :].rearrange("p k a b -> p k (a b)"))
                staged.up(nc.gpsimd.tensor_copy(xs.unsqueeze(1), p[:, one(i), :]))
                for d, q, n in unit:
                    p4.wait(pool, i, n + 1)
                    nc.gpsimd.tensor_tensor(t1, t1, t2, ALU.subtract)
                    add1.up(nc.gpsimd.tensor_tensor(t3, t3, t4, ALU.add))
                    q4.wait(pool, i, n + 1)
                    nc.gpsimd.tensor_tensor(hr[:, 0:LAT], t1[:, 0:LAT], t2[:, 0:LAT], ALU.subtract)
                    add2.up(nc.gpsimd.tensor_tensor(hi[:, 0:LAT], t3[:, 0:LAT], t4[:, 0:LAT], ALU.subtract))
            body(0)
            with pool.Fori(1, 16) as i:
                body(i)

        @block.scalar
        def _(act):
            def body(i):
                for d, q, n in unit:
                    ph.wait(act, i, n + 1)
                    nc.scalar.activation(fs, fs, ACT.Sin, scale=-TURN)
                    trig.up(nc.scalar.activation(fc, fc, ACT.Sin, scale=TURN))
            body(0)
            with act.Fori(1, 16) as i:
                body(i)

        @block.vector
        def _(dve):
            dve.wait_ge(landed, 16)
            V = nc.vector

            def body(i):
                staged.wait(dve, i, 1)
                n_ = [0]

                def step(ins):
                    chain.up(ins)
                    n_[0] += 1
                    chain.wait(dve, i, n_[0])
                for d, q, n in unit:
                    hi_turn, lo_turn, r_ = col[:, 1, n:n + 1], col[:, 2, n:n + 1], col[:, 0, n:n + 1]
                    cr, ci = col[:, 3, n:n + 1], col[:, 4, n:n + 1]
                    step(V.tensor_scalar(A, steps, hi_turn, None, ALU.mult))
                    step(V.tensor_scalar(N_, A, MAGIC, -MAGIC, ALU.add, ALU.add))
                    step(V.tensor_tensor(A, A, N_, ALU.subtract))
                    step(V.scalar_tensor_tensor(out=A, in0=steps, scalar=lo_turn, in1=A, op0=ALU.mult, op1=ALU.add))
                    step(V.tensor_scalar(N_, A, MAGIC, -MAGIC, ALU.add, ALU.add))
                    step(V.tensor_tensor(fs, A, N_, ALU.subtract))
                    step(V.tensor_scalar(A, fs, 0.25, None, ALU.add))
                    step(V.tensor_scalar(N_, A, MAGIC, -MAGIC, ALU.add, ALU.add))
                    ph.up(V.tensor_tensor(fc, A, N_, ALU.subtract))
                    trig.wait(dve, i, n + 1)
                    V.tensor_scalar(Ti, fc, ci, None, ALU.mult)
                    V.tensor_scalar(Tr, fc, cr, None, ALU.mult)
                    add2.wait(dve, i, n)
                    step(V.tensor_scalar(t1, fs, ci, None, ALU.mult))
                    step(V.scalar_tensor_tensor(out=Ti, in0=fs, scalar=cr, in1=Ti, op0=ALU.mult, op1=ALU.add))
                    step(V.tensor_tensor(Tr, Tr, t1, ALU.subtract))
                    bu.wait(dve, i, n + 1)
                    V.tensor_tensor(t1, PR, Tr, ALU.mult)
                    V.tensor_tensor(t2, PI, Ti, ALU.mult)
                    y.wait(dve, i, n)
                    V.tensor_tensor(t3, PI, Tr, ALU.mult)
                    p4.up(V.tensor_tensor(t4, PR, Ti, ALU.mult))
                    add1.wait(dve, i, n + 1)
                    rb = r_.broadcast_to([128, T])
                    V.tensor_tensor_scan(gr, rb, t1, 0.0, ALU.mult, ALU.add)
                    step(V.tensor_tensor_scan(gi, rb, t3, 0.0, ALU.mult, ALU.add))
                    V.tensor_tensor(t1[:, 0:LAT], gr[:, CTX:T], fc[:, CTX:T], ALU.mult)
                    V.tensor_tensor(t2[:, 0:LAT], gi[:, CTX:T], fs[:, CTX:T], ALU.mult)
                    step(V.tensor_tensor(t3[:, 0:LAT], gr[:, CTX:T], fs[:, CTX:T], ALU.mult))
                    V.tensor_scalar(t2[:, 0:LAT], t2[:, 0:LAT], -1.0, None, ALU.mult)
                    q4.up(V.tensor_tensor(t4[:, 0:LAT], gi[:, CTX:T], fc[:, CTX:T], ALU.mult))
                y.wait(dve, i, U)
                out.up(V.scalar_tensor_tensor(out=p[:, one(i), 0:LAT], in0=xs[:, 0:LAT].unsqueeze(1), scalar=skip(i),
                                              in1=PY.unsqueeze(1), op0=ALU.mult, op1=ALU.add))
            body(0)
            with dve.Fori(1, 16) as i:
                body(i)

        @block.tensor
        def _(pe):
            def body(i):
                staged.wait(pe, i, 1)
                pe.wait_ge(mats, i * 32 + 32)

                def inputs(n):
                    d, q, _ = unit[n]
                    p4.wait(pe, i, n)
                    for k, ps in enumerate((PR, PI)):
                        for a, cols in order(d):
                            ins = nc.tensor.matmul(ps[:, a:a + 256], Bm[32 * q:32 * q + 32, d, k, :],
                                                   xs[32 * q:32 * q + 32, cols], start=True, stop=True)
                    bu.up(ins)

                def outputs(n):
                    d, q, _ = unit[n]
                    add2.wait(pe, i, n + 1)
                    for k, x in enumerate((hr, hi)):
                        cols = slice(0, LAT) if d == 0 else slice(LAT - 1, None, -1)
                        ins = nc.tensor.matmul(PY[32 * q:32 * q + 32, :], Cm[:, d, q, k, :], x[:, 0:LAT][:, cols],
                                               start=d == 0 and k == 0, stop=d == 1 and k == 1, skip_group_check=True)
                    y.up(ins)
                for n in range(U + 1):
                    if n < U:
                        inputs(n)
                    if n:
                        outputs(n - 1)
            body(0)
            with pe.Fori(1, 16) as i:
                body(i)


def gelu(c, p):
    nc = c.nc
    with nc.Block() as block:
        @block.scalar
        def _(act):
            for g in range(4):
                nc.scalar.activation(p[:, 4 * g:4 * g + 4, 0:LAT], p[:, 4 * g:4 * g + 4, 0:LAT], ACT.Gelu_apprx_tanh)


VECS = [("b_mod0", 48), ("b_mod1", 48), ("ada_b_20", 24), ("ada_b_21", 24),
        ("c", 8), ("c_ctx", 8), ("c_2", 8), ("c_ctx_2", 8),
        ("ln1_g0", 8), ("ln1_b0", 8), ("ln2_g0", 8), ("ln2_b0", 8), ("ln1_g1", 8), ("ln1_b1", 8), ("ln2_g1", 8), ("ln2_b1", 8),
        ("ln_g_20", 8), ("ln_b_20", 8), ("ln_g_21", 8), ("ln_b_21", 8),
        ("mla_q_norm", 4), ("mla_kv_norm", 2), ("gdn_norm", 1), ("s5_d", 16), ("s5_glu_b", 16), ("sink", 16)]
VEC_AT = {}
_at = 0
for _n, _w in VECS:
    VEC_AT[_n] = _at
    _at += _w
VEC_WIDTH = _at


def program(nc, ins, out):
    c = Core(nc, ins)
    P = c.P
    act_fn, vec_fn = nc.scalar.activation, nc.vector
    h, u, area = c.h, c.u, c.view
    vcol = lambda name: (lambda k: c.vec[:, VEC_AT[name] + k:VEC_AT[name] + k + 1])

    landed, silu_c = c.sem("landed"), c.sem("silu_c")
    cond = area(0, KD, 4)
    with nc.Block() as block:
        @block.sync
        def _(sp):
            sp.dma_start(c.vec[:, :], ins["vecs"]).then_inc(landed, 16)
            c.load_slot(sp, "mod", 0, 0)
            c.load_slot(sp, "mod", 1, 1)
            sp.dma_start(h[:, :, 0:LAT], ins["x"].rearrange("p (k t) -> p k t", k=KD)).then_inc(landed, 16)
            sp.dma_start(h[:, :, LAT:T], ins["ctx"].rearrange("p (k t) -> p k t", k=KD)).then_inc(landed, 16)
            sp.dma_start(c.ones[:, :], ins["ones"]).then_inc(landed, 16)
            sp.dma_start(c.ident[:, :], ins["ident"]).then_inc(landed, 16)

        @block.scalar
        def _(act):
            act.wait_ge(landed, 80)
            v = c.vec[:, VEC_AT["c"]:VEC_AT["c"] + 32].rearrange("p (c k) -> p k c", c=4)
            act_fn(cond, v, ACT.Silu).then_inc(silu_c, 1)

    def keep_mod(g, j, ps, tmp):
        return act_fn(c.mod[:, one(g * 2 + j), :], ps[:, 0:4].unsqueeze(1), ACT.Copy)
    dense(c, "mod", cond, ((0, 4),), keep_mod)
    bias_in = c.sem("bias_in")
    with nc.Block() as block:
        @block.vector
        def _(dve):
            vec_fn.tensor_tensor(c.mod[:, :, :], c.mod[:, :, :], c.vec[:, 0:144].unsqueeze(2).broadcast_to([128, 144, 4]), ALU.add
                                 ).then_inc(bias_in, 1)
            dve.wait_ge(bias_in, 1)
            for a in (8, 32, 56, 80, 104, 128):
                vec_fn.tensor_scalar(c.mod[:, a:a + 8, :], c.mod[:, a:a + 8, :], 1.0, None, ALU.add)

    def modcol(base, cond_):
        return lambda k: c.mod[:, base + k, cond_:cond_ + 1]

    def modulated(base, conds=(0, 1)):
        segs = [(0, LAT), (LAT, T)][:len(conds)]
        return [(modcol(base + 8, cc), modcol(base, cc), a, b) for cc, (a, b) in zip(conds, segs)]

    def modulate(parts, loads=None):
        got = c.sem("ctx_landed")
        with nc.Block() as block:
            if loads is not None:
                @block.sync
                def _(sp):
                    sp.dma_start(h[:, :, LAT:T], loads.rearrange("p (k t) -> p k t", k=KD)).then_inc(got, 16)

            @block.scalar
            def _(act):
                if loads is not None:
                    act.wait_ge(got, 16)
                for k in range(KD):
                    for scale, add, a, b in parts:
                        act_fn(u[:, k, a:b], h[:, k, a:b], ACT.Identity, scale=scale(k), bias=add(k))

    def residual(name, x, gate, conds, segs):
        per = c.shape_of(name)[1]

        def act(g, j, ps, tmp):
            for cc, (a, b) in zip(conds, ((0, LAT), (LAT, T))):
                last = act_fn(tmp[:, a:b], ps[:, a:b], ACT.Copy, scale=c.mod[:, bass.ds(g * per + (j + gate), 1), cc:cc + 1].rearrange("p a b -> p (a b)"))
            return last

        def vec(g, j, ps, tmp):
            w = T if len(conds) > 1 else LAT
            hk = h[:, one(g * per + j), 0:w]
            return vec_fn.scalar_tensor_tensor(out=hk, in0=hk, scalar=ALPHA, in1=tmp[:, 0:w].unsqueeze(1), op0=ALU.mult, op1=ALU.add)
        dense(c, name, x, segs, act, vec)

    def feed_forward(layer, conds, segs, hidden):
        w = T if len(conds) > 1 else LAT

        def act(g, j, ps, tmp):
            return act_fn(tmp[:, 0:w], ps[:, 0:w], ACT.Silu if j == 0 else ACT.Copy)

        def vec(g, j, ps, tmp):
            if j == 0:
                return None
            other = c.tmp[:, g_slot[0], 0, 0:w]
            return vec_fn.tensor_tensor(hidden[:, one(g), 0:w], other.unsqueeze(1), tmp[:, 0:w].unsqueeze(1), ALU.mult)
        g_slot = [0]

        def act_s(g, j, ps, tmp):
            return act(g, j, ps, tmp)

        def vec_s(g, j, ps, tmp):
            if j == 0:
                pairs_first[0] = tmp
                return None
            return vec_fn.tensor_tensor(hidden[:, one(g), 0:w], pairs_first[0][:, 0:w].unsqueeze(1), tmp[:, 0:w].unsqueeze(1), ALU.mult)
        pairs_first = [None]
        dense(c, f"ffn_in{layer}", u, segs, act_s, vec_s)
        residual(f"ffn_out{layer}", hidden, layer * 48 + 40, conds, segs)

    def copy_to(dst, off=0, per=2, w=T):
        return lambda g, j, ps, tmp: act_fn(dst[:, one(g * per + (j + off)), 0:w], ps[:, 0:w].unsqueeze(1), ACT.Copy)

    def silu_times(dst, w):
        act = lambda g, j, ps, tmp: act_fn(tmp[:, 0:w], ps[:, 0:w], ACT.Silu)

        def vec(g, j, ps, tmp):
            d = dst[:, one(g * 2 + j), 0:w]
            return vec_fn.tensor_tensor(d, d, tmp[:, 0:w].unsqueeze(1), ALU.mult)
        return act, vec

    modulate(modulated(0))
    rope_x, q_nope = area(0, 5, T), area(5 * T, 8, T)
    lat = area(13 * T, 7, T)
    k_nope = area(20 * T, 8, T)
    v_tok = area(28 * T, 6, D)
    dense(c, "mla_in", u, BOTH, copy_to(lat, per=1))
    moved = c.sem("k_rope_moved")
    with nc.Block() as block:
        @block.vector
        def _(dve):
            vec_fn.tensor_copy(rope_x[:, 4, :], lat[:, 6, :]).then_inc(moved, 1)
    normalise(c, "q_rms", lat, 4, T, BOTH, 1e-6, vcol("mla_q_norm"))
    normalise(c, "kv_rms", lat[:, 4:6, :], 2, T, BOTH, 1e-6, vcol("mla_kv_norm"))
    qx = area(0, 13, T)

    def q_act(g, j, ps, tmp):
        return act_fn(q_nope[:, one(g * 2 + j), :], ps[:, 0:T].unsqueeze(1), ACT.Copy)
    q_all = area(0, 13, T)
    k_hold = lat[:, 6, :]
    dense(c, "q_up", lat, BOTH, lambda g, j, ps, tmp: act_fn(q_all[:, one(g * 2 + (j + 1)), :], ps[:, 0:T].unsqueeze(1), ACT.Copy))
    with nc.Block() as block:
        order = c.sem("rope_order")
        @block.scalar
        def _(act):
            act_fn(q_all[:, 0, :], k_hold, ACT.Copy)
    dense(c, "k_up", lat[:, 4:6, :], BOTH, copy_to(k_nope))
    dense_tokens(c, "v_up", lat[:, 4:6, :], 256, v_tok)
    turn(c, "mla_rope", q_all, 5, area(13 * T, 3, 512), ("mla_trig", "mla_perm"))
    attention(c, "mla", 4, 2, False,
              q=lambda i, j: q_all[:, one(i * 2 + (5 + j)), :],
              k=lambda i, j, a, b: k_nope[:, one(i * 2 + j), a:b].rearrange("p a b -> p (a b)"),
              v=lambda i, j: v_tok[:, :, bass.ds(i * 256 + j * 128, 128)],
              out=lambda i, j, t: q_all[:, one(i * 2 + (5 + j)), 128 * t:128 * t + 128],
              at=13 * T, scale=MLA_SCALE,
              rope=(lambda i: q_all[:, one(i + 1), :],
                    lambda j, a, b: q_all[64 * j:64 * j + 64, 0, a:b]))
    residual("mla_out", q_all[:, 5:13, :], 16, (0, 1), BOTH)
    normalise(c, "ln1_0", h, 8, T, BOTH, 1e-5, vcol("ln1_g0"), vcol("ln1_b0"), after=(u, modulated(24)))
    hidden = area(0, KF, T)
    feed_forward(0, (0, 1), BOTH, hidden)
    normalise(c, "ln2_0", h, 8, T, BOTH, 1e-5, vcol("ln2_g0"), vcol("ln2_b0"), after=(u, modulated(48)))

    c.clear_sems()
    qkv = area(0, 32, T)
    at = 32 * T
    cols = area(at, 8, 6, 6, 2, 2) if False else None
    cols_flat = area(at, 1152)
    cols = cols_flat.rearrange("p (k q t d v) -> p k q t d v", k=8, q=6, t=6, d=2)
    at += 1152
    ba = area(at, 6, 64)
    dense(c, "gdn_qkv", u, BOTH, copy_to(qkv))
    dense_tokens(c, "gdn_ba", u, 64, ba)
    gdn_gates(c, ba, cols, at + 384)
    c.clear_sems()
    gdn_heads(c, qkv, cols, at)
    c.clear_sems()
    o_gdn = qkv[:, 16:32, :]
    head_norm(c, o_gdn, 0, c.vec[:, VEC_AT["gdn_norm"]:VEC_AT["gdn_norm"] + 1])
    modulate(modulated(48, (0,)))
    dense(c, "gdn_z", u, LATS, *silu_times(o_gdn, LAT))
    residual("gdn_out", o_gdn, 48 + 16, (0,), LATS)
    normalise(c, "ln1_1", h, 8, LAT, LATS, 1e-5, vcol("ln1_g1"), vcol("ln1_b1"), after=(u, modulated(48 + 24, (0,))))
    feed_forward(1, (0,), LATS, hidden)
    normalise(c, "ln2_1", h, 8, LAT, LATS, 1e-5, vcol("ln2_g1"), vcol("ln2_b1"))

    c.clear_sems()
    modulate(modulated(96, (2, 3)), loads=ins["ctx_2"])
    qk = area(0, 20, T)
    v2 = area(20 * T, 6, 512)
    dense(c, "att_qk", u, BOTH, copy_to(qk))
    dense_tokens(c, "att_v", u, 256, v2)
    turn(c, "att_rope", qk, 20, area(24 * T, 3, 512), ("att_trig", "att_perm"))
    attention(c, "att", 4, 4, True,
              q=lambda i, j: qk[:, one(i * 4 + j), :],
              k=lambda i, j, a, b: qk[:, one(i + 16), a:b].rearrange("p a b -> p (a b)"),
              v=lambda i, j: v2[:, :, bass.ds(i * 128, 128)],
              out=lambda i, j, t: qk[:, one(i * 4 + j), 128 * t:128 * t + 128],
              at=24 * T, scale=ATT_SCALE,
              sink=lambda i, j: c.vec[:, bass.ds(i * 4 + (VEC_AT["sink"] + j), 1)])
    dense(c, "att_z", u, BOTH, *silu_times(qk, T))
    residual("att_out", qk, 96 + 16, (2, 3), BOTH)
    normalise(c, "ln_2_0", h, 8, T, BOTH, 1e-5, vcol("ln_g_20"), vcol("ln_b_20"), after=(u, modulated(120, (2, 3))))

    c.clear_sems()
    p = area(0, 16, T)
    dense(c, "s5_in", u, BOTH, copy_to(p))
    par = area(16 * T, 16, 5, 8)
    s5_params(c, par, 16 * T + 640)
    s5_scan(c, p, par, 16 * T + 640, lambda i: c.vec[:, bass.ds(i + VEC_AT["s5_d"], 1)])
    gelu(c, p)
    y5 = area(16 * T, 16, LAT)

    def glu_act(g, j, ps, tmp):
        return act_fn(tmp[:, 0:LAT], ps[:, 0:LAT], ACT.Sigmoid, bias=c.vec[:, bass.ds(g + VEC_AT["s5_glu_b"], 1)])

    def glu_vec(g, j, ps, tmp):
        return vec_fn.tensor_tensor(y5[:, one(g), :], p[:, one(g), 0:LAT], tmp[:, 0:LAT].unsqueeze(1), ALU.mult)
    dense(c, "s5_glu", p, LATS, glu_act, glu_vec)
    dense(c, "s5_z", u, LATS, *silu_times(y5, LAT))
    residual("s5_out", y5, 120 + 16, (2,), LATS)
    normalise(c, "ln_2_1", h, 8, LAT, LATS, 1e-5, vcol("ln_g_21"), vcol("ln_b_21"))
    stored = c.sem("stored")
    with nc.Block() as block:
        @block.sync
        def _(sp):
            sp.dma_start(out.rearrange("p (k t) -> p k t", k=KD), h[:, :, 0:LAT]).then_inc(stored, 16)
            sp.wait_ge(stored, 16)


def blocks(w, per, width=128):
    k, n = w.shape
    b = w.reshape(k // 128, 128, n // (per * width), per, width)
    return np.ascontiguousarray(b.transpose(2, 1, 3, 0, 4)).reshape(n // (per * width), 128, -1)


def columns(v):
    return v.reshape(-1, 128).T


def feature_major(x):
    t, n = x.shape
    return np.ascontiguousarray(x.T.reshape(n // 128, 128, t).transpose(1, 0, 2)).reshape(128, -1)


def rope_tables():
    row, col = np.arange(LAT) // GRID_W, np.arange(LAT) % GRID_W
    out = {}
    for name, width, half in (("mla", 64, 16), ("att", 128, 32)):
        ch = np.arange(128) % width
        inv = (10000.0 ** (-(ch % half).astype(np.float64) / half)).astype(np.float32)
        pos = np.where((ch // (2 * half) % 2)[:, None] == 0, row[None, :], col[None, :]).astype(np.float32)
        ang = (pos * inv[:, None]).astype(np.float32)
        sign = np.where((ch // half) % 2 == 0, -1.0, 1.0)[:, None]
        out[name + "_trig"] = np.concatenate([np.cos(ang), np.sin(ang) * sign], 1).astype(np.float32)
        out[name + "_perm"] = np.eye(128, dtype=np.float32)[np.arange(128) ^ half]
    return out


def constants():
    i = np.arange(128)
    out = {"ones": np.ones((128, 128)), "ident": np.eye(128)}
    fwd = (i[:, None] <= i[None, :]).astype(np.float32)
    out["tri"] = np.concatenate([fwd, fwd.T], 1)
    levels = []
    for l in range(LEVELS):
        s = 1 << l
        m = (i[:, None] // (2 * s) == i[None, :] // (2 * s)) & (i[None, :] // s % 2 == 1) & (i[:, None] // s % 2 == 0)
        levels += [m, m.T]
    out["level_masks"] = np.concatenate(levels, 1)
    a, b = i[:, None], i[None, :]
    out["window_mask"] = np.concatenate([np.where(b >= a, 0, -1e30), np.zeros((128, 128)), np.where(b <= a, 0, -1e30)], 1)
    out["s5_steps"] = np.broadcast_to(np.arange(1, T + 1), (128, T))
    out = {k: np.ascontiguousarray(v, dtype=np.float32) for k, v in out.items()}
    out.update(rope_tables())
    return out


def layouts(x):
    a = constants()
    a["x"], a["ctx"], a["ctx_2"] = feature_major(x["x"][0]), feature_major(x["ctx"][0]), feature_major(x["ctx_2"][0])
    a["w_mod"] = np.concatenate([blocks(w, 2) for w in (*x["w_mod"], *x["ada_w_2"])])
    w = x["mla_w_in"][0]
    a["w_mla_in"] = blocks(np.concatenate([w, w[:, 768:832]], 1), 1)
    q = x["mla_w_q_up"][0].reshape(512, HEADS, 192)
    a["w_q_up"] = blocks(np.concatenate([q[:, :, 128:].reshape(512, 512), q[:, :, :128].reshape(512, 1024)], 1), 2)
    kv = x["mla_w_kv_up"][0].reshape(256, HEADS, 256)
    a["w_k_up"] = blocks(np.ascontiguousarray(kv[:, :, :128]).reshape(256, 1024), 2)
    a["w_v_up"] = blocks(np.ascontiguousarray(kv[:, :, 128:]).reshape(256, 1024), 1, 256)
    a["w_mla_out"] = blocks(x["mla_w_out"][0], 2)
    for l in range(2):
        f = x["w_ffn_in"][l].reshape(D, 2, KF, 128).transpose(0, 2, 1, 3).reshape(D, 2 * FF)
        a[f"w_ffn_in{l}"] = blocks(f, 2)
        a[f"w_ffn_out{l}"] = blocks(x["w_ffn_out"][l], 1)
    w = x["gdn_w_in"][0]
    a["w_gdn_qkv"], a["w_gdn_z"], a["w_gdn_ba"] = blocks(w[:, :4096], 2), blocks(w[:, 4096:6144], 2), blocks(w[:, 6144:], 1, 64)
    a["w_gdn_out"] = blocks(x["gdn_w_out"][0], 1)
    a["gdn_taps"] = np.ascontiguousarray(x["gdn_conv"][0].T.reshape(32, 128, 5).transpose(1, 0, 2)).reshape(128, 160)
    rows = np.concatenate([x["gdn_a_log"][0].reshape(32), x["gdn_dt_bias"][0].reshape(32)])
    a["gdn_rows"] = np.ascontiguousarray(np.broadcast_to(rows, (128, 64)))
    w = x["attn_w_in_2"][0]
    a["w_att_qk"], a["w_att_v"], a["w_att_z"] = blocks(w[:, :2560], 2), blocks(w[:, 2560:3072], 1, 256), blocks(w[:, 3072:], 2)
    a["w_att_out"], a["w_s5_out"] = blocks(x["w_out_2"][0], 1), blocks(x["w_out_2"][1], 1)
    w = x["s5_w_in_2"][0]
    a["w_s5_in"], a["w_s5_z"] = blocks(w[:, :2048], 2), blocks(w[:, 2048:], 2)
    a["w_s5_glu"] = blocks(x["s5_glu_w_2"][0], 1)
    st = lambda v: v.reshape(2, 16, 4, 128).transpose(3, 1, 0, 2).reshape(128, 128)
    step = np.repeat(x["s5_log_step_2"][0][:, :, None], 64, 2)
    a["s5_lam"] = np.concatenate([st(x["s5_lam_re_2"][0]), st(x["s5_lam_im_2"][0]), st(step)], 1)
    b = np.stack([x["s5_b_re_2"][0], x["s5_b_im_2"][0]]).reshape(2, 2, 16, 4, 2, 64, 16)
    bm = np.zeros((16, 4, 2, 16, 2, 2, 2, 64), np.float32)
    cm = np.zeros((16, 2, 64, 2, 4, 2, 2, 16), np.float32)
    cc = np.stack([x["s5_c_re_2"][0], x["s5_c_im_2"][0]]).reshape(2, 2, 16, 4, 2, 16, 64)
    for g in range(2):
        bm[:, :, g, :, :, :, g, :] = b[:, :, :, :, g].transpose(2, 3, 5, 1, 0, 4)
        cm[:, g, :, :, :, :, g, :] = cc[:, :, :, :, g].transpose(2, 5, 1, 3, 0, 4)
    a["s5_b"], a["s5_c"] = bm.reshape(16, 128, 512), cm.reshape(16, 128, 512)
    vec = {"sink": np.broadcast_to(x["attn_sink_2"][0], (128, 16)), "c": columns(x["c"][0]), "c_ctx": columns(x["c_ctx"]),
           "c_2": columns(x["c_2"][0]), "c_ctx_2": columns(x["c_ctx_2"]), "mla_q_norm": columns(x["mla_q_norm"][0]),
           "mla_kv_norm": columns(x["mla_kv_norm"][0]), "gdn_norm": columns(x["gdn_norm"][0]), "s5_d": columns(x["s5_d_2"][0]),
           "s5_glu_b": columns(x["s5_glu_b_2"][0])}
    for l in range(2):
        for n in ("b_mod", "ln1_g", "ln1_b", "ln2_g", "ln2_b", "ada_b_2", "ln_g_2", "ln_b_2"):
            vec[f"{n}{l}"] = columns(x[n][l])
    a["vecs"] = np.concatenate([vec[n] for n, _ in VECS], 1)
    return {k: np.ascontiguousarray(v) for k, v in a.items()}


def kernel(**inputs):
    import concourse.bacc as bacc
    from concourse.bass_utils import run_bass_kernel_spmd
    names = [n for n, v in inputs.items() if v.size]
    arrays = layouts({n: np.asarray(inputs[n]) for n in names})
    nc = bacc.Bacc("TRN2", target_bir_lowering=False, num_devices=1)
    ins = {n: nc.dram_tensor("in_" + n, v.shape, F32, kind="ExternalInput").ap() for n, v in arrays.items()}
    out = nc.dram_tensor("out", (128, KD * LAT), F32, kind="ExternalOutput").ap()
    program(nc, ins, out)
    r = run_bass_kernel_spmd(nc, [{"in_" + n: v for n, v in arrays.items()}], core_ids=[0])
    y = r.results[0]["out"].reshape(128, KD, LAT)
    return np.ascontiguousarray(y.transpose(2, 1, 0)).reshape(1, LAT, D)
```

```python
import numpy as np
import concourse.bass as bass
from concourse import mybir

F32 = mybir.dt.float32
ACT = mybir.ActivationFunctionType
ALU = mybir.AluOpType
AX = mybir.AxisListType

D = 1024
LAT, CTX = 512, 256
T = LAT + CTX
KD = D // 128
GRID_W = 64
ALPHA = 4.0 ** 0.25
FF = 2816
KF = FF // 128
SLOT = KF * 128
HEADS = 8
MLA_SCALE = 192 ** -0.5
ATT_SCALE = 128 ** -0.5
BOTH = ((0, 512), (512, 768))
LATS = ((0, 512),)
LEVELS = 7


def pairs(eng, groups, body):
    for g in range(min(2, groups)):
        body(g, g, True)
    if groups > 3:
        with eng.Fori(1, groups // 2) as p:
            for s in range(2):
                body(p * 2 + s, s, False)
    if groups > 2 and groups % 2:
        body(groups - 1, 0, False)


def one(g):
    return bass.ds(g, 1)


def rows_of(dram, g):
    return dram[one(g), :, :].rearrange("o p n -> (o p) n")


PRODUCTS = [
    ("mod", 8, 2), ("mla_in", 8, 1), ("q_up", 4, 2), ("k_up", 2, 2), ("v_up", 2, 2), ("mla_out", 8, 2),
    ("ffn_in0", 8, 2), ("ffn_out0", KF, 1),
    ("gdn_qkv", 8, 2), ("gdn_ba", 8, 1), ("gdn_z", 8, 2), ("gdn_out", 16, 1), ("ffn_in1", 8, 2), ("ffn_out1", KF, 1),
    ("att_qk", 8, 2), ("att_v", 8, 2), ("att_z", 8, 2), ("att_out", 16, 1),
    ("s5_in", 8, 2), ("s5_glu", 16, 1), ("s5_z", 8, 2), ("s5_out", 16, 1),
]


class Core:

    def __init__(self, nc, ins):
        self.nc, self.ins = nc, ins
        self.sems, self.live = 0, []
        f = lambda name, *shape: nc.alloc_sbuf_tensor(name, [128, *shape], F32)
        self.h = f("h", KD, T)
        self.u = f("u", KD, T)
        self.ring = f("ring", 2, SLOT)
        self.tmp = f("tmp", 2, 2, T)
        self.mod = f("mod", 144, 4)
        self.vec = f("vec", ins["vecs"].shape[1])
        self.ones = f("ones", 128)
        self.ident = f("ident", 128)
        self.stat = f("stat", 2, T)
        self.area_size = (nc.sbuf_bytes_remaining // 4) - 64
        self.area = f("area", self.area_size)
        self.P = nc.alloc_psum_tensor("P", [128, 4, 1024], F32)
        self.ring_ready = [self.sem(f"ring_ready{s}") for s in range(2)]
        self.mm_done = self.sem("mm_done")
        self.live = []
        self.first = {}
        n = 0
        for name, _, _ in PRODUCTS:
            self.first[name] = n
            n += ins["w_" + name].shape[0]
        self.total = n

    def sem(self, name):
        self.sems += 1
        got = self.nc.alloc_semaphore(f"{name}_{self.sems}")
        self.live.append(got)
        return got

    def clear_sems(self):
        self.nc.clear_and_free_semaphores(self.live)
        self.nc.all_engine_barrier()
        self.live = []

    def view(self, at, *shape):
        n = int(np.prod(shape))
        assert at + n <= self.area_size, (at, shape, self.area_size)
        v = self.area[:, at:at + n]
        names = "abcd"[:len(shape)]
        if len(shape) > 1:
            v = v.rearrange(f"p ({' '.join(names)}) -> p {' '.join(names)}", **dict(zip(names[1:], shape[1:])))
        return v

    def load_slot(self, sp, name, g, slot):
        w = self.ins["w_" + name]
        n = w.shape[2]
        sp.dma_start(self.ring[:, slot, 0:n], rows_of(w, g)).then_inc(self.ring_ready[slot], 16)

    def prefetch(self, sp, name):
        order = [p[0] for p in PRODUCTS]
        i = order.index(name) + 1
        if i == len(order):
            return
        at = self.first[order[i]]
        for g in range(min(2, self.ins["w_" + order[i]].shape[0])):
            sp.wait_ge(self.mm_done, at + g - 1)
            self.load_slot(sp, order[i], g, (at + g) % 2)

    def shape_of(self, name):
        return next((kt, per) for n, kt, per in PRODUCTS if n == name)


def stream(c, sp, name, ahead=True):
    at, groups = c.first[name], c.ins["w_" + name].shape[0]

    def body(g, s, first):
        if not first:
            sp.wait_ge(c.mm_done, g + (at - 1))
            c.load_slot(sp, name, g, (at + s) % 2)
    pairs(sp, groups, body)
    if ahead:
        c.prefetch(sp, name)


def dense(c, name, x, segs, act, vec=None, act_frees=True):
    nc = c.nc
    kt, per = c.shape_of(name)
    at, groups = c.first[name], c.ins["w_" + name].shape[0]
    act_done, vec_done = c.sem(name + "_act_done"), c.sem(name + "_vec_done")
    freed = act_done if act_frees else vec_done
    with nc.Block() as block:
        @block.sync
        def _(sp):
            stream(c, sp, name)

        @block.tensor
        def _(pe):
            def body(g, s, first):
                slot = (at + s) % 2
                pe.wait_ge(c.ring_ready[slot], (g - s) * 8 + 16 * ((at + s) // 2 + 1))
                if not first:
                    pe.wait_ge(freed, g - 1)
                for j in range(per):
                    for a, b in segs:
                        for k in range(kt):
                            last = nc.tensor.matmul(
                                c.P[:, 2 * s + j, a:b], c.ring[:, slot, (j * kt + k) * 128:(j * kt + k + 1) * 128],
                                x[:, k, a:b], start=k == 0, stop=k == kt - 1)
                last.then_inc(c.mm_done, 1)
            pairs(pe, groups, body)

        @block.scalar
        def _(eng):
            def body(g, s, first):
                eng.wait_ge(c.mm_done, g + (at + 1))
                if vec and not first:
                    eng.wait_ge(vec_done, g - 1)
                for j in range(per):
                    last = act(g, j, c.P[:, 2 * s + j, :], c.tmp[:, s, j, :])
                last.then_inc(act_done, 1)
            pairs(eng, groups, body)

        if vec:
            @block.vector
            def _(eng):
                def body(g, s, first):
                    eng.wait_ge(act_done, g + 1)
                    for j in range(per):
                        last = vec(g, j, c.P[:, 2 * s + j, :], c.tmp[:, s, j, :])
                    last.then_inc(vec_done, 1)
                pairs(eng, groups, body)


def dense_tokens(c, name, x, width, out, ahead=True):
    nc = c.nc
    kt, _ = c.shape_of(name)
    at, groups = c.first[name], c.ins["w_" + name].shape[0]
    copied = c.sem(name + "_copied")
    psum = c.P[:, :, :].rearrange("p a b -> p (a b)")
    with nc.Block() as block:
        @block.sync
        def _(sp):
            stream(c, sp, name, ahead)

        @block.tensor
        def _(pe):
            def body(g, s, first):
                slot = (at + s) % 2
                pe.wait_ge(c.ring_ready[slot], (g - s) * 8 + 16 * ((at + s) // 2 + 1))
                if not first:
                    pe.wait_ge(copied, g - 1)
                for t in range(T // 128):
                    for k in range(kt):
                        last = nc.tensor.matmul(
                            psum[:, 2048 * s + t * width:2048 * s + (t + 1) * width], x[:, k, t * 128:(t + 1) * 128],
                            c.ring[:, slot, k * width:(k + 1) * width], start=k == 0, stop=k == kt - 1)
                last.then_inc(c.mm_done, 1)
            pairs(pe, groups, body)

        @block.scalar
        def _(eng):
            def body(g, s, first):
                eng.wait_ge(c.mm_done, g + (at + 1))
                nc.scalar.activation(out[:, :, bass.ds(g * width, width)],
                                     psum[:, 2048 * s:2048 * s + T // 128 * width].rearrange("p (t n) -> p t n", n=width),
                                     ACT.Copy).then_inc(copied, 1)
            pairs(eng, groups, body)


def spread(ap, n, axis=1):
    return ap.unsqueeze(axis).broadcast_to([ap.shape[0], n, ap.shape[1]]) if axis == 1 else None


def normalise(c, name, src, kt, width, segs, eps, gain, shift=None, after=None):
    nc = c.nc
    inv = 1.0 / (kt * 128)
    s = {n: c.sem(f"{name}_{n}") for n in ("mean", "centred", "sq", "sq_used", "var", "sd", "rs", "unit", "affine")}
    ps_mean, ps_var = c.P[:, 0, 0:width], c.P[:, 1, 0:width]
    sq = [c.tmp[:, 0, 0, 0:width], c.tmp[:, 1, 0, 0:width]]
    sd, rs = c.stat[:, 0, 0:width], c.stat[:, 1, 0:width]
    x = src[:, 0:kt, 0:width]
    with nc.Block() as block:
        @block.tensor
        def _(pe):
            if shift is not None:
                for a, b in segs:
                    for k in range(kt):
                        last = nc.tensor.matmul(ps_mean[:, a:b], c.ones[:, :], src[:, k, a:b], start=k == 0, stop=k == kt - 1)
                last.then_inc(s["mean"], 1)
            for k in range(kt):
                pe.wait_ge(s["sq"], k + 1)
                for a, b in segs:
                    last = nc.tensor.matmul(ps_var[:, a:b], c.ones[:, :], sq[k % 2][:, a:b], start=k == 0, stop=k == kt - 1)
                last.then_inc(s["sq_used"], 1)

        @block.scalar
        def _(act):
            if shift is not None:
                act.wait_ge(s["centred"], 1)
            for k in range(kt):
                if k >= 2:
                    act.wait_ge(s["sq_used"], k - 1)
                nc.scalar.activation(sq[k % 2], src[:, k, 0:width], ACT.Square).then_inc(s["sq"], 1)
            act.wait_ge(s["var"], 1)
            nc.scalar.activation(sd, sd, ACT.Sqrt).then_inc(s["sd"], 1)
            if after:
                out, parts = after
                for k in range(kt):
                    act.wait_ge(s["affine"], k + 1)
                    for scale, add, a, b in parts:
                        nc.scalar.activation(out[:, k, a:b], src[:, k, a:b], ACT.Identity, scale=scale(k), bias=add(k))

        @block.vector
        def _(dve):
            if shift is not None:
                dve.wait_ge(s["mean"], 1)
                nc.vector.scalar_tensor_tensor(out=x, in0=spread(ps_mean, kt), scalar=-inv, in1=x,
                                               op0=ALU.mult, op1=ALU.add).then_inc(s["centred"], 1)
            dve.wait_ge(s["sq_used"], kt)
            nc.vector.tensor_scalar(sd, ps_var, inv, eps, ALU.mult, ALU.add).then_inc(s["var"], 1)
            dve.wait_ge(s["sd"], 1)
            nc.vector.reciprocal(rs, sd).then_inc(s["rs"], 1)
            dve.wait_ge(s["rs"], 1)
            nc.vector.tensor_tensor(x, x, spread(rs, kt), ALU.mult).then_inc(s["unit"], 1)
            dve.wait_ge(s["unit"], 1)
            for k in range(kt):
                if shift is not None:
                    nc.vector.tensor_scalar(src[:, k, 0:width], src[:, k, 0:width], gain(k), shift(k),
                                            ALU.mult, ALU.add).then_inc(s["affine"], 1)
                else:
                    nc.vector.tensor_scalar(src[:, k, 0:width], src[:, k, 0:width], gain(k), None,
                                            ALU.mult).then_inc(s["affine"], 1)


def turn(c, name, x, blocks, tables, perm):
    nc = c.nc
    landed, partner, turned, kept, done = (c.sem(f"{name}_{n}") for n in ("landed", "partner", "turned", "kept", "done"))
    cos, sin, perm_sb = tables[:, 0, :], tables[:, 1, :], tables[:, 2, 0:128]
    with nc.Block() as block:
        @block.sync
        def _(sp):
            sp.dma_start(tables[:, 0:2, :].rearrange("p a b -> p (a b)"), c.ins[perm[0]]).then_inc(landed, 16)
            sp.dma_start(perm_sb, c.ins[perm[1]]).then_inc(landed, 16)

        @block.tensor
        def _(pe):
            pe.wait_ge(landed, 32)
            for n in range(blocks):
                if n >= 4:
                    pe.wait_ge(turned, n - 3)
                nc.tensor.matmul(c.P[:, n % 4, 0:LAT], perm_sb, x[:, n, 0:LAT], start=True, stop=True).then_inc(partner, 1)

        @block.vector
        def _(dve):
            dve.wait_ge(landed, 32)
            for n in range(blocks):
                dve.wait_ge(partner, n + 1)
                if n >= 2:
                    dve.wait_ge(done, n - 1)
                nc.vector.tensor_tensor(c.tmp[:, n % 2, 0, 0:LAT], c.P[:, n % 4, 0:LAT], sin, ALU.mult).then_inc(turned, 1)
                nc.vector.tensor_tensor(x[:, n, 0:LAT], x[:, n, 0:LAT], cos, ALU.mult).then_inc(kept, 1)
                dve.wait_ge(turned, n + 1)
                dve.wait_ge(kept, n + 1)
                nc.vector.tensor_tensor(x[:, n, 0:LAT], x[:, n, 0:LAT], c.tmp[:, n % 2, 0, 0:LAT], ALU.add).then_inc(done, 1)


def attention(c, name, rounds, per, window, q, k, v, out, at, scale, rope=None, sink=None):
    nc = c.nc
    qs, vs = c.view(at, per, T), c.view(at + per * T, per, T // 128, 128)
    at += 2 * per * T
    if rope:
        rs = c.view(at, T)
        at += T
    prob, probT = c.tmp[:, 0, :, :], c.tmp[:, 1, :, :]
    small = c.stat[:, 0, 0:16].rearrange("p (a b) -> p a b", a=2)
    mask = None
    if window:
        mask = c.view(at, 3 * 128)
    units = []
    for j in range(per):
        for t in range(T // 128):
            if t >= LAT // 128:
                tiles = [4, 5]
            elif window:
                tiles = list(range(max(0, t - 1), min(4, t + 2))) + [4, 5]
            else:
                tiles = list(range(6))
            units.append((j, t, tiles))
    U = len(units)
    S = [c.P[:, 0, :], c.P[:, 1, :]]
    TP = c.P[:, 2, :]
    O = [c.P[:, 3, 0:128], c.P[:, 3, 512:640]]
    sem = {n: c.sem(f"{name}_{n}") for n in
           ("const", "staged", "head", "score", "masked", "top", "peak", "negpeak", "prob", "sinkexp", "total", "inv",
            "unit", "turned", "probT", "o", "ocopied")}
    with nc.Block() as block:
        if window:
            @block.sync
            def _(sp):
                sp.dma_start(mask, c.ins["window_mask"]).then_inc(sem["const"], 16)

        @block.gpsimd
        def _(pool):
            def body(i, s, first):
                for j in range(per):
                    if not first:
                        pool.wait_ge(sem["o"], (i - 1) * U + (j + 1) * (U // per))
                    elif i:
                        pool.wait_ge(sem["o"], (i - 1) * U + (j + 1) * (U // per))
                    if rope and j == 0:
                        if not (first and i == 0):
                            pool.wait_ge(sem["o"], i * U)
                        nc.gpsimd.tensor_copy(rs[:, :].unsqueeze(1), rope[0](i))
                    nc.gpsimd.tensor_copy(qs[:, j, :].unsqueeze(1), q(i, j))
                    nc.gpsimd.tensor_copy(vs[:, j, :, :], v(i, j)).then_inc(sem["staged"], 1)
            body(0, 0, True)
            with pool.Fori(1, rounds) as i:
                body(i, 0, False)

        @block.tensor
        def _(pe):
            def body(i, first):
                def score(n):
                    j, t, tiles = units[n]
                    w = 128 * (len(tiles) - 2)
                    if t == 0:
                        pe.wait_ge(sem["staged"], i * per + (j + 1))
                    if not (first and n < 2):
                        pe.wait_ge(sem["prob"], i * U + (n - 1))
                    segs = ([(512 - w, 512, tiles[0] * 128)] if w else []) + [(512, 768, 512)]
                    for a, b, key in segs:
                        last = nc.tensor.matmul(S[n % 2][:, a:b], qs[:, j, t * 128:t * 128 + 128],
                                                k(i, j, key, key + b - a), start=True, stop=rope is None)
                        if rope:
                            last = nc.tensor.matmul(S[n % 2][:, a:b], rs[64 * j:64 * j + 64, t * 128:t * 128 + 128],
                                                    rope[1](j, key, key + b - a), start=False, stop=True)
                    last.then_inc(sem["score"], 1)

                def flip(n):
                    pe.wait_ge(sem["unit"], i * U + (n + 1))
                    if not (first and n == 0):
                        pe.wait_ge(sem["probT"], i * U + n)
                    nb = len(units[n][2])
                    for b in range(nb):
                        a = 768 - 128 * nb + 128 * b
                        last = nc.tensor.transpose(TP[:, b * 128:b * 128 + 128], prob[:, n % 2, a:a + 128], c.ident[:, :])
                    last.then_inc(sem["turned"], 1)

                def value(n):
                    j, t, tiles = units[n]
                    pe.wait_ge(sem["probT"], i * U + (n + 1))
                    if not (first and n < 2):
                        pe.wait_ge(sem["ocopied"], i * U + (n - 1))
                    for b, key in enumerate(tiles):
                        last = nc.tensor.matmul(O[n % 2], vs[:, j, key, :], probT[:, n % 2, b * 128:b * 128 + 128],
                                                start=b == 0, stop=b == len(tiles) - 1)
                    last.then_inc(sem["o"], 1)
                for n in range(U + 2):
                    if n < U:
                        score(n)
                    if 1 <= n <= U:
                        flip(n - 1)
                    if n >= 2:
                        value(n - 2)
            body(0, True)
            with pe.Fori(1, rounds) as i:
                body(i, False)

        @block.scalar
        def _(act):
            def body(i, first):
                def exps(n):
                    a = 768 - 128 * len(units[n][2])
                    act.wait_ge(sem["negpeak"], i * U + (n + 1))
                    if not (first and n < 2):
                        act.wait_ge(sem["turned"], i * U + (n - 1))
                    nc.scalar.activation(prob[:, n % 2, a:768], prob[:, n % 2, a:768] if window else S[n % 2][:, a:768],
                                         ACT.Exp, bias=small[:, n % 2, 1:2], scale=scale,
                                         accum_out=small[:, n % 2, 2:3]).then_inc(sem["prob"], 1)
                    if sink:
                        nc.scalar.activation(small[:, n % 2, 3:4], sink(i, units[n][0]), ACT.Exp,
                                             bias=small[:, n % 2, 1:2]).then_inc(sem["sinkexp"], 1)

                def copy(n):
                    nb = len(units[n][2])
                    act.wait_ge(sem["turned"], i * U + (n + 1))
                    if not (first and n < 2):
                        act.wait_ge(sem["o"], i * U + (n - 1))
                    nc.scalar.activation(probT[:, n % 2, 0:nb * 128], TP[:, 0:nb * 128], ACT.Copy).then_inc(sem["probT"], 1)
                for n in range(U + 1):
                    if n < U:
                        exps(n)
                    if n >= 1:
                        copy(n - 1)
            body(0, True)
            with act.Fori(1, rounds) as i:
                body(i, False)

        @block.vector
        def _(dve):
            if window:
                dve.wait_ge(sem["const"], 16)

            def body(i, first):
                def peak(n):
                    j, t, tiles = units[n]
                    a = 768 - 128 * len(tiles)
                    dve.wait_ge(sem["score"], i * U + (n + 1))
                    seen = S[n % 2]
                    if window:
                        if not (first and n < 2):
                            dve.wait_ge(sem["turned"], i * U + (n - 1))
                        if t < 4:
                            m0 = 128 * (tiles[0] - t + 1)
                            nc.vector.tensor_tensor(prob[:, n % 2, a:512], seen[:, a:512], mask[:, m0:m0 + 512 - a], ALU.add)
                        nc.vector.tensor_copy(prob[:, n % 2, 512:768], seen[:, 512:768]).then_inc(sem["masked"], 1)
                        dve.wait_ge(sem["masked"], i * U + (n + 1))
                        seen = prob[:, n % 2, :]
                    nc.vector.reduce_max(small[:, n % 2, 0:1], seen[:, a:768], AX.X).then_inc(sem["top"], 1)
                    dve.wait_ge(sem["top"], i * U + (n + 1))
                    if sink:
                        nc.vector.tensor_scalar(small[:, n % 2, 4:5], small[:, n % 2, 0:1], scale, None, ALU.mult
                                                ).then_inc(sem["peak"], 1)
                        dve.wait_ge(sem["peak"], i * U + (n + 1))
                        nc.vector.tensor_scalar(small[:, n % 2, 1:2], small[:, n % 2, 4:5], sink(i, j), -1.0, ALU.max, ALU.mult
                                                ).then_inc(sem["negpeak"], 1)
                    else:
                        nc.vector.tensor_scalar(small[:, n % 2, 1:2], small[:, n % 2, 0:1], -scale, None, ALU.mult
                                                ).then_inc(sem["negpeak"], 1)

                def finish(n):
                    a = 768 - 128 * len(units[n][2])
                    dve.wait_ge(sem["prob"], i * U + (n + 1))
                    total = small[:, n % 2, 2:3]
                    if sink:
                        dve.wait_ge(sem["sinkexp"], i * U + (n + 1))
                        total = small[:, n % 2, 5:6]
                        nc.vector.tensor_tensor(total, small[:, n % 2, 2:3], small[:, n % 2, 3:4], ALU.add).then_inc(sem["total"], 1)
                        dve.wait_ge(sem["total"], i * U + (n + 1))
                    nc.vector.reciprocal(small[:, n % 2, 6:7], total).then_inc(sem["inv"], 1)
                    dve.wait_ge(sem["inv"], i * U + (n + 1))
                    nc.vector.tensor_scalar(prob[:, n % 2, a:768], prob[:, n % 2, a:768], small[:, n % 2, 6:7], None, ALU.mult
                                            ).then_inc(sem["unit"], 1)

                def keep(n):
                    j, t, _ = units[n]
                    dve.wait_ge(sem["o"], i * U + (n + 1))
                    nc.vector.tensor_copy(out(i, j, t), O[n % 2].unsqueeze(1)).then_inc(sem["ocopied"], 1)
                for n in range(U + 2):
                    if n < U:
                        peak(n)
                    if 1 <= n <= U:
                        finish(n - 1)
                    if n >= 2:
                        keep(n - 2)
            body(0, True)
            with dve.Fori(1, rounds) as i:
                body(i, False)


class Flag:

    def __init__(self, c, name, per):
        self.sem, self.per = c.sem(name), per

    def up(self, instruction):
        instruction.then_inc(self.sem, 1)

    def wait(self, eng, i, n):
        if isinstance(i, int) and i * self.per + n <= 0:
            return
        eng.wait_ge(self.sem, i * self.per + n)


def four(ap):
    return ap.rearrange("p (d v t) -> p d v t", d=2, v=2)


def over_heads(ap, d):
    return ap[:, d:d + 1, :].broadcast_to([128, 2, 128])


def gdn_gates(c, ba, cols, at):
    nc = c.nc
    N = 6 * 32
    tri = c.view(at, 2, 128)
    rows = c.view(at + 256, 2, 32)
    w = [c.view(at + 320 + N * n, 6, 32) for n in range(6)]
    names = "bcgv"
    b_in = ba.rearrange("p t (d k h) -> p t d k h", d=2, k=2)[:, :, :, 0, :]
    a_in = ba.rearrange("p t (d k h) -> p t d k h", d=2, k=2)[:, :, :, 1, :]
    tdh = lambda x: x.rearrange("p t (d h) -> p t d h", d=2)
    flat = lambda x: x.rearrange("p t h -> p (t h)")
    quantity = lambda q, d: cols[:, :, q, :, d, :].rearrange("p k t v -> p t k v")
    s = {n: c.sem("gates_" + n) for n in ("landed", "a", "act", "dve", "pe")}
    cum, tot = c.P[:, 0, 0:2 * 96], c.P[:, 1, 0:2 * 96]
    with nc.Block() as block:
        @block.sync
        def _(sp):
            sp.dma_start(tri[:, :, :].rearrange("p a b -> p (a b)"), c.ins["tri"]).then_inc(s["landed"], 16)
            sp.dma_start(rows[:, :, :].rearrange("p a b -> p (a b)"), c.ins["gdn_rows"]).then_inc(s["landed"], 16)

        @block.scalar
        def _(act):
            act.wait_ge(s["landed"], 32)
            nc.scalar.activation(rows[:, 0, :], rows[:, 0, :], ACT.Exp).then_inc(s["act"], 1)
            act.wait_ge(s["dve"], 3)
            nc.scalar.activation(flat(w[1]), flat(w[1]), ACT.Exp).then_inc(s["act"], 1)
            nc.scalar.activation(flat(w[5]), flat(w[5]), ACT.Exp).then_inc(s["act"], 1)
            act.wait_ge(s["dve"], 4)
            nc.scalar.activation(flat(w[1]), flat(w[1]), ACT.Ln).then_inc(s["act"], 1)
            act.wait_ge(s["dve"], 9)
            nc.scalar.activation(flat(w[1]), flat(w[2]), ACT.Exp).then_inc(s["act"], 1)
            nc.scalar.activation(flat(w[0]), flat(w[0]), ACT.Exp).then_inc(s["act"], 1)
            nc.scalar.activation(flat(w[3]), flat(w[3]), ACT.Exp).then_inc(s["act"], 1)

        @block.vector
        def _(dve):
            n = [0]

            def step(ins):
                ins.then_inc(s["dve"], 1)
                n[0] += 1
                dve.wait_ge(s["dve"], n[0])
            dve.wait_ge(s["landed"], 32)
            for d in range(2):
                last = nc.vector.tensor_tensor(tdh(w[0])[:, :, d, :], a_in[:, :, d, :],
                                               rows[:, 1, 16 * d:16 * d + 16].unsqueeze(1).broadcast_to([128, 6, 16]), ALU.add)
            step(last)
            nc.vector.tensor_scalar(flat(w[1]), flat(w[0]), -1.0, None, ALU.mult).then_inc(s["dve"], 1)
            n[0] += 1
            dve.wait_ge(s["dve"], n[0])
            for d in range(2):
                nc.vector.tensor_scalar(tdh(w[5])[:, :, d, :], b_in[:, :, d, :], -1.0, None, ALU.mult)
            step(nc.vector.tensor_tensor(flat(w[1]), flat(w[1]), flat(w[0]), ALU.min))
            dve.wait_ge(s["act"], 2)
            step(nc.vector.tensor_scalar(flat(w[1]), flat(w[1]), 1.0, None, ALU.add))
            dve.wait_ge(s["act"], 4)
            step(nc.vector.scalar_tensor_tensor(out=flat(w[0]), in0=flat(w[0]), scalar=0.0, in1=flat(w[1]), op0=ALU.max, op1=ALU.add))
            step(nc.vector.scalar_tensor_tensor(out=w[0], in0=w[0], scalar=-1.0,
                                                in1=rows[:, 0, :].unsqueeze(1).broadcast_to([128, 6, 32]), op0=ALU.mult, op1=ALU.mult))
            for d in range(2):
                for t in range(6):
                    last = nc.vector.tensor_copy(cols[:, :, 5, t, d, :], w[0][:, t, 16 * d:16 * d + 16].rearrange("p (k v) -> p k v", v=2))
            step(last)
            nc.vector.tensor_scalar(flat(w[5]), flat(w[5]), 1.0, None, ALU.add).then_inc(s["dve"], 1)
            n[0] += 1
            dve.wait_ge(s["pe"], 1)
            dve.wait_ge(s["dve"], n[0])
            nc.vector.reciprocal(flat(w[4]), flat(w[5]))
            for d in range(2):
                nc.vector.tensor_copy(tdh(w[2])[:, :, d, :], cum[:, 96 * d:96 * d + 96].rearrange("p (t h) -> p t h", h=16))
                last = nc.vector.tensor_copy(tdh(w[0])[:, :, d, :], tot[:, 96 * d:96 * d + 96].rearrange("p (t h) -> p t h", h=16))
            last.then_inc(s["a"], 1)
            dve.wait_ge(s["a"], 1)
            step(nc.vector.tensor_tensor(flat(w[3]), flat(w[0]), flat(w[2]), ALU.subtract))
            dve.wait_ge(s["act"], 7)
            nc.vector.scalar_tensor_tensor(out=flat(w[1]), in0=flat(w[1]), scalar=-1.0, in1=flat(w[4]), op0=ALU.mult, op1=ALU.mult)
            step(nc.vector.tensor_scalar(flat(w[5]), flat(w[2]), -1.0, None, ALU.mult))
            for q, x in ((0, w[4]), (1, w[1]), (2, w[5]), (3, w[3]), (4, w[0])):
                for d in range(2):
                    for t in range(6):
                        nc.vector.tensor_copy(cols[:, :, q, t, d, :], x[:, t, 16 * d:16 * d + 16].rearrange("p (k v) -> p k v", v=2))

        @block.tensor
        def _(pe):
            pe.wait_ge(s["dve"], 7)
            for d in range(2):
                g = tdh(w[0])[:, :, d, :]
                nc.tensor.matmul(cum[:, 96 * d:96 * d + 96], tri[:, d, :], g, start=True, stop=True)
                last = nc.tensor.matmul(tot[:, 96 * d:96 * d + 96], c.ones[:, :], g, start=True, stop=True)
            last.then_inc(s["pe"], 1)


def gdn_heads(c, qkv, cols, at):
    nc = c.nc
    u = c.u[:, :, :].rearrange("p a b -> p (a b)")
    tmp = c.tmp[:, :, :, :].rearrange("p a b c -> p (a b c)")
    stat = c.stat[:, :, :].rearrange("p a b -> p (a b)")
    masks = c.view(at, LEVELS, 2, 128)
    tri = c.view(at + LEVELS * 256, 2, 128)
    at += (LEVELS + 1) * 256
    col = c.view(at, 6, 6, 2, 2)
    taps_all = c.view(at + 144, 32, 5)
    taps = c.view(at + 304, 4, 5)
    ring = c.ring[:, :, :].rearrange("p a b -> p (a b)")
    slot = lambda n, w: ring[:, n:n + w]
    Vt = [c.view(at + 324, 6, 128), tmp[:, 2048:2816].rearrange("p (t n) -> p t n", t=6)]
    GK = stat.rearrange("p (t k n) -> p t k n", t=6, k=2)
    Kt = slot(0, 768).rearrange("p (t n) -> p t n", t=6)
    S, XF, R, D1, Q1, EM = (slot(768 + 512 * n, 512) for n in range(6))
    row = u[:, 0:4 * T].rearrange("p (r t) -> p r t", r=4)
    raw = u[:, 4 * T:8 * T].rearrange("p (r t) -> p r t", r=4)
    D0, LT, Q0, E0, E1 = (u[:, 4 * T + 512 * n:4 * T + 512 * (n + 1)] for n in range(5))
    DTs, QDs = [D0, D1], [Q0, Q1]
    E = [E0, E1]
    XX = tmp[:, 0:1024].rearrange("p (d n) -> p d n", d=2)
    VN, KD_ = (tmp[:, 1024 + 512 * n:1024 + 512 * (n + 1)] for n in range(2))
    Y = slot(768 + 512 * 6, 512)
    o_sum = row[:, 2:4, 0:LAT]
    PF = c.P[:, :, :].rearrange("p a b -> p (a b)")
    PA, PB, PY0, PY1, PZ0, PZ1, PKS, PVN = (PF[:, 512 * n:512 * (n + 1)] for n in range(8))
    PY, PZ = [PY0, PY1], [PZ0, PZ1]
    STEPS = 6
    chunk = [[4, 5, 0, 1, 2, 3], [5, 4, 3, 2, 1, 0]]
    L = LEVELS - 1
    F = lambda name, per: Flag(c, "gdn_" + name, per)
    landed = c.sem("gdn_landed")
    raws, colss, conv, tap, silu, sq, ss, sse, ssd, ssr, qk, vturn, vt, kturn, kt, gk = (
        F(n, p) for n, p in (("raw", 1), ("cols", 1), ("conv", 4), ("tap", 16), ("silu", 4), ("sq", 1), ("ss", 1), ("sse", 1), ("ssd", 1),
                             ("ssr", 1), ("qk", 1), ("vturn", 1), ("vt", 1), ("kturn", 1), ("kt", 1), ("gk", 1)))
    rows, dm, dt, dtm, lt0, lt, e0, x0, xturn, xcp = (
        F(n, STEPS) for n in ("rows", "dm", "dt", "dtm", "lt0", "lt", "e0", "x0", "xturn", "xcp"))
    half = lambda x, d: x[:, 256 * d:256 * d + 256]
    xt = lambda n: XX[:, n // 2, 128 * (n % 2):128 * (n % 2) + 128]
    xi = lambda n: XX[:, n // 2, 256 + 128 * (n % 2):256 + 128 * (n % 2) + 128]
    er, attn, qd, o, oadd = (F(n, STEPS - 2) for n in ("er", "attn", "qd", "o", "oadd"))
    et, y, ycp, z, xl = (F(n, STEPS * L * 2) for n in ("et", "y", "ycp", "z", "xl"))
    bv, kd, ks, r, vn, vncp, sn, st = (F(n, STEPS) for n in ("bv", "kd", "ks", "r", "vn", "vncp", "sn", "st"))
    out = F("out", 1)

    def nth(s, l, d):
        return (s * L + l - 1) * 2 + d + 1
    unit = [(d, v, 2 * d + v) for d in range(2) for v in range(2)]
    at_u = lambda x, n: x[:, 128 * n:128 * n + 128]
    scalar = lambda q, s, d, v: col[:, q, chunk[d][s], d, v:v + 1]
    with nc.Block() as block:
        @block.sync
        def _(sp):
            sp.dma_start(masks[:, :, :, :].rearrange("p a b c -> p (a b c)"), c.ins["level_masks"]).then_inc(landed, 16)
            sp.dma_start(tri[:, :, :].rearrange("p a b -> p (a b)"), c.ins["tri"]).then_inc(landed, 16)
            sp.dma_start(taps_all[:, :, :].rearrange("p a b -> p (a b)"), c.ins["gdn_taps"]).then_inc(landed, 16)

        @block.gpsimd
        def _(pool):
            pool.wait_ge(landed, 48)

            def body(i):
                out.wait(pool, i, 0)
                nc.gpsimd.tensor_copy(col.rearrange("p a b c d -> p (a b c d)").unsqueeze(1),
                                      cols[:, one(i), :, :, :, :].rearrange("p k a b c d -> p k (a b c d)"))
                nc.gpsimd.tensor_copy(taps[:, 0:1, :], taps_all[:, one(i), :])
                nc.gpsimd.tensor_copy(taps[:, 1:2, :], taps_all[:, one(i + 8), :])
                nc.gpsimd.tensor_copy(taps[:, 2:4, :], taps_all[:, bass.ds(i * 2 + 16, 2), :])
                colss.up(nc.gpsimd.memset(S, 0.0))
                for s in range(STEPS):
                    for l in range(1, LEVELS):
                        lt.wait(pool, i, s + 1)
                        for d in range(2):
                            y.wait(pool, i, nth(s, l, d) - 4)
                            et.up(nc.gpsimd.tensor_tensor(four(E[l % 2])[:, d], four(LT)[:, d], over_heads(masks[:, l], d), ALU.mult))
                    sn.wait(pool, i, s)
                    for d, v, n in unit:
                        ins = nc.gpsimd.tensor_tensor(at_u(KD_, n), Kt[:, chunk[d][s], :], scalar(3, s, d, v).broadcast_to([128, 128]),
                                                      ALU.mult)
                    kd.up(ins)
            body(0)
            with pool.Fori(1, HEADS) as i:
                body(i)

        @block.scalar
        def _(act):
            def body(i):
                out.wait(act, i, 0)
                for r_, blk in enumerate((i, i + 8, i * 2 + 16, i * 2 + 17)):
                    ins = nc.scalar.activation(raw[:, r_:r_ + 1, :], qkv[:, one(blk), :], ACT.Copy)
                raws.up(ins)
                for r_ in (2, 3, 0, 1):
                    conv.wait(act, i, {2: 1, 3: 2, 0: 3, 1: 4}[r_])
                    silu.up(nc.scalar.activation(row[:, r_, :], row[:, r_, :], ACT.Silu))
                silu.wait(act, i, 4)
                nc.scalar.activation(raw[:, 0, :], row[:, 0, :], ACT.Square)
                sq.up(nc.scalar.activation(raw[:, 1, :], row[:, 1, :], ACT.Square))
                vturn.wait(act, i, 1)
                for v in range(2):
                    ins = nc.scalar.activation(Vt[v].rearrange("p t n -> p (t n)"), c.P[:, v, 0:T], ACT.Copy)
                vt.up(ins)
                sse.wait(act, i, 1)
                ssd.up(nc.scalar.activation(raw[:, 2:4, :].rearrange("p a b -> p (a b)"),
                                            raw[:, 2:4, :].rearrange("p a b -> p (a b)"), ACT.Sqrt))
                kturn.wait(act, i, 1)
                kt.up(nc.scalar.activation(Kt.rearrange("p t n -> p (t n)"), PF[:, 0:T], ACT.Copy))
                for s in range(STEPS + 1):
                    if s < STEPS:
                        dm.wait(act, i, s + 1)
                        if s >= 2:
                            er.up(nc.scalar.activation(QDs[s % 2], PA, ACT.Exp))
                        dt.up(nc.scalar.activation(DTs[s % 2], DTs[s % 2], ACT.Exp))
                    if s:
                        vn.wait(act, i, s)
                        vncp.up(nc.scalar.activation(VN, PVN, ACT.Copy))
                    if s < STEPS:
                        xturn.wait(act, i, s + 1)
                        for d in range(2):
                            ins = nc.scalar.activation(XX[:, d, 256:512], half(PY[d], 0), ACT.Copy)
                        xcp.up(ins)
                        for l in range(1, LEVELS):
                            for d in range(2):
                                y.wait(act, i, nth(s, l, d))
                                z.wait(act, i, nth(s, l, d) - 2)
                                ycp.up(nc.scalar.activation(half(Y, d), half(PY[d], 0), ACT.Copy))
                        for d, v, n in unit:
                            ins = nc.scalar.activation(at_u(R, n), Vt[v][:, chunk[d][s], :], ACT.Copy, scale=scalar(0, s, d, v))
                        bv.up(ins)
            body(0)
            with act.Fori(1, HEADS) as i:
                body(i)

        @block.vector
        def _(dve):
            dve.wait_ge(landed, 48)

            def body(i):
                raws.wait(dve, i, 1)
                colss.wait(dve, i, 1)
                k = 0
                for r_ in (2, 3, 0, 1):
                    ins = nc.vector.tensor_scalar(row[:, r_, :], raw[:, r_, :], taps[:, r_, 2:3], None, ALU.mult)
                    for sh in (-2, -1, 1, 2):
                        tap.up(ins)
                        k += 1
                        tap.wait(dve, i, k)
                        for a, b in ((0, LAT), (LAT, T)):
                            lo, hi = max(a, a - sh), min(b, b - sh)
                            ins = nc.vector.scalar_tensor_tensor(out=row[:, r_, lo:hi], in0=raw[:, r_, lo + sh:hi + sh],
                                                                 scalar=taps[:, r_, sh + 2:sh + 3], in1=row[:, r_, lo:hi],
                                                                 op0=ALU.mult, op1=ALU.add)
                    conv.up(ins)
                ss.wait(dve, i, 1)
                for n in range(2):
                    ins = nc.vector.tensor_scalar(raw[:, 2 + n, :], c.P[:, 2 + n, 0:T], 1.0, 1e-6, ALU.mult, ALU.add)
                sse.up(ins)
                ssd.wait(dve, i, 1)
                ssr.up(nc.vector.reciprocal(raw[:, 0:2, :].rearrange("p a b -> p (a b)"),
                                            raw[:, 2:4, :].rearrange("p a b -> p (a b)")))
                ssr.wait(dve, i, 1)
                nc.vector.scalar_tensor_tensor(out=row[:, 0, :], in0=row[:, 0, :], scalar=128 ** -0.5, in1=raw[:, 0, :],
                                               op0=ALU.mult, op1=ALU.mult)
                qk.up(nc.vector.tensor_tensor(row[:, 1, :], row[:, 1, :], raw[:, 1, :], ALU.mult))
                kturn.wait(dve, i, 1)
                gk.up(nc.vector.tensor_copy(GK.rearrange("p t k n -> p (t k n)"), PF[:, 1024:2560]))
                for s in range(STEPS + 1):
                    DT, QD = DTs[s % 2], QDs[s % 2]
                    if s < STEPS:
                        rows.wait(dve, i, s + 1)
                        for d, v, n in unit:
                            ins = nc.vector.tensor_scalar(at_u(DT, n), at_u(PA, n), scalar(2, s, d, v), 0.0, ALU.add, ALU.min)
                        dm.up(ins)
                        for d in range(2):
                            ins = nc.vector.tensor_tensor(four(LT)[:, d], GK[:, chunk[d][s], 0:1, :].broadcast_to([128, 2, 128]),
                                                          four(PB)[:, d], ALU.mult)
                        lt0.up(ins)
                    if s:
                        ks.wait(dve, i, s)
                        bv.wait(dve, i, s)
                        for d, v, n in unit:
                            ins = nc.vector.scalar_tensor_tensor(out=at_u(R, n), in0=at_u(PKS, n), scalar=scalar(1, s - 1, d, v),
                                                                 in1=at_u(R, n), op0=ALU.mult, op1=ALU.add)
                        r.up(ins)
                    if s < STEPS:
                        dt.wait(dve, i, s + 1)
                        for d in range(2):
                            ins = nc.vector.tensor_tensor(four(DT)[:, d], four(DT)[:, d], over_heads(tri, d), ALU.mult)
                        dtm.up(ins)
                        lt0.wait(dve, i, s + 1)
                        dtm.wait(dve, i, s + 1)
                        lt.up(nc.vector.tensor_tensor(LT, LT, DT, ALU.mult))
                        lt.wait(dve, i, s + 1)
                        for d in range(2):
                            ins = nc.vector.tensor_tensor(four(EM)[:, d], four(LT)[:, d], over_heads(masks[:, 0], d), ALU.mult)
                        e0.up(ins)
                        e0.wait(dve, i, s + 1)
                        for d in range(2):
                            ins = nc.vector.tensor_tensor(XX[:, d, 0:256].rearrange("p (v t) -> p v t", v=2),
                                                          c.ident[:, :].unsqueeze(1).broadcast_to([128, 2, 128]),
                                                          four(EM)[:, d], ALU.subtract)
                        x0.up(ins)
                        if s >= 2:
                            for d in range(2):
                                ins = nc.vector.tensor_tensor(four(DT)[:, d], four(DT)[:, d],
                                                              GK[:, chunk[d][s], 1:2, :].broadcast_to([128, 2, 128]), ALU.mult)
                            attn.up(ins)
                            er.wait(dve, i, s - 1)
                            for d in range(2):
                                t0 = chunk[d][s] * 128
                                ins = nc.vector.tensor_tensor(four(QD)[:, d], four(QD)[:, d],
                                                              row[:, 0:1, t0:t0 + 128].broadcast_to([128, 2, 128]), ALU.mult)
                            qd.up(ins)
                    if s:
                        sn.wait(dve, i, s)
                        for d, v, n in unit:
                            ins = nc.vector.scalar_tensor_tensor(out=at_u(S, n), in0=at_u(S, n), scalar=scalar(4, s - 1, d, v),
                                                                 in1=at_u(PKS, n), op0=ALU.mult, op1=ALU.add)
                        st.up(ins)
                        if s >= 3:
                            for d in range(2):
                                t0 = chunk[d][s - 1] * 128
                                part = o_sum[:, :, t0:t0 + 128]
                                po = half(PZ[d], 0).rearrange("p (v t) -> p v t", v=2)
                                if s - 1 < 4:
                                    ins = nc.vector.tensor_copy(part, po)
                                else:
                                    ins = nc.vector.tensor_tensor(part, part, po, ALU.add)
                            oadd.up(ins)
                    if s < STEPS:
                        for l in range(1, LEVELS):
                            for d in range(2):
                                z.wait(dve, i, nth(s, l, d))
                                if l < L:
                                    ins = nc.vector.tensor_tensor(XX[:, d], XX[:, d], PZ[d], ALU.subtract)
                                else:
                                    ins = nc.vector.tensor_tensor(half(XF, d), XX[:, d, 0:256], half(PZ[d], 0), ALU.subtract)
                                xl.up(ins)
                oadd.wait(dve, i, STEPS - 2)
                out.up(nc.vector.tensor_scalar(qkv[:, bass.ds(i * 2 + 16, 2), 0:LAT], o_sum, 1.0, None, ALU.mult))
            body(0)
            with dve.Fori(1, HEADS) as i:
                body(i)

        @block.tensor
        def _(pe):
            pe.wait_ge(landed, 48)

            def body(i):
                silu.wait(pe, i, 2)
                oadd.wait(pe, i, 0)
                for v in range(2):
                    for t in range(6):
                        ins = nc.tensor.transpose(c.P[:, v, 128 * t:128 * t + 128], row[:, 2 + v, 128 * t:128 * t + 128], c.ident[:, :])
                vturn.up(ins)
                sq.wait(pe, i, 1)
                for n in range(2):
                    for a, b in BOTH:
                        ins = nc.tensor.matmul(c.P[:, 2 + n, a:b], c.ones[:, :], raw[:, n, a:b], start=True, stop=True)
                ss.up(ins)
                qk.wait(pe, i, 1)
                vt.wait(pe, i, 1)
                for t in range(6):
                    k_t, q_t = row[:, 1, 128 * t:128 * t + 128], row[:, 0, 128 * t:128 * t + 128]
                    nc.tensor.transpose(PF[:, 128 * t:128 * t + 128], k_t, c.ident[:, :])
                    nc.tensor.matmul(PF[:, 1024 + 256 * t:1152 + 256 * t], k_t, k_t, start=True, stop=True)
                    ins = nc.tensor.matmul(PF[:, 1152 + 256 * t:1280 + 256 * t], k_t, q_t, start=True, stop=True)
                kturn.up(ins)
                kt.wait(pe, i, 1)
                gk.wait(pe, i, 1)
                for s in range(STEPS + 1):
                    if s < STEPS:
                        lt0.wait(pe, i, s)
                        for d, v, n in unit:
                            g, b = scalar(5, s, d, v), scalar(0, s, d, v)
                            nc.tensor.matmul(at_u(PA, n), g.broadcast_to([128, 128]), tri[:, d, :], start=True, stop=True)
                            ins = nc.tensor.matmul(at_u(PB, n), b.broadcast_to([128, 128]), c.ident[:, :], start=True, stop=True)
                        rows.up(ins)
                    if s:
                        st.wait(pe, i, s - 1)
                        for d in range(2):
                            t0 = 128 * chunk[d][s - 1]
                            ins = nc.tensor.matmul(half(PKS, d), row[:, 1, t0:t0 + 128], half(S, d), start=True, stop=True)
                        ks.up(ins)
                        r.wait(pe, i, s)
                        xl.wait(pe, i, nth(s - 1, L, 1))
                        for d, v, n in unit:
                            ins = nc.tensor.matmul(at_u(PVN, n), at_u(XF, n), at_u(R, n), start=True, stop=True)
                        vn.up(ins)
                    if s < STEPS:
                        x0.wait(pe, i, s + 1)
                        for d, v, n in unit:
                            ins = nc.tensor.transpose(at_u(PY[d], v), xt(n), c.ident[:, :])
                        xturn.up(ins)
                    if s:
                        vncp.wait(pe, i, s)
                        if s >= 3:
                            qd.wait(pe, i, s - 2)
                            for d, v, n in unit:
                                nc.tensor.matmul(at_u(PZ[d], v), at_u(VN, n), at_u(DTs[(s - 1) % 2], n), start=True, stop=False)
                                ins = nc.tensor.matmul(at_u(PZ[d], v), at_u(S, n), at_u(QDs[(s - 1) % 2], n), start=False, stop=True)
                            o.up(ins)
                        kd.wait(pe, i, s)
                        for d, v, n in unit:
                            ins = nc.tensor.matmul(at_u(PKS, n), at_u(KD_, n), at_u(VN, n), start=True, stop=True)
                        sn.up(ins)
                    if s < STEPS:
                        xcp.wait(pe, i, s + 1)
                        for l in range(1, LEVELS):
                            for d in range(2):
                                et.wait(pe, i, nth(s, l, d))
                                if l > 1:
                                    xl.wait(pe, i, nth(s, l, d) - 2)
                                for v in range(2):
                                    n = 2 * d + v
                                    ins = nc.tensor.matmul(at_u(PY[d], v), at_u(E[l % 2], n), xi(n), start=True, stop=True)
                                y.up(ins)
                            if l == 1 and s >= 3:
                                oadd.wait(pe, i, s - 2)
                            for d in range(2):
                                ycp.wait(pe, i, nth(s, l, d))
                                for v in range(2):
                                    n = 2 * d + v
                                    ins = nc.tensor.matmul(at_u(PZ[d], v), at_u(Y, n), xt(n), start=True, stop=True)
                                if l < L:
                                    for v in range(2):
                                        n = 2 * d + v
                                        ins = nc.tensor.matmul(at_u(PZ[d], 2 + v), xt(n), at_u(Y, n), start=True, stop=True)
                                z.up(ins)
            body(0)
            with pe.Fori(1, HEADS) as i:
                body(i)


def head_norm(c, o, at, gain):
    nc = c.nc
    sq, rs = c.view(at, 4, LAT), c.view(at + 4 * LAT, 4, LAT)
    flat = lambda x: x.rearrange("p a b -> p (a b)")
    s = {n: c.sem("headnorm_" + n) for n in ("sq", "sum", "var", "sd", "rs", "out")}
    psum = c.P[:, 0:2, :].rearrange("p a b -> p (a b)")
    with nc.Block() as block:
        @block.sync
        def _(sp):
            c.prefetch(sp, "gdn_ba")

        @block.scalar
        def _(act):
            for q in range(4):
                if q:
                    act.wait_ge(s["sum"], q)
                nc.scalar.activation(sq, o[:, 4 * q:4 * q + 4, 0:LAT], ACT.Square).then_inc(s["sq"], 1)
                act.wait_ge(s["var"], q + 1)
                nc.scalar.activation(flat(rs), flat(rs), ACT.Sqrt).then_inc(s["sd"], 1)

        @block.tensor
        def _(pe):
            for q in range(4):
                pe.wait_ge(s["sq"], q + 1)
                if q:
                    pe.wait_ge(s["var"], q)
                for n in range(4):
                    last = nc.tensor.matmul(psum[:, 512 * n:512 * n + 512], c.ones[:, :], sq[:, n, :], start=True, stop=True)
                last.then_inc(s["sum"], 1)

        @block.vector
        def _(dve):
            for q in range(4):
                dve.wait_ge(s["sum"], q + 1)
                if q:
                    dve.wait_ge(s["out"], q)
                nc.vector.tensor_scalar(flat(rs), psum, 1.0 / 128, 1e-6, ALU.mult, ALU.add).then_inc(s["var"], 1)
                dve.wait_ge(s["sd"], q + 1)
                nc.vector.reciprocal(flat(rs), flat(rs)).then_inc(s["rs"], 1)
                dve.wait_ge(s["rs"], q + 1)
                x = o[:, 4 * q:4 * q + 4, 0:LAT]
                nc.vector.scalar_tensor_tensor(out=x, in0=x, scalar=gain, in1=rs, op0=ALU.mult, op1=ALU.mult
                                               ).then_inc(s["out"], 1)


MAGIC = 1.5 * 2.0 ** 23
TURN = 6.283185307179586


def s5_params(c, par, at):
    nc = c.nc
    N = 128
    raw = c.view(at, 3, N)
    w = [c.view(at + 3 * N + N * n, N) for n in range(12)]
    out = lambda q: par[:, :, q, :]
    sq2 = lambda x: x.rearrange("p (b e) -> p b e", e=8)
    landed, dv, ac = (c.sem("s5par_" + n) for n in ("landed", "dve", "act"))
    re, im, ls = raw[:, 0, :], raw[:, 1, :], raw[:, 2, :]
    with nc.Block() as block:
        @block.sync
        def _(sp):
            sp.dma_start(raw.rearrange("p a b -> p (a b)"), c.ins["s5_lam"]).then_inc(landed, 16)

        @block.scalar
        def _(act):
            act.wait_ge(landed, 16)
            nc.scalar.activation(w[0], ls, ACT.Exp).then_inc(ac, 1)
            act.wait_ge(dv, 1)
            nc.scalar.activation(w[2], w[1], ACT.Exp).then_inc(ac, 1)
            act.wait_ge(dv, 9)
            nc.scalar.activation(w[5], w[4], ACT.Sin, scale=TURN).then_inc(ac, 1)
            nc.scalar.activation(w[7], w[6], ACT.Sin, scale=TURN).then_inc(ac, 1)

        @block.vector
        def _(dve):
            n = [0]

            def step(ins):
                ins.then_inc(dv, 1)
                n[0] += 1
                dve.wait_ge(dv, n[0])
            V = nc.vector
            dve.wait_ge(ac, 1)
            step(V.tensor_tensor(w[1], re, w[0], ALU.mult))
            step(V.tensor_tensor(w[3], im, w[0], ALU.mult))
            step(V.tensor_scalar(w[3], w[3], 1.0 / TURN, None, ALU.mult))
            step(V.tensor_scalar(w[4], w[3], MAGIC, -MAGIC, ALU.add, ALU.add))
            step(V.tensor_tensor(w[4], w[3], w[4], ALU.subtract))
            step(V.tensor_scalar(w[6], w[4], 0.25, None, ALU.add))
            step(V.tensor_scalar(w[8], w[6], MAGIC, -MAGIC, ALU.add, ALU.add))
            step(V.tensor_tensor(w[6], w[6], w[8], ALU.subtract))
            step(V.tensor_scalar(w[8], w[4], 3.0 * 2.0 ** 10, -3.0 * 2.0 ** 10, ALU.add, ALU.add))
            V.tensor_copy(out(1), sq2(w[8]))
            step(V.tensor_tensor(out(2), sq2(w[4]), sq2(w[8]), ALU.subtract))
            dve.wait_ge(ac, 4)
            V.tensor_copy(out(0), sq2(w[2]))
            step(V.tensor_tensor(w[9], w[2], w[7], ALU.mult))
            V.tensor_scalar(w[9], w[9], -1.0, None, ALU.add)
            step(V.tensor_tensor(w[10], w[2], w[5], ALU.mult))
            V.tensor_tensor(w[0], re, re, ALU.mult)
            step(V.tensor_tensor(w[1], im, im, ALU.mult))
            step(V.tensor_tensor(w[0], w[0], w[1], ALU.add))
            step(V.reciprocal(w[11], w[0]))
            V.tensor_tensor(w[0], w[9], re, ALU.mult)
            V.tensor_tensor(w[1], w[10], im, ALU.mult)
            V.tensor_tensor(w[2], w[10], re, ALU.mult)
            step(V.tensor_tensor(w[3], w[9], im, ALU.mult))
            V.tensor_tensor(w[0], w[0], w[1], ALU.add)
            step(V.tensor_tensor(w[2], w[2], w[3], ALU.subtract))
            V.tensor_tensor(out(3), sq2(w[0]), sq2(w[11]), ALU.mult)
            V.tensor_tensor(out(4), sq2(w[2]), sq2(w[11]), ALU.mult)


def s5_scan(c, p, par, at, skip):
    nc = c.nc
    U, CH, N = 8, 128, T // 128
    take = lambda *shape: (c.view(place[0], *shape), place.__setitem__(0, place[0] + int(np.prod(shape))))[0]
    place = [at]
    steps, Bm, Cm = take(CH), take(2, 2, 128), take(2, 4, 2, 32)
    xs, col, s_end, small = take(T), take(5, 8), take(8), take(4)
    fs, fc, Tr, Ti = take(U, CH), take(U, CH), take(U, CH), take(U, CH)
    t4 = [take(4, T), take(4, T)]
    tmp = c.tmp[:, :, :, :].rearrange("p a b c -> p (a b c)")
    p12, p34 = tmp[:, 0:1024].rearrange("p (a t) -> p a t", a=2), tmp[:, 1024:2048].rearrange("p (a t) -> p a t", a=2)
    hh = tmp[:, 2048:3072].rearrange("p (a t) -> p a t", a=2)
    gr, gi = c.stat[:, 0, :], c.stat[:, 1, :]
    A, W = (t4[0][:, :, :].rearrange("p a t -> p (a t)")[:, 1024 * n:1024 * n + 1024].rearrange("p (u t) -> p u t", u=U)
            for n in range(2))
    landed, mats = c.sem("s5_landed"), c.sem("s5_mats")
    F = lambda name, per: Flag(c, "s5_" + name, per)
    staged, out, phase, trig, tables = F("staged", 1), F("out", 1), F("phase", 1), F("trig", 1), F("tables", 1)
    bu, p4, add1, g, p2, add2, y = (F(n, U) for n in ("bu", "p4", "add1", "g", "p2", "add2", "y"))
    chain, pool_chain = F("chain", 0), F("pool_chain", U)
    PR, PI, PY = c.P[:, 0, 0:T], c.P[:, 1, 0:T], c.P[:, 2, 0:LAT]
    unit = [(d, q, 4 * d + q) for d in range(2) for q in range(4)]
    chunks = lambda x: x.rearrange("p (c t) -> p c t", t=CH)
    table = lambda x, n, reps: x[:, n:n + 1, :].broadcast_to([128, reps, CH])

    def order(d):
        if d == 0:
            return [(0, slice(LAT, T)), (256, slice(0, 256)), (512, slice(256, 512))]
        return [(0, slice(T - 1, LAT - 1, -1)), (256, slice(LAT - 1, 255, -1)), (512, slice(255, None, -1))]
    with nc.Block() as block:
        @block.sync
        def _(sp):
            sp.dma_start(steps, c.ins["s5_steps"]).then_inc(landed, 16)

            def body(i):
                out.wait(sp, i, 0)
                sp.dma_start(Bm.rearrange("p a b c -> p (a b c)"), rows_of(c.ins["s5_b"], i)).then_inc(mats, 16)
                sp.dma_start(Cm.rearrange("p a b c d -> p (a b c d)"), rows_of(c.ins["s5_c"], i)).then_inc(mats, 16)
            body(0)
            with sp.Fori(1, 16) as i:
                body(i)

        @block.gpsimd
        def _(pool):
            tt = nc.gpsimd.tensor_tensor

            def body(i):
                out.wait(pool, i, 0)
                nc.gpsimd.tensor_copy(col.rearrange("p a b -> p (a b)").unsqueeze(1),
                                      par[:, one(i), :, :].rearrange("p k a b -> p k (a b)"))
                staged.up(nc.gpsimd.tensor_copy(xs.unsqueeze(1), p[:, one(i), :]))

                def inputs(n):
                    x = t4[n % 2]
                    p4.wait(pool, i, n + 1)
                    tt(x[:, 0, :], x[:, 0, :], x[:, 1, :], ALU.subtract)
                    add1.up(tt(x[:, 2, :], x[:, 2, :], x[:, 3, :], ALU.add))

                def states(n):
                    g.wait(pool, i, n + 1)
                    tt(chunks(p34[:, 0, :]), chunks(gr[:, CTX:T]), table(fs, n, 4), ALU.mult)
                    pool_chain.up(tt(chunks(p34[:, 1, :]), chunks(gi[:, CTX:T]), table(fc, n, 4), ALU.mult))
                    p2.wait(pool, i, n + 1)
                    y.wait(pool, i, n)
                    tt(hh[:, 0, :], p12[:, 0, :], p12[:, 1, :], ALU.add)
                    pool_chain.wait(pool, i, n + 1)
                    add2.up(tt(hh[:, 1, :], p34[:, 0, :], p34[:, 1, :], ALU.subtract))
                inputs(0)
                for n in range(U):
                    if n + 1 < U:
                        inputs(n + 1)
                    states(n)
            body(0)
            with pool.Fori(1, 16) as i:
                body(i)

        @block.scalar
        def _(act):
            def body(i):
                phase.wait(act, i, 1)
                nc.scalar.activation(fs, fs, ACT.Sin, scale=-TURN)
                trig.up(nc.scalar.activation(fc, fc, ACT.Sin, scale=TURN))
            body(0)
            with act.Fori(1, 16) as i:
                body(i)

        @block.vector
        def _(dve):
            dve.wait_ge(landed, 16)
            V = nc.vector
            ts, tt, stt = V.tensor_scalar, V.tensor_tensor, V.scalar_tensor_tensor

            def body(i):
                staged.wait(dve, i, 1)
                n_ = [0]

                def step(ins):
                    chain.up(ins)
                    n_[0] += 1
                    chain.wait(dve, i, n_[0])
                by_t = lambda q: col[:, q, :].unsqueeze(2).broadcast_to([128, U, CH])
                by_u = steps.unsqueeze(1).broadcast_to([128, U, CH])
                step(tt(A, by_u, by_t(1), ALU.mult))
                step(ts(W, A, MAGIC, -MAGIC, ALU.add, ALU.add))
                step(tt(A, A, W, ALU.subtract))
                step(tt(W, by_u, by_t(2), ALU.mult))
                step(tt(A, A, W, ALU.add))
                step(ts(W, A, MAGIC, -MAGIC, ALU.add, ALU.add))
                step(tt(fs, A, W, ALU.subtract))
                step(ts(W, fs, 0.25, None, ALU.is_gt))
                phase.up(stt(out=fc, in0=fs, scalar=0.25, in1=W, op0=ALU.add, op1=ALU.subtract))
                trig.wait(dve, i, 1)
                tt(Ti, fc, by_t(4), ALU.mult)
                tt(Tr, fc, by_t(3), ALU.mult)
                tt(W, fs, by_t(3), ALU.mult)
                ts(s_end.unsqueeze(2), fs[:, :, CH - 1:CH], -1.0, None, ALU.mult)
                step(tt(A, fs, by_t(4), ALU.mult))
                tt(Ti, Ti, W, ALU.add)
                step(tt(Tr, Tr, A, ALU.subtract))

                def inputs(n):
                    x = t4[n % 2]
                    bu.wait(dve, i, n + 1)
                    for k, (ps, tab) in enumerate(((PR, Tr), (PI, Ti), (PI, Tr), (PR, Ti))):
                        ins = tt(chunks(x[:, k, :]), chunks(ps), table(tab, n, N), ALU.mult)
                    p4.up(ins)

                def scan(n):
                    x = t4[n % 2]
                    add1.wait(dve, i, n + 1)
                    add2.wait(dve, i, n)
                    rb = col[:, 0, n:n + 1].broadcast_to([128, CH])
                    c_end = fc[:, n, CH - 1:CH]
                    for k in range(N):
                        a, b = CH * k, CH * k + CH
                        V.tensor_tensor_scan(gr[:, a:b], rb, x[:, 0, a:b], small[:, 2:3] if k else 0.0, ALU.mult, ALU.add)
                        ins = V.tensor_tensor_scan(gi[:, a:b], rb, x[:, 2, a:b], small[:, 3:4] if k else 0.0, ALU.mult, ALU.add)
                        if k == N - 1:
                            g.up(ins)
                            continue
                        step(ins)
                        ts(small[:, 0:1], gr[:, b - 1:b], c_end, None, ALU.mult)
                        step(ts(small[:, 1:2], gi[:, b - 1:b], c_end, None, ALU.mult))
                        stt(out=small[:, 2:3], in0=gi[:, b - 1:b], scalar=fs[:, n, CH - 1:CH], in1=small[:, 0:1], op0=ALU.mult, op1=ALU.add)
                        step(stt(out=small[:, 3:4], in0=gr[:, b - 1:b], scalar=s_end[:, n:n + 1], in1=small[:, 1:2], op0=ALU.mult, op1=ALU.add))
                    g.wait(dve, i, n + 1)
                    tt(chunks(p12[:, 0, :]), chunks(gr[:, CTX:T]), table(fc, n, 4), ALU.mult)
                    p2.up(tt(chunks(p12[:, 1, :]), chunks(gi[:, CTX:T]), table(fs, n, 4), ALU.mult))
                inputs(0)
                for n in range(U):
                    if n + 1 < U:
                        inputs(n + 1)
                    scan(n)
                y.wait(dve, i, U)
                out.up(stt(out=p[:, one(i), 0:LAT], in0=xs[:, 0:LAT].unsqueeze(1), scalar=skip(i),
                           in1=PY.unsqueeze(1), op0=ALU.mult, op1=ALU.add))
                return n_[0]
            chain.per = body(0)
            with dve.Fori(1, 16) as i:
                body(i)

        @block.tensor
        def _(pe):
            def body(i):
                staged.wait(pe, i, 1)
                pe.wait_ge(mats, i * 32 + 32)

                def inputs(n):
                    d, q, _ = unit[n]
                    p4.wait(pe, i, n)
                    for k, ps in enumerate((PR, PI)):
                        for a, cols in order(d):
                            ins = nc.tensor.matmul(ps[:, a:a + 256], Bm[32 * q:32 * q + 32, d, k, :],
                                                   xs[32 * q:32 * q + 32, cols], start=True, stop=True)
                    bu.up(ins)

                def outputs(n):
                    d, q, _ = unit[n]
                    add2.wait(pe, i, n + 1)
                    for k in range(2):
                        cols = slice(0, LAT) if d == 0 else slice(LAT - 1, None, -1)
                        ins = nc.tensor.matmul(PY[32 * q:32 * q + 32, :], Cm[:, d, q, k, :], hh[:, k, :][:, cols],
                                               start=d == 0 and k == 0, stop=d == 1 and k == 1, skip_group_check=True)
                    y.up(ins)
                inputs(0)
                inputs(1)
                for n in range(U):
                    if n + 2 < U:
                        inputs(n + 2)
                    outputs(n)
            body(0)
            with pe.Fori(1, 16) as i:
                body(i)


def gelu(c, p):
    nc = c.nc
    with nc.Block() as block:
        @block.scalar
        def _(act):
            for g in range(4):
                nc.scalar.activation(p[:, 4 * g:4 * g + 4, 0:LAT], p[:, 4 * g:4 * g + 4, 0:LAT], ACT.Gelu_apprx_tanh)


VECS = [("b_mod0", 48), ("b_mod1", 48), ("ada_b_20", 24), ("ada_b_21", 24),
        ("c", 8), ("c_ctx", 8), ("c_2", 8), ("c_ctx_2", 8),
        ("ln1_g0", 8), ("ln1_b0", 8), ("ln2_g0", 8), ("ln2_b0", 8), ("ln1_g1", 8), ("ln1_b1", 8), ("ln2_g1", 8), ("ln2_b1", 8),
        ("ln_g_20", 8), ("ln_b_20", 8), ("ln_g_21", 8), ("ln_b_21", 8),
        ("mla_q_norm", 4), ("mla_kv_norm", 2), ("gdn_norm", 1), ("s5_d", 16), ("s5_glu_b", 16), ("sink", 16)]
VEC_AT = {}
_at = 0
for _n, _w in VECS:
    VEC_AT[_n] = _at
    _at += _w
VEC_WIDTH = _at


def program(nc, ins, out):
    c = Core(nc, ins)
    P = c.P
    act_fn, vec_fn = nc.scalar.activation, nc.vector
    h, u, area = c.h, c.u, c.view
    vcol = lambda name: (lambda k: c.vec[:, VEC_AT[name] + k:VEC_AT[name] + k + 1])

    landed, silu_c = c.sem("landed"), c.sem("silu_c")
    cond = area(0, KD, 4)
    with nc.Block() as block:
        @block.sync
        def _(sp):
            sp.dma_start(c.vec[:, :], ins["vecs"]).then_inc(landed, 16)
            c.load_slot(sp, "mod", 0, 0)
            c.load_slot(sp, "mod", 1, 1)
            sp.dma_start(h[:, :, 0:LAT], ins["x"].rearrange("p (k t) -> p k t", k=KD)).then_inc(landed, 16)
            sp.dma_start(h[:, :, LAT:T], ins["ctx"].rearrange("p (k t) -> p k t", k=KD)).then_inc(landed, 16)
            sp.dma_start(c.ones[:, :], ins["ones"]).then_inc(landed, 16)
            sp.dma_start(c.ident[:, :], ins["ident"]).then_inc(landed, 16)

        @block.scalar
        def _(act):
            act.wait_ge(landed, 80)
            v = c.vec[:, VEC_AT["c"]:VEC_AT["c"] + 32].rearrange("p (c k) -> p k c", c=4)
            act_fn(cond, v, ACT.Silu).then_inc(silu_c, 1)

    def keep_mod(g, j, ps, tmp):
        return act_fn(c.mod[:, one(g * 2 + j), :], ps[:, 0:4].unsqueeze(1), ACT.Copy)
    dense(c, "mod", cond, ((0, 4),), keep_mod)
    bias_in = c.sem("bias_in")
    with nc.Block() as block:
        @block.vector
        def _(dve):
            vec_fn.tensor_tensor(c.mod[:, :, :], c.mod[:, :, :], c.vec[:, 0:144].unsqueeze(2).broadcast_to([128, 144, 4]), ALU.add
                                 ).then_inc(bias_in, 1)
            dve.wait_ge(bias_in, 1)
            for a in (8, 32, 56, 80, 104, 128):
                vec_fn.tensor_scalar(c.mod[:, a:a + 8, :], c.mod[:, a:a + 8, :], 1.0, None, ALU.add)

    def modcol(base, cond_):
        return lambda k: c.mod[:, base + k, cond_:cond_ + 1]

    def modulated(base, conds=(0, 1)):
        segs = [(0, LAT), (LAT, T)][:len(conds)]
        return [(modcol(base + 8, cc), modcol(base, cc), a, b) for cc, (a, b) in zip(conds, segs)]

    def modulate(parts, loads=None):
        got = c.sem("ctx_landed")
        with nc.Block() as block:
            if loads is not None:
                @block.sync
                def _(sp):
                    sp.dma_start(h[:, :, LAT:T], loads.rearrange("p (k t) -> p k t", k=KD)).then_inc(got, 16)

            @block.scalar
            def _(act):
                if loads is not None:
                    act.wait_ge(got, 16)
                for k in range(KD):
                    for scale, add, a, b in parts:
                        act_fn(u[:, k, a:b], h[:, k, a:b], ACT.Identity, scale=scale(k), bias=add(k))

    def residual(name, x, gate, conds, segs):
        per = c.shape_of(name)[1]

        def act(g, j, ps, tmp):
            for cc, (a, b) in zip(conds, ((0, LAT), (LAT, T))):
                last = act_fn(tmp[:, a:b], ps[:, a:b], ACT.Copy, scale=c.mod[:, bass.ds(g * per + (j + gate), 1), cc:cc + 1].rearrange("p a b -> p (a b)"))
            return last

        def vec(g, j, ps, tmp):
            w = T if len(conds) > 1 else LAT
            hk = h[:, one(g * per + j), 0:w]
            return vec_fn.scalar_tensor_tensor(out=hk, in0=hk, scalar=ALPHA, in1=tmp[:, 0:w].unsqueeze(1), op0=ALU.mult, op1=ALU.add)
        dense(c, name, x, segs, act, vec)

    def feed_forward(layer, conds, segs, hidden):
        w = T if len(conds) > 1 else LAT

        def act(g, j, ps, tmp):
            return act_fn(tmp[:, 0:w], ps[:, 0:w], ACT.Silu if j == 0 else ACT.Copy)

        def vec(g, j, ps, tmp):
            if j == 0:
                return None
            other = c.tmp[:, g_slot[0], 0, 0:w]
            return vec_fn.tensor_tensor(hidden[:, one(g), 0:w], other.unsqueeze(1), tmp[:, 0:w].unsqueeze(1), ALU.mult)
        g_slot = [0]

        def act_s(g, j, ps, tmp):
            return act(g, j, ps, tmp)

        def vec_s(g, j, ps, tmp):
            if j == 0:
                pairs_first[0] = tmp
                return None
            return vec_fn.tensor_tensor(hidden[:, one(g), 0:w], pairs_first[0][:, 0:w].unsqueeze(1), tmp[:, 0:w].unsqueeze(1), ALU.mult)
        pairs_first = [None]
        dense(c, f"ffn_in{layer}", u, segs, act_s, vec_s)
        residual(f"ffn_out{layer}", hidden, layer * 48 + 40, conds, segs)

    def copy_to(dst, off=0, per=2, w=T):
        return lambda g, j, ps, tmp: act_fn(dst[:, one(g * per + (j + off)), 0:w], ps[:, 0:w].unsqueeze(1), ACT.Copy)

    def silu_times(dst, w):
        act = lambda g, j, ps, tmp: act_fn(tmp[:, 0:w], ps[:, 0:w], ACT.Silu)

        def vec(g, j, ps, tmp):
            d = dst[:, one(g * 2 + j), 0:w]
            return vec_fn.tensor_tensor(d, d, tmp[:, 0:w].unsqueeze(1), ALU.mult)
        return act, vec

    modulate(modulated(0))
    rope_x, q_nope = area(0, 5, T), area(5 * T, 8, T)
    lat = area(13 * T, 7, T)
    k_nope = area(20 * T, 8, T)
    v_tok = area(28 * T, 6, D)
    dense(c, "mla_in", u, BOTH, copy_to(lat, per=1))
    moved = c.sem("k_rope_moved")
    with nc.Block() as block:
        @block.vector
        def _(dve):
            vec_fn.tensor_copy(rope_x[:, 4, :], lat[:, 6, :]).then_inc(moved, 1)
    normalise(c, "q_rms", lat, 4, T, BOTH, 1e-6, vcol("mla_q_norm"))
    normalise(c, "kv_rms", lat[:, 4:6, :], 2, T, BOTH, 1e-6, vcol("mla_kv_norm"))
    qx = area(0, 13, T)

    def q_act(g, j, ps, tmp):
        return act_fn(q_nope[:, one(g * 2 + j), :], ps[:, 0:T].unsqueeze(1), ACT.Copy)
    q_all = area(0, 13, T)
    k_hold = lat[:, 6, :]
    dense(c, "q_up", lat, BOTH, lambda g, j, ps, tmp: act_fn(q_all[:, one(g * 2 + (j + 1)), :], ps[:, 0:T].unsqueeze(1), ACT.Copy))
    with nc.Block() as block:
        order = c.sem("rope_order")
        @block.scalar
        def _(act):
            act_fn(q_all[:, 0, :], k_hold, ACT.Copy)
    dense(c, "k_up", lat[:, 4:6, :], BOTH, copy_to(k_nope))
    dense_tokens(c, "v_up", lat[:, 4:6, :], 256, v_tok)
    turn(c, "mla_rope", q_all, 5, area(13 * T, 3, 512), ("mla_trig", "mla_perm"))
    attention(c, "mla", 4, 2, False,
              q=lambda i, j: q_all[:, one(i * 2 + (5 + j)), :],
              k=lambda i, j, a, b: k_nope[:, one(i * 2 + j), a:b].rearrange("p a b -> p (a b)"),
              v=lambda i, j: v_tok[:, :, bass.ds(i * 256 + j * 128, 128)],
              out=lambda i, j, t: q_all[:, one(i * 2 + (5 + j)), 128 * t:128 * t + 128],
              at=13 * T, scale=MLA_SCALE,
              rope=(lambda i: q_all[:, one(i + 1), :],
                    lambda j, a, b: q_all[64 * j:64 * j + 64, 0, a:b]))
    residual("mla_out", q_all[:, 5:13, :], 16, (0, 1), BOTH)
    normalise(c, "ln1_0", h, 8, T, BOTH, 1e-5, vcol("ln1_g0"), vcol("ln1_b0"), after=(u, modulated(24)))
    hidden = area(0, KF, T)
    feed_forward(0, (0, 1), BOTH, hidden)
    normalise(c, "ln2_0", h, 8, T, BOTH, 1e-5, vcol("ln2_g0"), vcol("ln2_b0"), after=(u, modulated(48)))

    c.clear_sems()
    qkv = area(0, 32, T)
    at = 32 * T
    cols = area(at, 8, 6, 6, 2, 2) if False else None
    cols_flat = area(at, 1152)
    cols = cols_flat.rearrange("p (k q t d v) -> p k q t d v", k=8, q=6, t=6, d=2)
    at += 1152
    ba = area(at, 6, 64)
    dense(c, "gdn_qkv", u, BOTH, copy_to(qkv))
    dense_tokens(c, "gdn_ba", u, 64, ba, ahead=False)
    gdn_gates(c, ba, cols, at + 384)
    c.clear_sems()
    gdn_heads(c, qkv, cols, at)
    c.clear_sems()
    o_gdn = qkv[:, 16:32, :]
    head_norm(c, o_gdn, 0, c.vec[:, VEC_AT["gdn_norm"]:VEC_AT["gdn_norm"] + 1])
    modulate(modulated(48, (0,)))
    dense(c, "gdn_z", u, LATS, *silu_times(o_gdn, LAT))
    residual("gdn_out", o_gdn, 48 + 16, (0,), LATS)
    normalise(c, "ln1_1", h, 8, LAT, LATS, 1e-5, vcol("ln1_g1"), vcol("ln1_b1"), after=(u, modulated(48 + 24, (0,))))
    feed_forward(1, (0,), LATS, hidden)
    normalise(c, "ln2_1", h, 8, LAT, LATS, 1e-5, vcol("ln2_g1"), vcol("ln2_b1"))

    c.clear_sems()
    modulate(modulated(96, (2, 3)), loads=ins["ctx_2"])
    qk = area(0, 20, T)
    v2 = area(20 * T, 6, 512)
    dense(c, "att_qk", u, BOTH, copy_to(qk))
    dense_tokens(c, "att_v", u, 256, v2)
    turn(c, "att_rope", qk, 20, area(24 * T, 3, 512), ("att_trig", "att_perm"))
    attention(c, "att", 4, 4, True,
              q=lambda i, j: qk[:, one(i * 4 + j), :],
              k=lambda i, j, a, b: qk[:, one(i + 16), a:b].rearrange("p a b -> p (a b)"),
              v=lambda i, j: v2[:, :, bass.ds(i * 128, 128)],
              out=lambda i, j, t: qk[:, one(i * 4 + j), 128 * t:128 * t + 128],
              at=24 * T, scale=ATT_SCALE,
              sink=lambda i, j: c.vec[:, bass.ds(i * 4 + (VEC_AT["sink"] + j), 1)])
    dense(c, "att_z", u, BOTH, *silu_times(qk, T))
    residual("att_out", qk, 96 + 16, (2, 3), BOTH)
    normalise(c, "ln_2_0", h, 8, T, BOTH, 1e-5, vcol("ln_g_20"), vcol("ln_b_20"), after=(u, modulated(120, (2, 3))))

    c.clear_sems()
    p = area(0, 16, T)
    dense(c, "s5_in", u, BOTH, copy_to(p))
    par = area(16 * T, 16, 5, 8)
    s5_params(c, par, 16 * T + 640)
    s5_scan(c, p, par, 16 * T + 640, lambda i: c.vec[:, bass.ds(i + VEC_AT["s5_d"], 1)])
    gelu(c, p)
    y5 = area(16 * T, 16, LAT)

    def glu_act(g, j, ps, tmp):
        return act_fn(tmp[:, 0:LAT], ps[:, 0:LAT], ACT.Sigmoid, bias=c.vec[:, bass.ds(g + VEC_AT["s5_glu_b"], 1)])

    def glu_vec(g, j, ps, tmp):
        return vec_fn.tensor_tensor(y5[:, one(g), :], p[:, one(g), 0:LAT], tmp[:, 0:LAT].unsqueeze(1), ALU.mult)
    dense(c, "s5_glu", p, LATS, glu_act, glu_vec)
    dense(c, "s5_z", u, LATS, *silu_times(y5, LAT))
    residual("s5_out", y5, 120 + 16, (2,), LATS)
    normalise(c, "ln_2_1", h, 8, LAT, LATS, 1e-5, vcol("ln_g_21"), vcol("ln_b_21"))
    stored = c.sem("stored")
    with nc.Block() as block:
        @block.sync
        def _(sp):
            sp.dma_start(out.rearrange("p (k t) -> p k t", k=KD), h[:, :, 0:LAT]).then_inc(stored, 16)
            sp.wait_ge(stored, 16)


def blocks(w, per, width=128):
    k, n = w.shape
    b = w.reshape(k // 128, 128, n // (per * width), per, width)
    return np.ascontiguousarray(b.transpose(2, 1, 3, 0, 4)).reshape(n // (per * width), 128, -1)


def columns(v):
    return v.reshape(-1, 128).T


def feature_major(x):
    t, n = x.shape
    return np.ascontiguousarray(x.T.reshape(n // 128, 128, t).transpose(1, 0, 2)).reshape(128, -1)


def rope_tables():
    row, col = np.arange(LAT) // GRID_W, np.arange(LAT) % GRID_W
    out = {}
    for name, width, half in (("mla", 64, 16), ("att", 128, 32)):
        ch = np.arange(128) % width
        inv = (10000.0 ** (-(ch % half).astype(np.float64) / half)).astype(np.float32)
        pos = np.where((ch // (2 * half) % 2)[:, None] == 0, row[None, :], col[None, :]).astype(np.float32)
        ang = (pos * inv[:, None]).astype(np.float32)
        sign = np.where((ch // half) % 2 == 0, -1.0, 1.0)[:, None]
        out[name + "_trig"] = np.concatenate([np.cos(ang), np.sin(ang) * sign], 1).astype(np.float32)
        out[name + "_perm"] = np.eye(128, dtype=np.float32)[np.arange(128) ^ half]
    return out


def constants():
    i = np.arange(128)
    out = {"ones": np.ones((128, 128)), "ident": np.eye(128)}
    fwd = (i[:, None] <= i[None, :]).astype(np.float32)
    out["tri"] = np.concatenate([fwd, fwd.T], 1)
    levels = []
    for l in range(LEVELS):
        s = 1 << l
        m = (i[:, None] // (2 * s) == i[None, :] // (2 * s)) & (i[None, :] // s % 2 == 1) & (i[:, None] // s % 2 == 0)
        levels += [m, m.T]
    out["level_masks"] = np.concatenate(levels, 1)
    a, b = i[:, None], i[None, :]
    out["window_mask"] = np.concatenate([np.where(b >= a, 0, -1e30), np.zeros((128, 128)), np.where(b <= a, 0, -1e30)], 1)
    out["s5_steps"] = np.broadcast_to(np.arange(1, 129), (128, 128))
    out = {k: np.ascontiguousarray(v, dtype=np.float32) for k, v in out.items()}
    out.update(rope_tables())
    return out


def layouts(x):
    a = constants()
    a["x"], a["ctx"], a["ctx_2"] = feature_major(x["x"][0]), feature_major(x["ctx"][0]), feature_major(x["ctx_2"][0])
    a["w_mod"] = np.concatenate([blocks(w, 2) for w in (*x["w_mod"], *x["ada_w_2"])])
    w = x["mla_w_in"][0]
    a["w_mla_in"] = blocks(np.concatenate([w, w[:, 768:832]], 1), 1)
    q = x["mla_w_q_up"][0].reshape(512, HEADS, 192)
    a["w_q_up"] = blocks(np.concatenate([q[:, :, 128:].reshape(512, 512), q[:, :, :128].reshape(512, 1024)], 1), 2)
    kv = x["mla_w_kv_up"][0].reshape(256, HEADS, 256)
    a["w_k_up"] = blocks(np.ascontiguousarray(kv[:, :, :128]).reshape(256, 1024), 2)
    a["w_v_up"] = blocks(np.ascontiguousarray(kv[:, :, 128:]).reshape(256, 1024), 1, 256)
    a["w_mla_out"] = blocks(x["mla_w_out"][0], 2)
    for l in range(2):
        f = x["w_ffn_in"][l].reshape(D, 2, KF, 128).transpose(0, 2, 1, 3).reshape(D, 2 * FF)
        a[f"w_ffn_in{l}"] = blocks(f, 2)
        a[f"w_ffn_out{l}"] = blocks(x["w_ffn_out"][l], 1)
    w = x["gdn_w_in"][0]
    a["w_gdn_qkv"], a["w_gdn_z"], a["w_gdn_ba"] = blocks(w[:, :4096], 2), blocks(w[:, 4096:6144], 2), blocks(w[:, 6144:], 1, 64)
    a["w_gdn_out"] = blocks(x["gdn_w_out"][0], 1)
    a["gdn_taps"] = np.ascontiguousarray(x["gdn_conv"][0].T.reshape(32, 128, 5).transpose(1, 0, 2)).reshape(128, 160)
    rows = np.concatenate([x["gdn_a_log"][0].reshape(32), x["gdn_dt_bias"][0].reshape(32)])
    a["gdn_rows"] = np.ascontiguousarray(np.broadcast_to(rows, (128, 64)))
    w = x["attn_w_in_2"][0]
    a["w_att_qk"], a["w_att_v"], a["w_att_z"] = blocks(w[:, :2560], 2), blocks(w[:, 2560:3072], 1, 256), blocks(w[:, 3072:], 2)
    a["w_att_out"], a["w_s5_out"] = blocks(x["w_out_2"][0], 1), blocks(x["w_out_2"][1], 1)
    w = x["s5_w_in_2"][0]
    a["w_s5_in"], a["w_s5_z"] = blocks(w[:, :2048], 2), blocks(w[:, 2048:], 2)
    a["w_s5_glu"] = blocks(x["s5_glu_w_2"][0], 1)
    st = lambda v: v.reshape(2, 16, 4, 128).transpose(3, 1, 0, 2).reshape(128, 128)
    step = np.repeat(x["s5_log_step_2"][0][:, :, None], 64, 2)
    a["s5_lam"] = np.concatenate([st(x["s5_lam_re_2"][0]), st(x["s5_lam_im_2"][0]), st(step)], 1)
    b = np.stack([x["s5_b_re_2"][0], x["s5_b_im_2"][0]]).reshape(2, 2, 16, 4, 2, 64, 16)
    bm = np.zeros((16, 4, 2, 16, 2, 2, 2, 64), np.float32)
    cm = np.zeros((16, 2, 64, 2, 4, 2, 2, 16), np.float32)
    cc = np.stack([x["s5_c_re_2"][0], x["s5_c_im_2"][0]]).reshape(2, 2, 16, 4, 2, 16, 64)
    for g in range(2):
        bm[:, :, g, :, :, :, g, :] = b[:, :, :, :, g].transpose(2, 3, 5, 1, 0, 4)
        cm[:, g, :, :, :, :, g, :] = cc[:, :, :, :, g].transpose(2, 5, 1, 3, 0, 4)
    a["s5_b"], a["s5_c"] = bm.reshape(16, 128, 512), cm.reshape(16, 128, 512)
    vec = {"sink": np.broadcast_to(x["attn_sink_2"][0], (128, 16)), "c": columns(x["c"][0]), "c_ctx": columns(x["c_ctx"]),
           "c_2": columns(x["c_2"][0]), "c_ctx_2": columns(x["c_ctx_2"]), "mla_q_norm": columns(x["mla_q_norm"][0]),
           "mla_kv_norm": columns(x["mla_kv_norm"][0]), "gdn_norm": columns(x["gdn_norm"][0]), "s5_d": columns(x["s5_d_2"][0]),
           "s5_glu_b": columns(x["s5_glu_b_2"][0])}
    for l in range(2):
        for n in ("b_mod", "ln1_g", "ln1_b", "ln2_g", "ln2_b", "ada_b_2", "ln_g_2", "ln_b_2"):
            vec[f"{n}{l}"] = columns(x[n][l])
    a["vecs"] = np.concatenate([vec[n] for n, _ in VECS], 1)
    return {k: np.ascontiguousarray(v) for k, v in a.items()}


def kernel(**inputs):
    import concourse.bacc as bacc
    from concourse.bass_utils import run_bass_kernel_spmd
    names = [n for n, v in inputs.items() if v.size]
    arrays = layouts({n: np.asarray(inputs[n]) for n in names})
    nc = bacc.Bacc("TRN2", target_bir_lowering=False, num_devices=1)
    ins = {n: nc.dram_tensor("in_" + n, v.shape, F32, kind="ExternalInput").ap() for n, v in arrays.items()}
    out = nc.dram_tensor("out", (128, KD * LAT), F32, kind="ExternalOutput").ap()
    program(nc, ins, out)
    r = run_bass_kernel_spmd(nc, [{"in_" + n: v for n, v in arrays.items()}], core_ids=[0])
    y = r.results[0]["out"].reshape(128, KD, LAT)
    return np.ascontiguousarray(y.transpose(2, 1, 0)).reshape(1, LAT, D)
```

```python
import numpy as np
import concourse.bass as bass
from concourse import mybir

F32 = mybir.dt.float32
ACT = mybir.ActivationFunctionType
ALU = mybir.AluOpType
AX = mybir.AxisListType

D = 1024
LAT, CTX = 512, 256
T = LAT + CTX
KD = D // 128
GRID_W = 64
ALPHA = 4.0 ** 0.25
FF = 2816
KF = FF // 128
SLOT = KF * 128
HEADS = 8
MLA_SCALE = 192 ** -0.5
ATT_SCALE = 128 ** -0.5
BOTH = ((0, 512), (512, 768))
LATS = ((0, 512),)
LEVELS = 7


def pairs(eng, groups, body):
    for g in range(min(2, groups)):
        body(g, g, True)
    if groups > 3:
        with eng.Fori(1, groups // 2) as p:
            for s in range(2):
                body(p * 2 + s, s, False)
    if groups > 2 and groups % 2:
        body(groups - 1, 0, False)


def one(g):
    return bass.ds(g, 1)


def rows_of(dram, g):
    return dram[one(g), :, :].rearrange("o p n -> (o p) n")


PRODUCTS = [
    ("mla_in", 8, 1), ("q_up", 4, 2), ("k_up", 2, 2), ("v_up", 2, 2), ("mla_out", 8, 2),
    ("ffn_in0", 8, 2), ("ffn_out0", KF, 1),
    ("gdn_qkv", 8, 2), ("gdn_ba", 8, 1), ("gdn_z", 8, 2), ("gdn_out", 16, 1), ("ffn_in1", 8, 2), ("ffn_out1", KF, 1),
    ("att_qk", 8, 2), ("att_v", 8, 2), ("att_z", 8, 2), ("att_out", 16, 1),
    ("s5_in", 8, 2), ("s5_glu", 16, 1), ("s5_z", 8, 2), ("s5_out", 16, 1),
]


class Core:

    def __init__(self, nc, ins):
        self.nc, self.ins = nc, ins
        self.sems, self.live = 0, []
        f = lambda name, *shape: nc.alloc_sbuf_tensor(name, [128, *shape], F32)
        self.h = f("h", KD, T)
        self.u = f("u", KD, T)
        self.ring = f("ring", 2, SLOT)
        self.tmp = f("tmp", 2, 2, T)
        self.mod = f("mod", 144, 4)
        self.vec = f("vec", ins["vecs"].shape[1])
        self.ones = f("ones", 128)
        self.ident = f("ident", 128)
        self.stat = f("stat", 2, T)
        self.area_size = (nc.sbuf_bytes_remaining // 4) - 64
        self.area = f("area", self.area_size)
        self.P = nc.alloc_psum_tensor("P", [128, 4, 1024], F32)
        self.ring_ready = [self.sem(f"ring_ready{s}") for s in range(2)]
        self.mm_done = self.sem("mm_done")
        self.live = []
        self.first = {}
        n = 0
        for name, _, _ in PRODUCTS:
            self.first[name] = n
            n += ins["w_" + name].shape[0]
        self.total = n

    def sem(self, name):
        self.sems += 1
        got = self.nc.alloc_semaphore(f"{name}_{self.sems}")
        self.live.append(got)
        return got

    def clear_sems(self):
        self.nc.clear_and_free_semaphores(self.live)
        self.nc.all_engine_barrier()
        self.live = []

    def view(self, at, *shape):
        n = int(np.prod(shape))
        assert at + n <= self.area_size, (at, shape, self.area_size)
        v = self.area[:, at:at + n]
        names = "abcd"[:len(shape)]
        if len(shape) > 1:
            v = v.rearrange(f"p ({' '.join(names)}) -> p {' '.join(names)}", **dict(zip(names[1:], shape[1:])))
        return v

    def load_slot(self, sp, name, g, slot):
        w = self.ins["w_" + name]
        n = w.shape[2]
        sp.dma_start(self.ring[:, slot, 0:n], rows_of(w, g)).then_inc(self.ring_ready[slot], 16)

    def prefetch(self, sp, name):
        order = [p[0] for p in PRODUCTS]
        i = order.index(name) + 1
        if i == len(order):
            return
        at = self.first[order[i]]
        for g in range(min(2, self.ins["w_" + order[i]].shape[0])):
            sp.wait_ge(self.mm_done, at + g - 1)
            self.load_slot(sp, order[i], g, (at + g) % 2)

    def shape_of(self, name):
        return next((kt, per) for n, kt, per in PRODUCTS if n == name)


def stream(c, sp, name, ahead=True):
    at, groups = c.first[name], c.ins["w_" + name].shape[0]

    def body(g, s, first):
        if not first:
            sp.wait_ge(c.mm_done, g + (at - 1))
            c.load_slot(sp, name, g, (at + s) % 2)
    pairs(sp, groups, body)
    if ahead:
        c.prefetch(sp, name)


def dense(c, name, x, segs, act, vec=None, act_frees=True):
    nc = c.nc
    kt, per = c.shape_of(name)
    at, groups = c.first[name], c.ins["w_" + name].shape[0]
    act_done, vec_done = c.sem(name + "_act_done"), c.sem(name + "_vec_done")
    freed = act_done if act_frees else vec_done
    with nc.Block() as block:
        @block.sync
        def _(sp):
            stream(c, sp, name)

        @block.tensor
        def _(pe):
            def body(g, s, first):
                slot = (at + s) % 2
                pe.wait_ge(c.ring_ready[slot], (g - s) * 8 + 16 * ((at + s) // 2 + 1))
                if not first:
                    pe.wait_ge(freed, g - 1)
                for j in range(per):
                    for a, b in segs:
                        for k in range(kt):
                            last = nc.tensor.matmul(
                                c.P[:, 2 * s + j, a:b], c.ring[:, slot, (j * kt + k) * 128:(j * kt + k + 1) * 128],
                                x[:, k, a:b], start=k == 0, stop=k == kt - 1)
                last.then_inc(c.mm_done, 1)
            pairs(pe, groups, body)

        @block.scalar
        def _(eng):
            def body(g, s, first):
                eng.wait_ge(c.mm_done, g + (at + 1))
                if vec and not first:
                    eng.wait_ge(vec_done, g - 1)
                for j in range(per):
                    last = act(g, j, c.P[:, 2 * s + j, :], c.tmp[:, s, j, :])
                last.then_inc(act_done, 1)
            pairs(eng, groups, body)

        if vec:
            @block.vector
            def _(eng):
                def body(g, s, first):
                    eng.wait_ge(act_done, g + 1)
                    for j in range(per):
                        last = vec(g, j, c.P[:, 2 * s + j, :], c.tmp[:, s, j, :])
                    last.then_inc(vec_done, 1)
                pairs(eng, groups, body)


def dense_tokens(c, name, x, width, out, ahead=True):
    nc = c.nc
    kt, _ = c.shape_of(name)
    at, groups = c.first[name], c.ins["w_" + name].shape[0]
    copied = c.sem(name + "_copied")
    psum = c.P[:, :, :].rearrange("p a b -> p (a b)")
    with nc.Block() as block:
        @block.sync
        def _(sp):
            stream(c, sp, name, ahead)

        @block.tensor
        def _(pe):
            def body(g, s, first):
                slot = (at + s) % 2
                pe.wait_ge(c.ring_ready[slot], (g - s) * 8 + 16 * ((at + s) // 2 + 1))
                if not first:
                    pe.wait_ge(copied, g - 1)
                for t in range(T // 128):
                    for k in range(kt):
                        last = nc.tensor.matmul(
                            psum[:, 2048 * s + t * width:2048 * s + (t + 1) * width], x[:, k, t * 128:(t + 1) * 128],
                            c.ring[:, slot, k * width:(k + 1) * width], start=k == 0, stop=k == kt - 1)
                last.then_inc(c.mm_done, 1)
            pairs(pe, groups, body)

        @block.scalar
        def _(eng):
            def body(g, s, first):
                eng.wait_ge(c.mm_done, g + (at + 1))
                nc.scalar.activation(out[:, :, bass.ds(g * width, width)],
                                     psum[:, 2048 * s:2048 * s + T // 128 * width].rearrange("p (t n) -> p t n", n=width),
                                     ACT.Copy).then_inc(copied, 1)
            pairs(eng, groups, body)


def spread(ap, n, axis=1):
    return ap.unsqueeze(axis).broadcast_to([ap.shape[0], n, ap.shape[1]]) if axis == 1 else None


def normalise(c, name, src, kt, width, segs, eps, gain, shift=None, after=None):
    nc = c.nc
    inv = 1.0 / (kt * 128)
    s = {n: c.sem(f"{name}_{n}") for n in ("mean", "centred", "sq", "sq_used", "var", "sd", "rs", "unit", "affine")}
    ps_mean, ps_var = c.P[:, 0, 0:width], c.P[:, 1, 0:width]
    sq = [c.tmp[:, 0, 0, 0:width], c.tmp[:, 1, 0, 0:width]]
    sd, rs = c.stat[:, 0, 0:width], c.stat[:, 1, 0:width]
    x = src[:, 0:kt, 0:width]
    with nc.Block() as block:
        @block.tensor
        def _(pe):
            if shift is not None:
                for a, b in segs:
                    for k in range(kt):
                        last = nc.tensor.matmul(ps_mean[:, a:b], c.ones[:, :], src[:, k, a:b], start=k == 0, stop=k == kt - 1)
                last.then_inc(s["mean"], 1)
            for k in range(kt):
                pe.wait_ge(s["sq"], k + 1)
                for a, b in segs:
                    last = nc.tensor.matmul(ps_var[:, a:b], c.ones[:, :], sq[k % 2][:, a:b], start=k == 0, stop=k == kt - 1)
                last.then_inc(s["sq_used"], 1)

        @block.scalar
        def _(act):
            for k in range(kt):
                if shift is not None:
                    act.wait_ge(s["centred"], k + 1)
                if k >= 2:
                    act.wait_ge(s["sq_used"], k - 1)
                nc.scalar.activation(sq[k % 2], src[:, k, 0:width], ACT.Square).then_inc(s["sq"], 1)
            act.wait_ge(s["var"], 1)
            nc.scalar.activation(sd, sd, ACT.Sqrt).then_inc(s["sd"], 1)
            if after:
                out, parts = after
                for k in range(kt):
                    act.wait_ge(s["affine"], k + 1)
                    for scale, add, a, b in parts:
                        nc.scalar.activation(out[:, k, a:b], src[:, k, a:b], ACT.Identity, scale=scale(k), bias=add(k))

        @block.vector
        def _(dve):
            if shift is not None:
                dve.wait_ge(s["mean"], 1)
                for k in range(kt):
                    nc.vector.scalar_tensor_tensor(out=src[:, k, 0:width], in0=ps_mean, scalar=-inv, in1=src[:, k, 0:width],
                                                   op0=ALU.mult, op1=ALU.add).then_inc(s["centred"], 1)
            dve.wait_ge(s["sq_used"], kt)
            nc.vector.tensor_scalar(sd, ps_var, inv, eps, ALU.mult, ALU.add).then_inc(s["var"], 1)
            dve.wait_ge(s["sd"], 1)
            nc.vector.reciprocal(rs, sd).then_inc(s["rs"], 1)
            dve.wait_ge(s["rs"], 1)
            nc.vector.tensor_tensor(x, x, spread(rs, kt), ALU.mult).then_inc(s["unit"], 1)
            dve.wait_ge(s["unit"], 1)
            for k in range(kt):
                if shift is not None:
                    nc.vector.tensor_scalar(src[:, k, 0:width], src[:, k, 0:width], gain(k), shift(k),
                                            ALU.mult, ALU.add).then_inc(s["affine"], 1)
                else:
                    nc.vector.tensor_scalar(src[:, k, 0:width], src[:, k, 0:width], gain(k), None,
                                            ALU.mult).then_inc(s["affine"], 1)


def turn(c, name, x, blocks, tables, perm):
    nc = c.nc
    landed, partner, turned, kept, done = (c.sem(f"{name}_{n}") for n in ("landed", "partner", "turned", "kept", "done"))
    cos, sin, perm_sb = tables[:, 0, :], tables[:, 1, :], tables[:, 2, 0:128]
    with nc.Block() as block:
        @block.sync
        def _(sp):
            sp.dma_start(tables[:, 0:2, :].rearrange("p a b -> p (a b)"), c.ins[perm[0]]).then_inc(landed, 16)
            sp.dma_start(perm_sb, c.ins[perm[1]]).then_inc(landed, 16)

        @block.tensor
        def _(pe):
            pe.wait_ge(landed, 32)
            for n in range(blocks):
                if n >= 4:
                    pe.wait_ge(turned, n - 3)
                nc.tensor.matmul(c.P[:, n % 4, 0:LAT], perm_sb, x[:, n, 0:LAT], start=True, stop=True).then_inc(partner, 1)

        @block.vector
        def _(dve):
            dve.wait_ge(landed, 32)
            for n in range(blocks):
                dve.wait_ge(partner, n + 1)
                if n >= 2:
                    dve.wait_ge(done, n - 1)
                nc.vector.tensor_tensor(c.tmp[:, n % 2, 0, 0:LAT], c.P[:, n % 4, 0:LAT], sin, ALU.mult).then_inc(turned, 1)
                nc.vector.tensor_tensor(x[:, n, 0:LAT], x[:, n, 0:LAT], cos, ALU.mult).then_inc(kept, 1)
                dve.wait_ge(turned, n + 1)
                dve.wait_ge(kept, n + 1)
                nc.vector.tensor_tensor(x[:, n, 0:LAT], x[:, n, 0:LAT], c.tmp[:, n % 2, 0, 0:LAT], ALU.add).then_inc(done, 1)


def attention(c, name, rounds, per, window, q, k, v, out, at, scale, rope=None, sink=None):
    nc = c.nc
    qs, vs = c.view(at, per, T), c.view(at + per * T, per, T // 128, 128)
    at += 2 * per * T
    if rope:
        rs = c.view(at, T)
        at += T
    prob = [c.tmp[:, 0, 0, :], c.tmp[:, 0, 1, :], c.view(at, T)]
    probT = c.tmp[:, 1, :, :]
    small = c.stat[:, 0, 0:24].rearrange("p (a b) -> p a b", a=3)
    mask = None
    if window:
        mask = c.view(at + T, 3 * 128)
    units = []
    for j in range(per):
        for t in range(T // 128):
            if t >= LAT // 128:
                tiles = [4, 5]
            elif window:
                tiles = list(range(max(0, t - 1), min(4, t + 2))) + [4, 5]
            else:
                tiles = list(range(6))
            units.append((j, t, tiles))
    U = len(units)
    S = [c.P[:, 0, :], c.P[:, 1, :]]
    TP = c.P[:, 2, :]
    O = [c.P[:, 3, 0:128], c.P[:, 3, 512:640]]
    sem = {n: c.sem(f"{name}_{n}") for n in
           ("const", "staged", "head", "score", "masked", "top", "peak", "negpeak", "prob", "sinkexp", "total", "inv",
            "unit", "turned", "probT", "o", "ocopied")}
    with nc.Block() as block:
        if window:
            @block.sync
            def _(sp):
                sp.dma_start(mask, c.ins["window_mask"]).then_inc(sem["const"], 16)

        @block.gpsimd
        def _(pool):
            def body(i, s, first):
                for j in range(per):
                    if not first:
                        pool.wait_ge(sem["o"], (i - 1) * U + (j + 1) * (U // per))
                    elif i:
                        pool.wait_ge(sem["o"], (i - 1) * U + (j + 1) * (U // per))
                    if rope and j == 0:
                        if not (first and i == 0):
                            pool.wait_ge(sem["o"], i * U)
                        nc.gpsimd.tensor_copy(rs[:, :].unsqueeze(1), rope[0](i))
                    nc.gpsimd.tensor_copy(qs[:, j, :].unsqueeze(1), q(i, j))
                    nc.gpsimd.tensor_copy(vs[:, j, :, :], v(i, j)).then_inc(sem["staged"], 1)
            body(0, 0, True)
            with pool.Fori(1, rounds) as i:
                body(i, 0, False)

        @block.tensor
        def _(pe):
            def body(i, first):
                def score(n):
                    j, t, tiles = units[n]
                    w = 128 * (len(tiles) - 2)
                    if t == 0:
                        pe.wait_ge(sem["staged"], i * per + (j + 1))
                    if not (first and n < 2):
                        pe.wait_ge(sem["masked" if window else "prob"], i * U + (n - 1))
                    segs = ([(512 - w, 512, tiles[0] * 128)] if w else []) + [(512, 768, 512)]
                    for a, b, key in segs:
                        last = nc.tensor.matmul(S[n % 2][:, a:b], qs[:, j, t * 128:t * 128 + 128],
                                                k(i, j, key, key + b - a), start=True, stop=rope is None)
                        if rope:
                            last = nc.tensor.matmul(S[n % 2][:, a:b], rs[64 * j:64 * j + 64, t * 128:t * 128 + 128],
                                                    rope[1](j, key, key + b - a), start=False, stop=True)
                    last.then_inc(sem["score"], 1)

                def flip(n):
                    pe.wait_ge(sem["unit"], i * U + (n + 1))
                    if not (first and n == 0):
                        pe.wait_ge(sem["probT"], i * U + n)
                    nb = len(units[n][2])
                    for b in range(nb):
                        a = 768 - 128 * nb + 128 * b
                        last = nc.tensor.transpose(TP[:, b * 128:b * 128 + 128], prob[n % 3][:, a:a + 128], c.ident[:, :])
                    last.then_inc(sem["turned"], 1)

                def value(n):
                    j, t, tiles = units[n]
                    pe.wait_ge(sem["probT"], i * U + (n + 1))
                    if not (first and n < 2):
                        pe.wait_ge(sem["ocopied"], i * U + (n - 1))
                    for b, key in enumerate(tiles):
                        last = nc.tensor.matmul(O[n % 2], vs[:, j, key, :], probT[:, n % 2, b * 128:b * 128 + 128],
                                                start=b == 0, stop=b == len(tiles) - 1)
                    last.then_inc(sem["o"], 1)
                for n in range(U + 3):
                    if n < U:
                        score(n)
                    if 2 <= n < U + 2:
                        flip(n - 2)
                    if n >= 3:
                        value(n - 3)
            body(0, True)
            with pe.Fori(1, rounds) as i:
                body(i, False)

        @block.scalar
        def _(act):
            def body(i, first):
                def exps(n):
                    a = 768 - 128 * len(units[n][2])
                    act.wait_ge(sem["negpeak"], i * U + (n + 1))
                    if not (first and n < 3):
                        act.wait_ge(sem["turned"], i * U + (n - 2))
                    nc.scalar.activation(prob[n % 3][:, a:768], prob[n % 3][:, a:768] if window else S[n % 2][:, a:768],
                                         ACT.Exp, bias=small[:, n % 3, 1:2], scale=scale,
                                         accum_out=small[:, n % 3, 2:3]).then_inc(sem["prob"], 1)
                    if sink:
                        nc.scalar.activation(small[:, n % 3, 3:4], sink(i, units[n][0]), ACT.Exp,
                                             bias=small[:, n % 3, 1:2]).then_inc(sem["sinkexp"], 1)

                def copy(n):
                    nb = len(units[n][2])
                    act.wait_ge(sem["turned"], i * U + (n + 1))
                    if not (first and n < 2):
                        act.wait_ge(sem["o"], i * U + (n - 1))
                    nc.scalar.activation(probT[:, n % 2, 0:nb * 128], TP[:, 0:nb * 128], ACT.Copy).then_inc(sem["probT"], 1)
                for n in range(U + 2):
                    if n < U:
                        exps(n)
                    if n >= 2:
                        copy(n - 2)
            body(0, True)
            with act.Fori(1, rounds) as i:
                body(i, False)

        @block.vector
        def _(dve):
            if window:
                dve.wait_ge(sem["const"], 16)

            def body(i, first):
                def peak(n):
                    j, t, tiles = units[n]
                    a = 768 - 128 * len(tiles)
                    dve.wait_ge(sem["score"], i * U + (n + 1))
                    seen = S[n % 2]
                    if window:
                        if not (first and n < 3):
                            dve.wait_ge(sem["turned"], i * U + (n - 2))
                        if t < 4:
                            m0 = 128 * (tiles[0] - t + 1)
                            nc.vector.tensor_tensor(prob[n % 3][:, a:512], seen[:, a:512], mask[:, m0:m0 + 512 - a], ALU.add)
                        nc.vector.tensor_copy(prob[n % 3][:, 512:768], seen[:, 512:768]).then_inc(sem["masked"], 1)
                        dve.wait_ge(sem["masked"], i * U + (n + 1))
                        seen = prob[n % 3]
                    nc.vector.reduce_max(small[:, n % 3, 0:1], seen[:, a:768], AX.X).then_inc(sem["top"], 1)
                    dve.wait_ge(sem["top"], i * U + (n + 1))
                    if sink:
                        nc.vector.tensor_scalar(small[:, n % 3, 4:5], small[:, n % 3, 0:1], scale, None, ALU.mult
                                                ).then_inc(sem["peak"], 1)
                        dve.wait_ge(sem["peak"], i * U + (n + 1))
                        nc.vector.tensor_scalar(small[:, n % 3, 1:2], small[:, n % 3, 4:5], sink(i, j), -1.0, ALU.max, ALU.mult
                                                ).then_inc(sem["negpeak"], 1)
                    else:
                        nc.vector.tensor_scalar(small[:, n % 3, 1:2], small[:, n % 3, 0:1], -scale, None, ALU.mult
                                                ).then_inc(sem["negpeak"], 1)

                def finish(n):
                    a = 768 - 128 * len(units[n][2])
                    dve.wait_ge(sem["prob"], i * U + (n + 1))
                    total = small[:, n % 3, 2:3]
                    if sink:
                        dve.wait_ge(sem["sinkexp"], i * U + (n + 1))
                        total = small[:, n % 3, 5:6]
                        nc.vector.tensor_tensor(total, small[:, n % 3, 2:3], small[:, n % 3, 3:4], ALU.add).then_inc(sem["total"], 1)
                        dve.wait_ge(sem["total"], i * U + (n + 1))
                    nc.vector.reciprocal(small[:, n % 3, 6:7], total).then_inc(sem["inv"], 1)
                    dve.wait_ge(sem["inv"], i * U + (n + 1))
                    nc.vector.tensor_scalar(prob[n % 3][:, a:768], prob[n % 3][:, a:768], small[:, n % 3, 6:7], None, ALU.mult
                                            ).then_inc(sem["unit"], 1)

                def keep(n):
                    j, t, _ = units[n]
                    dve.wait_ge(sem["o"], i * U + (n + 1))
                    nc.vector.tensor_copy(out(i, j, t), O[n % 2].unsqueeze(1)).then_inc(sem["ocopied"], 1)
                for n in range(U + 3):
                    if n < U:
                        peak(n)
                    if 1 <= n <= U:
                        finish(n - 1)
                    if n >= 3:
                        keep(n - 3)
            body(0, True)
            with dve.Fori(1, rounds) as i:
                body(i, False)


class Flag:

    def __init__(self, c, name, per):
        self.sem, self.per = c.sem(name), per

    def up(self, instruction):
        instruction.then_inc(self.sem, 1)

    def wait(self, eng, i, n):
        if isinstance(i, int) and i * self.per + n <= 0:
            return
        eng.wait_ge(self.sem, i * self.per + n)


def four(ap):
    return ap.rearrange("p (d v t) -> p d v t", d=2, v=2)


def over_heads(ap, d):
    return ap[:, d:d + 1, :].broadcast_to([128, 2, 128])


def gdn_gates(c, ba, cols, at):
    nc = c.nc
    N = 6 * 32
    tri = c.view(at, 2, 128)
    rows = c.view(at + 256, 2, 32)
    w = [c.view(at + 320 + N * n, 6, 32) for n in range(6)]
    names = "bcgv"
    b_in = ba.rearrange("p t (d k h) -> p t d k h", d=2, k=2)[:, :, :, 0, :]
    a_in = ba.rearrange("p t (d k h) -> p t d k h", d=2, k=2)[:, :, :, 1, :]
    tdh = lambda x: x.rearrange("p t (d h) -> p t d h", d=2)
    flat = lambda x: x.rearrange("p t h -> p (t h)")
    quantity = lambda q, d: cols[:, :, q, :, d, :].rearrange("p k t v -> p t k v")
    s = {n: c.sem("gates_" + n) for n in ("landed", "a", "act", "dve", "pe")}
    cum, tot = c.P[:, 0, 0:2 * 96], c.P[:, 1, 0:2 * 96]
    with nc.Block() as block:
        @block.sync
        def _(sp):
            sp.dma_start(tri[:, :, :].rearrange("p a b -> p (a b)"), c.ins["tri"]).then_inc(s["landed"], 16)
            sp.dma_start(rows[:, :, :].rearrange("p a b -> p (a b)"), c.ins["gdn_rows"]).then_inc(s["landed"], 16)

        @block.scalar
        def _(act):
            act.wait_ge(s["landed"], 32)
            nc.scalar.activation(rows[:, 0, :], rows[:, 0, :], ACT.Exp).then_inc(s["act"], 1)
            act.wait_ge(s["dve"], 3)
            nc.scalar.activation(flat(w[1]), flat(w[1]), ACT.Exp).then_inc(s["act"], 1)
            nc.scalar.activation(flat(w[5]), flat(w[5]), ACT.Exp).then_inc(s["act"], 1)
            act.wait_ge(s["dve"], 4)
            nc.scalar.activation(flat(w[1]), flat(w[1]), ACT.Ln).then_inc(s["act"], 1)
            act.wait_ge(s["dve"], 9)
            nc.scalar.activation(flat(w[1]), flat(w[2]), ACT.Exp).then_inc(s["act"], 1)
            nc.scalar.activation(flat(w[0]), flat(w[0]), ACT.Exp).then_inc(s["act"], 1)
            nc.scalar.activation(flat(w[3]), flat(w[3]), ACT.Exp).then_inc(s["act"], 1)

        @block.vector
        def _(dve):
            n = [0]

            def step(ins):
                ins.then_inc(s["dve"], 1)
                n[0] += 1
                dve.wait_ge(s["dve"], n[0])
            dve.wait_ge(s["landed"], 32)
            for d in range(2):
                last = nc.vector.tensor_tensor(tdh(w[0])[:, :, d, :], a_in[:, :, d, :],
                                               rows[:, 1, 16 * d:16 * d + 16].unsqueeze(1).broadcast_to([128, 6, 16]), ALU.add)
            step(last)
            nc.vector.tensor_scalar(flat(w[1]), flat(w[0]), -1.0, None, ALU.mult).then_inc(s["dve"], 1)
            n[0] += 1
            dve.wait_ge(s["dve"], n[0])
            for d in range(2):
                nc.vector.tensor_scalar(tdh(w[5])[:, :, d, :], b_in[:, :, d, :], -1.0, None, ALU.mult)
            step(nc.vector.tensor_tensor(flat(w[1]), flat(w[1]), flat(w[0]), ALU.min))
            dve.wait_ge(s["act"], 2)
            step(nc.vector.tensor_scalar(flat(w[1]), flat(w[1]), 1.0, None, ALU.add))
            dve.wait_ge(s["act"], 4)
            step(nc.vector.scalar_tensor_tensor(out=flat(w[0]), in0=flat(w[0]), scalar=0.0, in1=flat(w[1]), op0=ALU.max, op1=ALU.add))
            step(nc.vector.scalar_tensor_tensor(out=w[0], in0=w[0], scalar=-1.0,
                                                in1=rows[:, 0, :].unsqueeze(1).broadcast_to([128, 6, 32]), op0=ALU.mult, op1=ALU.mult))
            for d in range(2):
                for t in range(6):
                    last = nc.vector.tensor_copy(cols[:, :, 5, t, d, :], w[0][:, t, 16 * d:16 * d + 16].rearrange("p (k v) -> p k v", v=2))
            step(last)
            nc.vector.tensor_scalar(flat(w[5]), flat(w[5]), 1.0, None, ALU.add).then_inc(s["dve"], 1)
            n[0] += 1
            dve.wait_ge(s["pe"], 1)
            dve.wait_ge(s["dve"], n[0])
            nc.vector.reciprocal(flat(w[4]), flat(w[5]))
            for d in range(2):
                nc.vector.tensor_copy(tdh(w[2])[:, :, d, :], cum[:, 96 * d:96 * d + 96].rearrange("p (t h) -> p t h", h=16))
                last = nc.vector.tensor_copy(tdh(w[0])[:, :, d, :], tot[:, 96 * d:96 * d + 96].rearrange("p (t h) -> p t h", h=16))
            last.then_inc(s["a"], 1)
            dve.wait_ge(s["a"], 1)
            step(nc.vector.tensor_tensor(flat(w[3]), flat(w[0]), flat(w[2]), ALU.subtract))
            dve.wait_ge(s["act"], 7)
            nc.vector.scalar_tensor_tensor(out=flat(w[1]), in0=flat(w[1]), scalar=-1.0, in1=flat(w[4]), op0=ALU.mult, op1=ALU.mult)
            step(nc.vector.tensor_scalar(flat(w[5]), flat(w[2]), -1.0, None, ALU.mult))
            for q, x in ((0, w[4]), (1, w[1]), (2, w[5]), (3, w[3]), (4, w[0])):
                for d in range(2):
                    for t in range(6):
                        nc.vector.tensor_copy(cols[:, :, q, t, d, :], x[:, t, 16 * d:16 * d + 16].rearrange("p (k v) -> p k v", v=2))

        @block.tensor
        def _(pe):
            pe.wait_ge(s["dve"], 7)
            for d in range(2):
                g = tdh(w[0])[:, :, d, :]
                nc.tensor.matmul(cum[:, 96 * d:96 * d + 96], tri[:, d, :], g, start=True, stop=True)
                last = nc.tensor.matmul(tot[:, 96 * d:96 * d + 96], c.ones[:, :], g, start=True, stop=True)
            last.then_inc(s["pe"], 1)


def gdn_heads(c, qkv, cols, at):
    nc = c.nc
    u = c.u[:, :, :].rearrange("p a b -> p (a b)")
    tmp = c.tmp[:, :, :, :].rearrange("p a b c -> p (a b c)")
    stat = c.stat[:, :, :].rearrange("p a b -> p (a b)")
    masks = c.view(at, LEVELS, 2, 128)
    tri = c.view(at + LEVELS * 256, 2, 128)
    at += (LEVELS + 1) * 256
    col = c.view(at, 6, 6, 2, 2)
    norm, inv_norm = c.view(at + 144, 12), c.view(at + 160, 12)
    ring = c.ring[:, :, :].rearrange("p a b -> p (a b)")
    slot = lambda n, w: ring[:, n:n + w]
    Vt = [c.view(at + 324, 6, 128), tmp[:, 2048:2816].rearrange("p (t n) -> p t n", t=6)]
    GK = stat.rearrange("p (t k n) -> p t k n", t=6, k=2)
    Kt = slot(0, 768).rearrange("p (t n) -> p t n", t=6)
    S, XF, R, D1, Q1, EM = (slot(768 + 512 * n, 512) for n in range(6))
    row = u[:, 0:4 * T].rearrange("p (r t) -> p r t", r=4)
    raw = u[:, 4 * T:8 * T].rearrange("p (r t) -> p r t", r=4)
    D0, LT, Q0, E0, E1 = (u[:, 4 * T + 512 * n:4 * T + 512 * (n + 1)] for n in range(5))
    DTs, QDs = [D0, D1], [Q0, Q1]
    E = [E0, E1]
    XX = tmp[:, 0:1024].rearrange("p (d n) -> p d n", d=2)
    VN, KD_ = (tmp[:, 1024 + 512 * n:1024 + 512 * (n + 1)] for n in range(2))
    Y = slot(768 + 512 * 6, 512)
    o_sum = row[:, 2:4, 0:LAT]
    PF = c.P[:, :, :].rearrange("p a b -> p (a b)")
    PA, PB, PY0, PY1, PZ0, PZ1, PKS, PVN = (PF[:, 512 * n:512 * (n + 1)] for n in range(8))
    PY, PZ = [PY0, PY1], [PZ0, PZ1]
    STEPS = 6
    chunk = [[4, 5, 0, 1, 2, 3], [5, 4, 3, 2, 1, 0]]
    L = LEVELS - 1
    F = lambda name, per: Flag(c, "gdn_" + name, per)
    landed = c.sem("gdn_landed")
    colss, silu, sq, ss, sse, ssd, ssr, qk, vturn, vt, kturn, kt, gk = (
        F(n, p) for n, p in (("cols", 1), ("silu", 4), ("sq", 1), ("ss", 1), ("sse", 1), ("ssd", 1),
                             ("ssr", 1), ("qk", 1), ("vturn", 1), ("vt", 1), ("kturn", 1), ("kt", 1), ("gk", 1)))
    rows, dm, dt, dtm, lt0, lt, e0, x0, xturn, xcp = (
        F(n, STEPS) for n in ("rows", "dm", "dt", "dtm", "lt0", "lt", "e0", "x0", "xturn", "xcp"))
    half = lambda x, d: x[:, 256 * d:256 * d + 256]
    xt = lambda n: XX[:, n // 2, 128 * (n % 2):128 * (n % 2) + 128]
    xi = lambda n: XX[:, n // 2, 256 + 128 * (n % 2):256 + 128 * (n % 2) + 128]
    er, attn, qd, o, oadd = (F(n, STEPS - 2) for n in ("er", "attn", "qd", "o", "oadd"))
    et, y, ycp, z, xl = (F(n, STEPS * L * 2) for n in ("et", "y", "ycp", "z", "xl"))
    bv, kd, ks, r, vn, vncp, sn, st = (F(n, STEPS) for n in ("bv", "kd", "ks", "r", "vn", "vncp", "sn", "st"))
    out, norm_rows = F("out", 1), F("norm_rows", 1)

    def nth(s, l, d):
        return (s * L + l - 1) * 2 + d + 1
    unit = [(d, v, 2 * d + v) for d in range(2) for v in range(2)]
    at_u = lambda x, n: x[:, 128 * n:128 * n + 128]
    scalar = lambda q, s, d, v: col[:, q, chunk[d][s], d, v:v + 1]
    with nc.Block() as block:
        @block.sync
        def _(sp):
            sp.dma_start(masks[:, :, :, :].rearrange("p a b c -> p (a b c)"), c.ins["level_masks"]).then_inc(landed, 16)
            sp.dma_start(tri[:, :, :].rearrange("p a b -> p (a b)"), c.ins["tri"]).then_inc(landed, 16)

        @block.gpsimd
        def _(pool):
            pool.wait_ge(landed, 32)

            def body(i):
                out.wait(pool, i, 0)
                nc.gpsimd.tensor_copy(col.rearrange("p a b c d -> p (a b c d)").unsqueeze(1),
                                      cols[:, one(i), :, :, :, :].rearrange("p k a b c d -> p k (a b c d)"))
                colss.up(nc.gpsimd.memset(S, 0.0))
                for s in range(STEPS):
                    for l in range(1, LEVELS):
                        lt.wait(pool, i, s + 1)
                        for d in range(2):
                            y.wait(pool, i, nth(s, l, d) - 4)
                            et.up(nc.gpsimd.tensor_tensor(four(E[l % 2])[:, d], four(LT)[:, d], over_heads(masks[:, l], d), ALU.mult))
                    sn.wait(pool, i, s)
                    for d, v, n in unit:
                        ins = nc.gpsimd.tensor_tensor(at_u(KD_, n), Kt[:, chunk[d][s], :], scalar(3, s, d, v).broadcast_to([128, 128]),
                                                      ALU.mult)
                    kd.up(ins)
            body(0)
            with pool.Fori(1, HEADS) as i:
                body(i)

        @block.scalar
        def _(act):
            def body(i):
                out.wait(act, i, 0)
                for r_, blk in ((2, i * 2 + 16), (3, i * 2 + 17), (0, i), (1, i + 8)):
                    silu.up(nc.scalar.activation(row[:, r_:r_ + 1, :], qkv[:, one(blk), :], ACT.Silu))
                silu.wait(act, i, 4)
                nc.scalar.activation(raw[:, 0, :], row[:, 0, :], ACT.Square)
                sq.up(nc.scalar.activation(raw[:, 1, :], row[:, 1, :], ACT.Square))
                vturn.wait(act, i, 1)
                for v in range(2):
                    ins = nc.scalar.activation(Vt[v].rearrange("p t n -> p (t n)"), c.P[:, v, 0:T], ACT.Copy)
                vt.up(ins)
                sse.wait(act, i, 1)
                ssd.up(nc.scalar.activation(norm, norm, ACT.Sqrt))
                kturn.wait(act, i, 1)
                kt.up(nc.scalar.activation(Kt.rearrange("p t n -> p (t n)"), PF[:, 0:T], ACT.Copy))
                for s in range(STEPS + 1):
                    if s < STEPS:
                        dm.wait(act, i, s + 1)
                        if s >= 2:
                            er.up(nc.scalar.activation(QDs[s % 2], PA, ACT.Exp))
                        dt.up(nc.scalar.activation(DTs[s % 2], DTs[s % 2], ACT.Exp))
                    if s:
                        vn.wait(act, i, s)
                        vncp.up(nc.scalar.activation(VN, PVN, ACT.Copy))
                    if s < STEPS:
                        xturn.wait(act, i, s + 1)
                        for d in range(2):
                            ins = nc.scalar.activation(XX[:, d, 256:512], half(PY[d], 0), ACT.Copy)
                        xcp.up(ins)
                        for l in range(1, LEVELS):
                            for d in range(2):
                                y.wait(act, i, nth(s, l, d))
                                z.wait(act, i, nth(s, l, d) - 2)
                                ycp.up(nc.scalar.activation(half(Y, d), half(PY[d], 0), ACT.Copy))
                        for d, v, n in unit:
                            ins = nc.scalar.activation(at_u(R, n), Vt[v][:, chunk[d][s], :], ACT.Copy, scale=scalar(0, s, d, v))
                        bv.up(ins)
            body(0)
            with act.Fori(1, HEADS) as i:
                body(i)

        @block.vector
        def _(dve):
            dve.wait_ge(landed, 32)

            def body(i):
                colss.wait(dve, i, 1)
                ss.wait(dve, i, 1)
                sse.up(nc.vector.tensor_scalar(norm, PF[:, 2048:2060], 1.0, 1e-6, ALU.mult, ALU.add))
                ssd.wait(dve, i, 1)
                ssr.up(nc.vector.reciprocal(inv_norm, norm))
                norm_rows.wait(dve, i, 1)
                nc.vector.scalar_tensor_tensor(out=row[:, 0, :], in0=row[:, 0, :], scalar=128 ** -0.5, in1=PF[:, 2560:2560 + T],
                                               op0=ALU.mult, op1=ALU.mult)
                qk.up(nc.vector.tensor_tensor(row[:, 1, :], row[:, 1, :], PF[:, 2560 + T:4096], ALU.mult))
                kturn.wait(dve, i, 1)
                gk.up(nc.vector.tensor_copy(GK.rearrange("p t k n -> p (t k n)"), PF[:, 1024:2560]))
                for s in range(STEPS + 1):
                    DT, QD = DTs[s % 2], QDs[s % 2]
                    if s < STEPS:
                        rows.wait(dve, i, s + 1)
                        for d, v, n in unit:
                            ins = nc.vector.tensor_scalar(at_u(DT, n), at_u(PA, n), scalar(2, s, d, v), 0.0, ALU.add, ALU.min)
                        dm.up(ins)
                        for d in range(2):
                            ins = nc.vector.tensor_tensor(four(LT)[:, d], GK[:, chunk[d][s], 0:1, :].broadcast_to([128, 2, 128]),
                                                          four(PB)[:, d], ALU.mult)
                        lt0.up(ins)
                    if s:
                        ks.wait(dve, i, s)
                        bv.wait(dve, i, s)
                        for d, v, n in unit:
                            ins = nc.vector.scalar_tensor_tensor(out=at_u(R, n), in0=at_u(PKS, n), scalar=scalar(1, s - 1, d, v),
                                                                 in1=at_u(R, n), op0=ALU.mult, op1=ALU.add)
                        r.up(ins)
                    if s < STEPS:
                        dt.wait(dve, i, s + 1)
                        for d in range(2):
                            ins = nc.vector.tensor_tensor(four(DT)[:, d], four(DT)[:, d], over_heads(tri, d), ALU.mult)
                        dtm.up(ins)
                        lt0.wait(dve, i, s + 1)
                        dtm.wait(dve, i, s + 1)
                        lt.up(nc.vector.tensor_tensor(LT, LT, DT, ALU.mult))
                        lt.wait(dve, i, s + 1)
                        for d in range(2):
                            ins = nc.vector.tensor_tensor(four(EM)[:, d], four(LT)[:, d], over_heads(masks[:, 0], d), ALU.mult)
                        e0.up(ins)
                        e0.wait(dve, i, s + 1)
                        for d in range(2):
                            ins = nc.vector.tensor_tensor(XX[:, d, 0:256].rearrange("p (v t) -> p v t", v=2),
                                                          c.ident[:, :].unsqueeze(1).broadcast_to([128, 2, 128]),
                                                          four(EM)[:, d], ALU.subtract)
                        x0.up(ins)
                        if s >= 2:
                            for d in range(2):
                                ins = nc.vector.tensor_tensor(four(DT)[:, d], four(DT)[:, d],
                                                              GK[:, chunk[d][s], 1:2, :].broadcast_to([128, 2, 128]), ALU.mult)
                            attn.up(ins)
                            er.wait(dve, i, s - 1)
                            for d in range(2):
                                t0 = chunk[d][s] * 128
                                ins = nc.vector.tensor_tensor(four(QD)[:, d], four(QD)[:, d],
                                                              row[:, 0:1, t0:t0 + 128].broadcast_to([128, 2, 128]), ALU.mult)
                            qd.up(ins)
                    if s:
                        sn.wait(dve, i, s)
                        for d, v, n in unit:
                            ins = nc.vector.scalar_tensor_tensor(out=at_u(S, n), in0=at_u(S, n), scalar=scalar(4, s - 1, d, v),
                                                                 in1=at_u(PKS, n), op0=ALU.mult, op1=ALU.add)
                        st.up(ins)
                        if s >= 3:
                            for d in range(2):
                                t0 = chunk[d][s - 1] * 128
                                part = o_sum[:, :, t0:t0 + 128]
                                po = half(PZ[d], 0).rearrange("p (v t) -> p v t", v=2)
                                if s - 1 < 4:
                                    ins = nc.vector.tensor_copy(part, po)
                                else:
                                    ins = nc.vector.tensor_tensor(part, part, po, ALU.add)
                            oadd.up(ins)
                    if s < STEPS:
                        for l in range(1, LEVELS):
                            for d in range(2):
                                z.wait(dve, i, nth(s, l, d))
                                if l < L:
                                    ins = nc.vector.tensor_tensor(XX[:, d], XX[:, d], PZ[d], ALU.subtract)
                                else:
                                    ins = nc.vector.tensor_tensor(half(XF, d), XX[:, d, 0:256], half(PZ[d], 0), ALU.subtract)
                                xl.up(ins)
                oadd.wait(dve, i, STEPS - 2)
                out.up(nc.vector.tensor_scalar(qkv[:, bass.ds(i * 2 + 16, 2), 0:LAT], o_sum, 1.0, None, ALU.mult))
            body(0)
            with dve.Fori(1, HEADS) as i:
                body(i)

        @block.tensor
        def _(pe):
            pe.wait_ge(landed, 32)

            def body(i):
                silu.wait(pe, i, 2)
                oadd.wait(pe, i, 0)
                for v in range(2):
                    for t in range(6):
                        ins = nc.tensor.transpose(c.P[:, v, 128 * t:128 * t + 128], row[:, 2 + v, 128 * t:128 * t + 128], c.ident[:, :])
                vturn.up(ins)
                sq.wait(pe, i, 1)
                for n in range(12):
                    ins = nc.tensor.matmul(PF[:, 2048 + n:2049 + n], raw[:, n // 6, 128 * (n % 6):128 * (n % 6) + 128], c.ones[:, 0:1],
                                           start=True, stop=True)
                ss.up(ins)
                ssr.wait(pe, i, 1)
                for n in range(12):
                    ins = nc.tensor.matmul(PF[:, 2560 + 128 * n:2688 + 128 * n], inv_norm[:, n:n + 1].broadcast_to([128, 128]), c.ident[:, :],
                                           start=True, stop=True)
                norm_rows.up(ins)
                qk.wait(pe, i, 1)
                vt.wait(pe, i, 1)
                for t in range(6):
                    k_t, q_t = row[:, 1, 128 * t:128 * t + 128], row[:, 0, 128 * t:128 * t + 128]
                    nc.tensor.transpose(PF[:, 128 * t:128 * t + 128], k_t, c.ident[:, :])
                    nc.tensor.matmul(PF[:, 1024 + 256 * t:1152 + 256 * t], k_t, k_t, start=True, stop=True)
                    ins = nc.tensor.matmul(PF[:, 1152 + 256 * t:1280 + 256 * t], k_t, q_t, start=True, stop=True)
                kturn.up(ins)
                kt.wait(pe, i, 1)
                gk.wait(pe, i, 1)
                for s in range(STEPS + 1):
                    if s < STEPS:
                        lt0.wait(pe, i, s)
                        for d, v, n in unit:
                            g, b = scalar(5, s, d, v), scalar(0, s, d, v)
                            nc.tensor.matmul(at_u(PA, n), g.broadcast_to([128, 128]), tri[:, d, :], start=True, stop=True)
                            ins = nc.tensor.matmul(at_u(PB, n), b.broadcast_to([128, 128]), c.ident[:, :], start=True, stop=True)
                        rows.up(ins)
                    if s:
                        st.wait(pe, i, s - 1)
                        for d in range(2):
                            t0 = 128 * chunk[d][s - 1]
                            ins = nc.tensor.matmul(half(PKS, d), row[:, 1, t0:t0 + 128], half(S, d), start=True, stop=True)
                        ks.up(ins)
                        r.wait(pe, i, s)
                        xl.wait(pe, i, nth(s - 1, L, 1))
                        for d, v, n in unit:
                            ins = nc.tensor.matmul(at_u(PVN, n), at_u(XF, n), at_u(R, n), start=True, stop=True)
                        vn.up(ins)
                    if s < STEPS:
                        x0.wait(pe, i, s + 1)
                        for d, v, n in unit:
                            ins = nc.tensor.transpose(at_u(PY[d], v), xt(n), c.ident[:, :])
                        xturn.up(ins)
                    if s:
                        vncp.wait(pe, i, s)
                        if s >= 3:
                            qd.wait(pe, i, s - 2)
                            for d, v, n in unit:
                                nc.tensor.matmul(at_u(PZ[d], v), at_u(VN, n), at_u(DTs[(s - 1) % 2], n), start=True, stop=False)
                                ins = nc.tensor.matmul(at_u(PZ[d], v), at_u(S, n), at_u(QDs[(s - 1) % 2], n), start=False, stop=True)
                            o.up(ins)
                        kd.wait(pe, i, s)
                        for d, v, n in unit:
                            ins = nc.tensor.matmul(at_u(PKS, n), at_u(KD_, n), at_u(VN, n), start=True, stop=True)
                        sn.up(ins)
                    if s < STEPS:
                        xcp.wait(pe, i, s + 1)
                        for l in range(1, LEVELS):
                            for d in range(2):
                                et.wait(pe, i, nth(s, l, d))
                                if l > 1:
                                    xl.wait(pe, i, nth(s, l, d) - 2)
                                for v in range(2):
                                    n = 2 * d + v
                                    ins = nc.tensor.matmul(at_u(PY[d], v), at_u(E[l % 2], n), xi(n), start=True, stop=True)
                                y.up(ins)
                            if l == 1 and s >= 3:
                                oadd.wait(pe, i, s - 2)
                            for d in range(2):
                                ycp.wait(pe, i, nth(s, l, d))
                                for v in range(2):
                                    n = 2 * d + v
                                    ins = nc.tensor.matmul(at_u(PZ[d], v), at_u(Y, n), xt(n), start=True, stop=True)
                                if l < L:
                                    for v in range(2):
                                        n = 2 * d + v
                                        ins = nc.tensor.matmul(at_u(PZ[d], 2 + v), xt(n), at_u(Y, n), start=True, stop=True)
                                z.up(ins)
            body(0)
            with pe.Fori(1, HEADS) as i:
                body(i)


def head_norm(c, o, at, gain):
    nc = c.nc
    sq, rs = c.view(at, 4, LAT), c.view(at + 4 * LAT, 4, LAT)
    flat = lambda x: x.rearrange("p a b -> p (a b)")
    s = {n: c.sem("headnorm_" + n) for n in ("sq", "sum", "var", "sd", "rs", "out")}
    psum = c.P[:, 0:2, :].rearrange("p a b -> p (a b)")
    with nc.Block() as block:
        @block.sync
        def _(sp):
            c.prefetch(sp, "gdn_ba")

        @block.scalar
        def _(act):
            for q in range(4):
                if q:
                    act.wait_ge(s["sum"], q)
                nc.scalar.activation(sq, o[:, 4 * q:4 * q + 4, 0:LAT], ACT.Square).then_inc(s["sq"], 1)
                act.wait_ge(s["var"], q + 1)
                nc.scalar.activation(flat(rs), flat(rs), ACT.Sqrt).then_inc(s["sd"], 1)

        @block.tensor
        def _(pe):
            for q in range(4):
                pe.wait_ge(s["sq"], q + 1)
                if q:
                    pe.wait_ge(s["var"], q)
                for n in range(4):
                    last = nc.tensor.matmul(psum[:, 512 * n:512 * n + 512], c.ones[:, :], sq[:, n, :], start=True, stop=True)
                last.then_inc(s["sum"], 1)

        @block.vector
        def _(dve):
            for q in range(4):
                dve.wait_ge(s["sum"], q + 1)
                if q:
                    dve.wait_ge(s["out"], q)
                nc.vector.tensor_scalar(flat(rs), psum, 1.0 / 128, 1e-6, ALU.mult, ALU.add).then_inc(s["var"], 1)
                dve.wait_ge(s["sd"], q + 1)
                nc.vector.reciprocal(flat(rs), flat(rs)).then_inc(s["rs"], 1)
                dve.wait_ge(s["rs"], q + 1)
                x = o[:, 4 * q:4 * q + 4, 0:LAT]
                nc.vector.scalar_tensor_tensor(out=x, in0=x, scalar=gain, in1=rs, op0=ALU.mult, op1=ALU.mult
                                               ).then_inc(s["out"], 1)


MAGIC = 1.5 * 2.0 ** 23
TURN = 6.283185307179586


def s5_params(c, par, at):
    nc = c.nc
    N = 128
    raw = c.view(at, 3, N)
    w = [c.view(at + 3 * N + N * n, N) for n in range(12)]
    out = lambda q: par[:, :, q, :]
    sq2 = lambda x: x.rearrange("p (b e) -> p b e", e=8)
    landed, dv, ac = (c.sem("s5par_" + n) for n in ("landed", "dve", "act"))
    re, im, ls = raw[:, 0, :], raw[:, 1, :], raw[:, 2, :]
    with nc.Block() as block:
        @block.sync
        def _(sp):
            sp.dma_start(raw.rearrange("p a b -> p (a b)"), c.ins["s5_lam"]).then_inc(landed, 16)

        @block.scalar
        def _(act):
            act.wait_ge(landed, 16)
            nc.scalar.activation(w[0], ls, ACT.Exp).then_inc(ac, 1)
            act.wait_ge(dv, 1)
            nc.scalar.activation(w[2], w[1], ACT.Exp).then_inc(ac, 1)
            act.wait_ge(dv, 9)
            nc.scalar.activation(w[5], w[4], ACT.Sin, scale=TURN).then_inc(ac, 1)
            nc.scalar.activation(w[7], w[6], ACT.Sin, scale=TURN).then_inc(ac, 1)

        @block.vector
        def _(dve):
            n = [0]

            def step(ins):
                ins.then_inc(dv, 1)
                n[0] += 1
                dve.wait_ge(dv, n[0])
            V = nc.vector
            dve.wait_ge(ac, 1)
            step(V.tensor_tensor(w[1], re, w[0], ALU.mult))
            step(V.tensor_tensor(w[3], im, w[0], ALU.mult))
            step(V.tensor_scalar(w[3], w[3], 1.0 / TURN, None, ALU.mult))
            step(V.tensor_scalar(w[4], w[3], MAGIC, -MAGIC, ALU.add, ALU.add))
            step(V.tensor_tensor(w[4], w[3], w[4], ALU.subtract))
            step(V.tensor_scalar(w[6], w[4], 0.25, None, ALU.add))
            step(V.tensor_scalar(w[8], w[6], MAGIC, -MAGIC, ALU.add, ALU.add))
            step(V.tensor_tensor(w[6], w[6], w[8], ALU.subtract))
            step(V.tensor_scalar(w[8], w[4], 3.0 * 2.0 ** 10, -3.0 * 2.0 ** 10, ALU.add, ALU.add))
            V.tensor_copy(out(1), sq2(w[8]))
            step(V.tensor_tensor(out(2), sq2(w[4]), sq2(w[8]), ALU.subtract))
            dve.wait_ge(ac, 4)
            V.tensor_copy(out(0), sq2(w[2]))
            step(V.tensor_tensor(w[9], w[2], w[7], ALU.mult))
            V.tensor_scalar(w[9], w[9], -1.0, None, ALU.add)
            step(V.tensor_tensor(w[10], w[2], w[5], ALU.mult))
            V.tensor_tensor(w[0], re, re, ALU.mult)
            step(V.tensor_tensor(w[1], im, im, ALU.mult))
            step(V.tensor_tensor(w[0], w[0], w[1], ALU.add))
            step(V.reciprocal(w[11], w[0]))
            V.tensor_tensor(w[0], w[9], re, ALU.mult)
            V.tensor_tensor(w[1], w[10], im, ALU.mult)
            V.tensor_tensor(w[2], w[10], re, ALU.mult)
            step(V.tensor_tensor(w[3], w[9], im, ALU.mult))
            V.tensor_tensor(w[0], w[0], w[1], ALU.add)
            step(V.tensor_tensor(w[2], w[2], w[3], ALU.subtract))
            V.tensor_tensor(out(3), sq2(w[0]), sq2(w[11]), ALU.mult)
            V.tensor_tensor(out(4), sq2(w[2]), sq2(w[11]), ALU.mult)


def s5_scan(c, p, par, at, skip):
    nc = c.nc
    U, CH, N = 8, 128, T // 128
    take = lambda *shape: (c.view(place[0], *shape), place.__setitem__(0, place[0] + int(np.prod(shape))))[0]
    place = [at]
    steps, Bm, Cm = take(CH), take(2, 2, 128), take(2, 4, 2, 32)
    xs, col, signed, turn_c, turn_s, carry = take(T), take(5, 8), take(8, 2), take(2, 2), take(2, 2), take(2, 2)
    fs, fc, Tr, Ti = take(U, CH), take(U, CH), take(U, CH), take(U, CH)
    t4 = [take(4, T), take(4, T)]
    tmp = c.tmp[:, :, :, :].rearrange("p a b c -> p (a b c)")
    half = [tmp[:, 1024 * n:1024 * n + 1024].rearrange("p (a t) -> p a t", a=2) for n in range(2)]
    ctx_g = c.stat[:, :, :].rearrange("p a t -> p (a t)")[:, 0:1024].rearrange("p (u r t) -> p u r t", u=2, r=2)
    lat_g = [take(2, 2, LAT) for _ in range(2)]
    Cneg = c.stat[:, :, :].rearrange("p a t -> p (a t)")[:, 1024:1280].rearrange("p (d q n) -> p d q n", d=2, q=4)
    A, W = (t4[0][:, :, :].rearrange("p a t -> p (a t)")[:, 1024 * n:1024 * n + 1024].rearrange("p (u t) -> p u t", u=U)
            for n in range(2))
    landed, mats = c.sem("s5_landed"), c.sem("s5_mats")
    F = lambda name, per: Flag(c, "s5_" + name, per)
    staged, out, phase, trig, tables = F("staged", 1), F("out", 1), F("phase", 1), F("trig", 1), F("tables", 1)
    bu, p4, add1 = F("bu", U), F("p4", U), F("add1", U // 2)
    g, halves, y, negated = F("g", U // 2), F("halves", 2 * U), F("y", 2 * U), F("negated", 1)
    chain = F("chain", 0)
    psum = c.P[:, :, :].rearrange("p a b -> p (a b)")
    PY = c.P[:, 2, 0:LAT]
    BU = [(psum[:, 0:T], psum[:, 1024:1024 + T]), (psum[:, 2560:2560 + T], psum[:, 2560 + T:4096])]
    unit = [(d, q, 4 * d + q) for d in range(2) for q in range(4)]
    chunks = lambda x: x.rearrange("p (c t) -> p c t", t=CH)
    table = lambda x, n, reps: x[:, n:n + 1, :].broadcast_to([128, reps, CH])

    def order(d):
        if d == 0:
            return [(0, slice(LAT, T)), (256, slice(0, 256)), (512, slice(256, 512))]
        return [(0, slice(T - 1, LAT - 1, -1)), (256, slice(LAT - 1, 255, -1)), (512, slice(255, None, -1))]
    with nc.Block() as block:
        @block.sync
        def _(sp):
            sp.dma_start(steps, c.ins["s5_steps"]).then_inc(landed, 16)

            def body(i):
                out.wait(sp, i, 0)
                sp.dma_start(Bm.rearrange("p a b c -> p (a b c)"), rows_of(c.ins["s5_b"], i)).then_inc(mats, 16)
                sp.dma_start(Cm.rearrange("p a b c d -> p (a b c d)"), rows_of(c.ins["s5_c"], i)).then_inc(mats, 16)
            body(0)
            with sp.Fori(1, 16) as i:
                body(i)

        @block.gpsimd
        def _(pool):
            tt = nc.gpsimd.tensor_tensor

            def body(i):
                out.wait(pool, i, 0)
                nc.gpsimd.tensor_copy(col.rearrange("p a b -> p (a b)").unsqueeze(1),
                                      par[:, one(i), :, :].rearrange("p k a b -> p k (a b)"))
                staged.up(nc.gpsimd.tensor_copy(xs.unsqueeze(1), p[:, one(i), :]))

                def inputs(n):
                    x = t4[0]
                    p4.wait(pool, i, n + 1)
                    tt(x[:, 0, :], x[:, 0, :], x[:, 1, :], ALU.subtract)
                    add1.up(tt(x[:, 2, :], x[:, 2, :], x[:, 3, :], ALU.add))

                def states(n):
                    if n % 2 == 0:
                        g.wait(pool, i, n // 2 + 1)
                    G = lat_g[n // 2 % 2][:, n % 2]
                    for k, tabs in enumerate(((fc, fs), (fs, fc))):
                        y.wait(pool, i, 2 * n + k - 1)
                        tt(chunks(half[k][:, 0, :]), chunks(G[:, 0, :]), table(tabs[0], n, 4), ALU.mult)
                        halves.up(tt(chunks(half[k][:, 1, :]), chunks(G[:, 1, :]), table(tabs[1], n, 4), ALU.mult))
                inputs(0)
                for n in range(0, U, 2):
                    if n + 2 < U:
                        inputs(n + 2)
                    states(n)
                    states(n + 1)
            body(0)
            with pool.Fori(1, 16) as i:
                body(i)

        @block.scalar
        def _(act):
            def body(i):
                act.wait_ge(mats, i * 32 + 32)
                negated.up(nc.scalar.activation(Cneg, Cm[:, :, :, 1, :], ACT.Copy, scale=-1.0))
                phase.wait(act, i, 1)
                nc.scalar.activation(fs, fs, ACT.Sin, scale=-TURN)
                trig.up(nc.scalar.activation(fc, fc, ACT.Sin, scale=TURN))
            body(0)
            with act.Fori(1, 16) as i:
                body(i)

        @block.vector
        def _(dve):
            dve.wait_ge(landed, 16)
            V = nc.vector
            ts, tt, stt = V.tensor_scalar, V.tensor_tensor, V.scalar_tensor_tensor

            def body(i):
                staged.wait(dve, i, 1)
                n_ = [0]

                def step(ins):
                    chain.up(ins)
                    n_[0] += 1
                    chain.wait(dve, i, n_[0])
                by_t = lambda q: col[:, q, :].unsqueeze(2).broadcast_to([128, U, CH])
                by_u = steps.unsqueeze(1).broadcast_to([128, U, CH])
                step(tt(A, by_u, by_t(1), ALU.mult))
                step(ts(W, A, MAGIC, -MAGIC, ALU.add, ALU.add))
                step(tt(A, A, W, ALU.subtract))
                step(tt(W, by_u, by_t(2), ALU.mult))
                step(tt(A, A, W, ALU.add))
                step(ts(W, A, MAGIC, -MAGIC, ALU.add, ALU.add))
                step(tt(fs, A, W, ALU.subtract))
                step(ts(W, fs, 0.25, None, ALU.is_gt))
                phase.up(stt(out=fc, in0=fs, scalar=0.25, in1=W, op0=ALU.add, op1=ALU.subtract))
                trig.wait(dve, i, 1)
                tt(Ti, fc, by_t(4), ALU.mult)
                tt(Tr, fc, by_t(3), ALU.mult)
                tt(W, fs, by_t(3), ALU.mult)
                ts(signed[:, :, 0:1], fs[:, :, CH - 1:CH], 1.0, None, ALU.mult)
                ts(signed[:, :, 1:2], fs[:, :, CH - 1:CH], -1.0, None, ALU.mult)
                step(tt(A, fs, by_t(4), ALU.mult))
                tt(Ti, Ti, W, ALU.add)
                step(tt(Tr, Tr, A, ALU.subtract))

                def inputs(n):
                    x = t4[n % 2]
                    bu.wait(dve, i, n + 1)
                    PR, PI = BU[n % 2]
                    for k, (ps, tab) in enumerate(((PR, Tr), (PI, Ti), (PI, Tr), (PR, Ti))):
                        ins = tt(chunks(x[:, k, :]), chunks(ps), table(tab, n, N), ALU.mult)
                    p4.up(ins)
                    if n % 2:
                        p4.wait(dve, i, n + 1)
                        tt(x[:, 0, :], x[:, 0, :], x[:, 1, :], ALU.subtract)
                        step(tt(x[:, 2, :], x[:, 2, :], x[:, 3, :], ALU.add))

                def scan(n):
                    add1.wait(dve, i, n // 2 + 1)
                    halves.wait(dve, i, 2 * n - 4)
                    for k in range(N):
                        into = ctx_g[:, :, :, CH * k:CH * k + CH] if k < 2 else lat_g[n // 2 % 2][:, :, :, CH * (k - 2):CH * (k - 1)]
                        for e in range(2):
                            rb = col[:, 0, n + e:n + e + 1].broadcast_to([128, CH])
                            for part in range(2):
                                ins = V.tensor_tensor_scan(into[:, e, part, :], rb, t4[e][:, 2 * part, CH * k:CH * k + CH],
                                                           carry[:, e, part:part + 1] if k else 0.0, ALU.mult, ALU.add)
                        if k == N - 1:
                            g.up(ins)
                            continue
                        step(ins)
                        last = into[:, :, :, CH - 1:CH].rearrange("p e r o -> p e (r o)")
                        tt(turn_c, last, fc[:, n:n + 2, CH - 1:CH].broadcast_to([128, 2, 2]), ALU.mult)
                        step(tt(turn_s, last[:, :, ::-1], signed[:, n:n + 2, :], ALU.mult))
                        step(tt(carry, turn_c, turn_s, ALU.add))
                inputs(0)
                inputs(1)
                for n in range(0, U, 2):
                    scan(n)
                    if n + 2 < U:
                        g.wait(dve, i, n // 2 + 1)
                        inputs(n + 2)
                        inputs(n + 3)
                y.wait(dve, i, 2 * U)
                out.up(stt(out=p[:, one(i), 0:LAT], in0=xs[:, 0:LAT].unsqueeze(1), scalar=skip(i),
                           in1=PY.unsqueeze(1), op0=ALU.mult, op1=ALU.add))
                return n_[0]
            chain.per = body(0)
            with dve.Fori(1, 16) as i:
                body(i)

        @block.tensor
        def _(pe):
            def body(i):
                staged.wait(pe, i, 1)
                pe.wait_ge(mats, i * 32 + 32)

                def inputs(n):
                    d, q, _ = unit[n]
                    p4.wait(pe, i, n - 1)
                    for k, ps in enumerate(BU[n % 2]):
                        for a, cols in order(d):
                            ins = nc.tensor.matmul(ps[:, a:a + 256], Bm[32 * q:32 * q + 32, d, k, :],
                                                   xs[32 * q:32 * q + 32, cols], start=True, stop=True)
                    bu.up(ins)

                def outputs(n):
                    d, q, _ = unit[n]
                    cols = slice(0, LAT) if d == 0 else slice(LAT - 1, None, -1)
                    for k, mats_k in enumerate(((Cm[:, d, q, 0, :], Cm[:, d, q, 0, :]), (Cm[:, d, q, 1, :], Cneg[:, d, q, :]))):
                        halves.wait(pe, i, 2 * n + k + 1)
                        for e in range(2):
                            ins = nc.tensor.matmul(PY[32 * q:32 * q + 32, :], mats_k[e], half[k][:, e, :][:, cols],
                                                   start=d == 0 and k == 0 and e == 0, stop=d == 1 and k == 1 and e == 1,
                                                   skip_group_check=True)
                        y.up(ins)
                negated.wait(pe, i, 1)
                inputs(0)
                inputs(1)
                for n in range(0, U, 2):
                    if n + 2 < U:
                        inputs(n + 2)
                        inputs(n + 3)
                    outputs(n)
                    outputs(n + 1)
            body(0)
            with pe.Fori(1, 16) as i:
                body(i)


def gelu(c, p):
    nc = c.nc
    with nc.Block() as block:
        @block.scalar
        def _(act):
            for g in range(4):
                nc.scalar.activation(p[:, 4 * g:4 * g + 4, 0:LAT], p[:, 4 * g:4 * g + 4, 0:LAT], ACT.Gelu_apprx_tanh)


VECS = [("b_mod0", 48), ("b_mod1", 48), ("ada_b_20", 24), ("ada_b_21", 24),
        ("c", 8), ("c_ctx", 8), ("c_2", 8), ("c_ctx_2", 8),
        ("ln1_g0", 8), ("ln1_b0", 8), ("ln2_g0", 8), ("ln2_b0", 8), ("ln1_g1", 8), ("ln1_b1", 8), ("ln2_g1", 8), ("ln2_b1", 8),
        ("ln_g_20", 8), ("ln_b_20", 8), ("ln_g_21", 8), ("ln_b_21", 8),
        ("mla_q_norm", 4), ("mla_kv_norm", 2), ("gdn_norm", 1), ("s5_d", 16), ("s5_glu_b", 16), ("sink", 16), ("gdn_taps", 160)]
VEC_AT = {}
_at = 0
for _n, _w in VECS:
    VEC_AT[_n] = _at
    _at += _w
VEC_WIDTH = _at


def program(nc, ins, out):
    c = Core(nc, ins)
    P = c.P
    act_fn, vec_fn = nc.scalar.activation, nc.vector
    h, u, area = c.h, c.u, c.view
    vcol = lambda name: (lambda k: c.vec[:, VEC_AT[name] + k:VEC_AT[name] + k + 1])

    landed, vec_landed, silu_c = c.sem("landed"), c.sem("vec_landed"), c.sem("silu_c")
    DEEP = 8
    rounds = ins["w_mod"].shape[0] // DEEP
    mod_ready = [c.sem(f"mod_ready{s}") for s in range(DEEP)]
    mod_done, mod_kept, bias_in = c.sem("mod_done"), c.sem("mod_kept"), c.sem("bias_in")
    rows_out, turned = c.sem("mod_rows_out"), c.sem("mod_turned")
    cond, rows, mod_ring = area(0, KD, 4), area(KD * 4, 2, 256)[0:4], area(KD * 4 + 512, DEEP, 2 * D)
    banks = P[:, :, :].rearrange("p a b -> p (a b)")

    def behind(eng, sem, r, g, by):
        if not isinstance(r, int) or r * DEEP + g + 1 > by:
            eng.wait_ge(sem, r * DEEP + (g + 1 - by))

    def load_mod(eng, r, slots):
        for g in slots:
            if not (isinstance(r, int) and r == 0):
                eng.wait_ge(mod_done, r * DEEP + (g + 1 - DEEP))
            eng.dma_start(mod_ring[:, g, :], rows_of(ins["w_mod"], r * DEEP + g)).then_inc(mod_ready[g], 16)
    with nc.Block() as block:
        @block.sync
        def _(sp):
            sp.dma_start(c.vec[:, :], ins["vecs"]).then_inc(vec_landed, 16)
            sp.dma_start(c.ident[:, :], ins["ident"]).then_inc(vec_landed, 16)
            pairs(sp, rounds, lambda r, s, first: load_mod(sp, r, range(0, DEEP, 2)))
            c.load_slot(sp, "mla_in", 0, 0)
            c.load_slot(sp, "mla_in", 1, 1)
            sp.dma_start(h[:, :, 0:LAT], ins["x"].rearrange("p (k t) -> p k t", k=KD)).then_inc(landed, 16)
            sp.dma_start(h[:, :, LAT:T], ins["ctx"].rearrange("p (k t) -> p k t", k=KD)).then_inc(landed, 16)
            sp.dma_start(c.ones[:, :], ins["ones"]).then_inc(landed, 16)

        @block.gpsimd
        def _(pool):
            pairs(pool, rounds, lambda r, s, first: load_mod(pool, r, range(1, DEEP, 2)))

        @block.tensor
        def _(pe):
            pe.wait_ge(silu_c, 1)

            def turn_rows(r, g):
                behind(pe, rows_out, r, g, 0)
                for j in range(2):
                    last = nc.tensor.matmul(banks[:, 512 * (g % DEEP) + 256 + 4 * j:][:, 0:4],
                                            rows[:, g % 2, j * 128:(j + 1) * 128], c.ident[0:4, 0:4], start=True, stop=True)
                last.then_inc(turned, 1)

            def body(r, s, first):
                for g in range(DEEP):
                    pe.wait_ge(mod_ready[g], r * 16 + 16)
                    behind(pe, mod_kept, r, g, DEEP)
                    for k in range(KD):
                        last = nc.tensor.matmul(banks[0:4, 512 * g:512 * g + 256], cond[:, k, :],
                                                mod_ring[:, g, :].rearrange("p (j k n) -> p j k n", j=2, k=KD)[:, :, k, :],
                                                start=k == 0, stop=k == KD - 1)
                    last.then_inc(mod_done, 1)
                    if g or not (isinstance(r, int) and r == 0):
                        turn_rows(r, g - 1)
            pairs(pe, rounds, body)
            turn_rows(rounds - 1, DEEP - 1)

        @block.scalar
        def _(act):
            act.wait_ge(vec_landed, 32)
            v = c.vec[:, VEC_AT["c"]:VEC_AT["c"] + 32].rearrange("p (c k) -> p k c", c=4)
            act_fn(cond, v, ACT.Silu).then_inc(silu_c, 1)

            def keep(r, g):
                behind(act, turned, r, g, 0)
                act_fn(c.mod[:, bass.ds(r * (2 * DEEP) + 2 * g, 2), :],
                       banks[:, 512 * (g % DEEP) + 256:][:, 0:8].rearrange("p (b c) -> p b c", c=4), ACT.Copy).then_inc(mod_kept, 1)

            def body(r, s, first):
                for g in range(DEEP):
                    behind(act, mod_done, r, g, 0)
                    behind(act, turned, r, g, 2)
                    act_fn(rows[:, g % 2, :], banks[0:4, 512 * g:512 * g + 256], ACT.Copy).then_inc(rows_out, 1)
                    if g or not (isinstance(r, int) and r == 0):
                        keep(r, g - 1)
            pairs(act, rounds, body)
            keep(rounds - 1, DEEP - 1)

        @block.vector
        def _(dve):
            dve.wait_ge(mod_kept, rounds * DEEP)
            vec_fn.tensor_tensor(c.mod[:, :, :], c.mod[:, :, :], c.vec[:, 0:144].unsqueeze(2).broadcast_to([128, 144, 4]), ALU.add
                                 ).then_inc(bias_in, 1)
            dve.wait_ge(bias_in, 1)
            for a in (8, 32, 56, 80, 104, 128):
                vec_fn.tensor_scalar(c.mod[:, a:a + 8, :], c.mod[:, a:a + 8, :], 1.0, None, ALU.add)
            dve.wait_ge(landed, 48)

    def modcol(base, cond_):
        return lambda k: c.mod[:, base + k, cond_:cond_ + 1]

    def modulated(base, conds=(0, 1)):
        segs = [(0, LAT), (LAT, T)][:len(conds)]
        return [(modcol(base + 8, cc), modcol(base, cc), a, b) for cc, (a, b) in zip(conds, segs)]

    def modulate(parts, loads=None):
        got = c.sem("ctx_landed")
        with nc.Block() as block:
            if loads is not None:
                @block.sync
                def _(sp):
                    sp.dma_start(h[:, :, LAT:T], loads.rearrange("p (k t) -> p k t", k=KD)).then_inc(got, 16)

            @block.scalar
            def _(act):
                if loads is not None:
                    act.wait_ge(got, 16)
                for k in range(KD):
                    for scale, add, a, b in parts:
                        act_fn(u[:, k, a:b], h[:, k, a:b], ACT.Identity, scale=scale(k), bias=add(k))

    def residual(name, x, gate, conds, segs):
        per = c.shape_of(name)[1]

        def act(g, j, ps, tmp):
            for cc, (a, b) in zip(conds, ((0, LAT), (LAT, T))):
                last = act_fn(tmp[:, a:b], ps[:, a:b], ACT.Copy, scale=c.mod[:, bass.ds(g * per + (j + gate), 1), cc:cc + 1].rearrange("p a b -> p (a b)"))
            return last

        def vec(g, j, ps, tmp):
            w = T if len(conds) > 1 else LAT
            hk = h[:, one(g * per + j), 0:w]
            return vec_fn.scalar_tensor_tensor(out=hk, in0=hk, scalar=ALPHA, in1=tmp[:, 0:w].unsqueeze(1), op0=ALU.mult, op1=ALU.add)
        dense(c, name, x, segs, act, vec)

    def feed_forward(layer, conds, segs, hidden):
        w = T if len(conds) > 1 else LAT

        def act(g, j, ps, tmp):
            return act_fn(tmp[:, 0:w], ps[:, 0:w], ACT.Silu if j == 0 else ACT.Copy)

        def vec(g, j, ps, tmp):
            if j == 0:
                return None
            other = c.tmp[:, g_slot[0], 0, 0:w]
            return vec_fn.tensor_tensor(hidden[:, one(g), 0:w], other.unsqueeze(1), tmp[:, 0:w].unsqueeze(1), ALU.mult)
        g_slot = [0]

        def act_s(g, j, ps, tmp):
            return act(g, j, ps, tmp)

        def vec_s(g, j, ps, tmp):
            if j == 0:
                pairs_first[0] = tmp
                return None
            return vec_fn.tensor_tensor(hidden[:, one(g), 0:w], pairs_first[0][:, 0:w].unsqueeze(1), tmp[:, 0:w].unsqueeze(1), ALU.mult)
        pairs_first = [None]
        dense(c, f"ffn_in{layer}", u, segs, act_s, vec_s)
        residual(f"ffn_out{layer}", hidden, layer * 48 + 40, conds, segs)

    def copy_to(dst, off=0, per=2, w=T):
        return lambda g, j, ps, tmp: act_fn(dst[:, one(g * per + (j + off)), 0:w], ps[:, 0:w].unsqueeze(1), ACT.Copy)

    def silu_times(dst, w):
        act = lambda g, j, ps, tmp: act_fn(tmp[:, 0:w], ps[:, 0:w], ACT.Silu)

        def vec(g, j, ps, tmp):
            d = dst[:, one(g * 2 + j), 0:w]
            return vec_fn.tensor_tensor(d, d, tmp[:, 0:w].unsqueeze(1), ALU.mult)
        return act, vec

    modulate(modulated(0))
    rope_x, q_nope = area(0, 5, T), area(5 * T, 8, T)
    lat = area(13 * T, 7, T)
    k_nope = area(20 * T, 8, T)
    v_tok = area(28 * T, 6, D)
    dense(c, "mla_in", u, BOTH, copy_to(lat, per=1))
    moved = c.sem("k_rope_moved")
    with nc.Block() as block:
        @block.vector
        def _(dve):
            vec_fn.tensor_copy(rope_x[:, 4, :], lat[:, 6, :]).then_inc(moved, 1)
    normalise(c, "q_rms", lat, 4, T, BOTH, 1e-6, vcol("mla_q_norm"))
    normalise(c, "kv_rms", lat[:, 4:6, :], 2, T, BOTH, 1e-6, vcol("mla_kv_norm"))
    qx = area(0, 13, T)

    def q_act(g, j, ps, tmp):
        return act_fn(q_nope[:, one(g * 2 + j), :], ps[:, 0:T].unsqueeze(1), ACT.Copy)
    q_all = area(0, 13, T)
    k_hold = lat[:, 6, :]
    dense(c, "q_up", lat, BOTH, lambda g, j, ps, tmp: act_fn(q_all[:, one(g * 2 + (j + 1)), :], ps[:, 0:T].unsqueeze(1), ACT.Copy))
    with nc.Block() as block:
        order = c.sem("rope_order")
        @block.scalar
        def _(act):
            act_fn(q_all[:, 0, :], k_hold, ACT.Copy)
    dense(c, "k_up", lat[:, 4:6, :], BOTH, copy_to(k_nope))
    dense_tokens(c, "v_up", lat[:, 4:6, :], 256, v_tok)
    turn(c, "mla_rope", q_all, 5, area(13 * T, 3, 512), ("mla_trig", "mla_perm"))
    attention(c, "mla", 4, 2, False,
              q=lambda i, j: q_all[:, one(i * 2 + (5 + j)), :],
              k=lambda i, j, a, b: k_nope[:, one(i * 2 + j), a:b].rearrange("p a b -> p (a b)"),
              v=lambda i, j: v_tok[:, :, bass.ds(i * 256 + j * 128, 128)],
              out=lambda i, j, t: q_all[:, one(i * 2 + (5 + j)), 128 * t:128 * t + 128],
              at=13 * T, scale=MLA_SCALE,
              rope=(lambda i: q_all[:, one(i + 1), :],
                    lambda j, a, b: q_all[64 * j:64 * j + 64, 0, a:b]))
    residual("mla_out", q_all[:, 5:13, :], 16, (0, 1), BOTH)
    normalise(c, "ln1_0", h, 8, T, BOTH, 1e-5, vcol("ln1_g0"), vcol("ln1_b0"), after=(u, modulated(24)))
    hidden = area(0, KF, T)
    feed_forward(0, (0, 1), BOTH, hidden)
    normalise(c, "ln2_0", h, 8, T, BOTH, 1e-5, vcol("ln2_g0"), vcol("ln2_b0"), after=(u, modulated(48)))

    c.clear_sems()
    qkv = area(0, 32, T)
    at = 32 * T
    cols = area(at, 8, 6, 6, 2, 2) if False else None
    cols_flat = area(at, 1152)
    cols = cols_flat.rearrange("p (k q t d v) -> p k q t d v", k=8, q=6, t=6, d=2)
    at += 1152
    ba = area(at, 6, 64)
    tapped = c.sem("gdn_tapped")
    taps = area(32 * T, 2, 5)
    STEPS = 6

    def raw_rows(g, j, ps, tmp):
        return act_fn(tmp, ps[:, 0:T], ACT.Copy)

    def short_conv(g, j, ps, tmp):
        acc, n = c.stat[:, j, :], [0]

        def step(ins):
            ins.then_inc(tapped, 1)
            n[0] += 1
            nc.vector.wait_ge(tapped, g * (2 * STEPS) + (j * STEPS + n[0]))
        step(vec_fn.tensor_scalar(taps[:, j:j + 1, :], c.vec[:, bass.ds(g * 10 + (VEC_AT["gdn_taps"] + 5 * j), 5)].unsqueeze(1),
                                  1.0, None, ALU.mult))
        step(vec_fn.tensor_scalar(acc, tmp, taps[:, j, 2:3], None, ALU.mult))
        for sh in (-2, -1, 1, 2):
            for a, b in BOTH:
                lo, hi = max(a, a - sh), min(b, b - sh)
                ins = vec_fn.scalar_tensor_tensor(out=acc[:, lo:hi], in0=tmp[:, lo + sh:hi + sh], scalar=taps[:, j, sh + 2:sh + 3],
                                                  in1=acc[:, lo:hi], op0=ALU.mult, op1=ALU.add)
            step(ins)
        return vec_fn.tensor_scalar(qkv[:, one(g * 2 + j), :], acc.unsqueeze(1), 1.0, None, ALU.mult)
    dense(c, "gdn_qkv", u, BOTH, raw_rows, short_conv)
    dense_tokens(c, "gdn_ba", u, 64, ba, ahead=False)
    gdn_gates(c, ba, cols, at + 384)
    c.clear_sems()
    gdn_heads(c, qkv, cols, at)
    c.clear_sems()
    o_gdn = qkv[:, 16:32, :]
    head_norm(c, o_gdn, 0, c.vec[:, VEC_AT["gdn_norm"]:VEC_AT["gdn_norm"] + 1])
    modulate(modulated(48, (0,)))
    dense(c, "gdn_z", u, LATS, *silu_times(o_gdn, LAT))
    residual("gdn_out", o_gdn, 48 + 16, (0,), LATS)
    normalise(c, "ln1_1", h, 8, LAT, LATS, 1e-5, vcol("ln1_g1"), vcol("ln1_b1"), after=(u, modulated(48 + 24, (0,))))
    feed_forward(1, (0,), LATS, hidden)
    normalise(c, "ln2_1", h, 8, LAT, LATS, 1e-5, vcol("ln2_g1"), vcol("ln2_b1"))

    c.clear_sems()
    modulate(modulated(96, (2, 3)), loads=ins["ctx_2"])
    qk = area(0, 20, T)
    v2 = area(20 * T, 6, 512)
    dense(c, "att_qk", u, BOTH, copy_to(qk))
    dense_tokens(c, "att_v", u, 256, v2)
    turn(c, "att_rope", qk, 20, area(24 * T, 3, 512), ("att_trig", "att_perm"))
    attention(c, "att", 4, 4, True,
              q=lambda i, j: qk[:, one(i * 4 + j), :],
              k=lambda i, j, a, b: qk[:, one(i + 16), a:b].rearrange("p a b -> p (a b)"),
              v=lambda i, j: v2[:, :, bass.ds(i * 128, 128)],
              out=lambda i, j, t: qk[:, one(i * 4 + j), 128 * t:128 * t + 128],
              at=24 * T, scale=ATT_SCALE,
              sink=lambda i, j: c.vec[:, bass.ds(i * 4 + (VEC_AT["sink"] + j), 1)])
    dense(c, "att_z", u, BOTH, *silu_times(qk, T))
    residual("att_out", qk, 96 + 16, (2, 3), BOTH)
    normalise(c, "ln_2_0", h, 8, T, BOTH, 1e-5, vcol("ln_g_20"), vcol("ln_b_20"), after=(u, modulated(120, (2, 3))))

    c.clear_sems()
    p = area(0, 16, T)
    dense(c, "s5_in", u, BOTH, copy_to(p))
    par = area(16 * T, 16, 5, 8)
    s5_params(c, par, 16 * T + 640)
    s5_scan(c, p, par, 16 * T + 640, lambda i: c.vec[:, bass.ds(i + VEC_AT["s5_d"], 1)])
    gelu(c, p)
    y5 = area(16 * T, 16, LAT)

    def glu_act(g, j, ps, tmp):
        return act_fn(tmp[:, 0:LAT], ps[:, 0:LAT], ACT.Sigmoid, bias=c.vec[:, bass.ds(g + VEC_AT["s5_glu_b"], 1)])

    def glu_vec(g, j, ps, tmp):
        return vec_fn.tensor_tensor(y5[:, one(g), :], p[:, one(g), 0:LAT], tmp[:, 0:LAT].unsqueeze(1), ALU.mult)
    dense(c, "s5_glu", p, LATS, glu_act, glu_vec)
    dense(c, "s5_z", u, LATS, *silu_times(y5, LAT))
    residual("s5_out", y5, 120 + 16, (2,), LATS)
    normalise(c, "ln_2_1", h, 8, LAT, LATS, 1e-5, vcol("ln_g_21"), vcol("ln_b_21"))
    stored = c.sem("stored")
    with nc.Block() as block:
        @block.sync
        def _(sp):
            sp.dma_start(out.rearrange("p (k t) -> p k t", k=KD), h[:, :, 0:LAT]).then_inc(stored, 16)
            sp.wait_ge(stored, 16)


def blocks(w, per, width=128):
    k, n = w.shape
    b = w.reshape(k // 128, 128, n // (per * width), per, width)
    return np.ascontiguousarray(b.transpose(2, 1, 3, 0, 4)).reshape(n // (per * width), 128, -1)


def columns(v):
    return v.reshape(-1, 128).T


def feature_major(x):
    t, n = x.shape
    return np.ascontiguousarray(x.T.reshape(n // 128, 128, t).transpose(1, 0, 2)).reshape(128, -1)


def rope_tables():
    row, col = np.arange(LAT) // GRID_W, np.arange(LAT) % GRID_W
    out = {}
    for name, width, half in (("mla", 64, 16), ("att", 128, 32)):
        ch = np.arange(128) % width
        inv = (10000.0 ** (-(ch % half).astype(np.float64) / half)).astype(np.float32)
        pos = np.where((ch // (2 * half) % 2)[:, None] == 0, row[None, :], col[None, :]).astype(np.float32)
        ang = (pos * inv[:, None]).astype(np.float32)
        sign = np.where((ch // half) % 2 == 0, -1.0, 1.0)[:, None]
        out[name + "_trig"] = np.concatenate([np.cos(ang), np.sin(ang) * sign], 1).astype(np.float32)
        out[name + "_perm"] = np.eye(128, dtype=np.float32)[np.arange(128) ^ half]
    return out


def constants():
    i = np.arange(128)
    out = {"ones": np.ones((128, 128)), "ident": np.eye(128)}
    fwd = (i[:, None] <= i[None, :]).astype(np.float32)
    out["tri"] = np.concatenate([fwd, fwd.T], 1)
    levels = []
    for l in range(LEVELS):
        s = 1 << l
        m = (i[:, None] // (2 * s) == i[None, :] // (2 * s)) & (i[None, :] // s % 2 == 1) & (i[:, None] // s % 2 == 0)
        levels += [m, m.T]
    out["level_masks"] = np.concatenate(levels, 1)
    a, b = i[:, None], i[None, :]
    out["window_mask"] = np.concatenate([np.where(b >= a, 0, -1e30), np.zeros((128, 128)), np.where(b <= a, 0, -1e30)], 1)
    out["s5_steps"] = np.broadcast_to(np.arange(1, 129), (128, 128))
    out = {k: np.ascontiguousarray(v, dtype=np.float32) for k, v in out.items()}
    out.update(rope_tables())
    return out


def layouts(x):
    a = constants()
    a["x"], a["ctx"], a["ctx_2"] = feature_major(x["x"][0]), feature_major(x["ctx"][0]), feature_major(x["ctx_2"][0])
    a["w_mod"] = np.concatenate([blocks(w, 2) for w in (*x["w_mod"], *x["ada_w_2"])])
    w = x["mla_w_in"][0]
    a["w_mla_in"] = blocks(np.concatenate([w, w[:, 768:832]], 1), 1)
    q = x["mla_w_q_up"][0].reshape(512, HEADS, 192)
    a["w_q_up"] = blocks(np.concatenate([q[:, :, 128:].reshape(512, 512), q[:, :, :128].reshape(512, 1024)], 1), 2)
    kv = x["mla_w_kv_up"][0].reshape(256, HEADS, 256)
    a["w_k_up"] = blocks(np.ascontiguousarray(kv[:, :, :128]).reshape(256, 1024), 2)
    a["w_v_up"] = blocks(np.ascontiguousarray(kv[:, :, 128:]).reshape(256, 1024), 1, 256)
    a["w_mla_out"] = blocks(x["mla_w_out"][0], 2)
    for l in range(2):
        f = x["w_ffn_in"][l].reshape(D, 2, KF, 128).transpose(0, 2, 1, 3).reshape(D, 2 * FF)
        a[f"w_ffn_in{l}"] = blocks(f, 2)
        a[f"w_ffn_out{l}"] = blocks(x["w_ffn_out"][l], 1)
    w = x["gdn_w_in"][0]
    a["w_gdn_qkv"], a["w_gdn_z"], a["w_gdn_ba"] = blocks(w[:, :4096], 2), blocks(w[:, 4096:6144], 2), blocks(w[:, 6144:], 1, 64)
    a["w_gdn_out"] = blocks(x["gdn_w_out"][0], 1)
    rows = np.concatenate([x["gdn_a_log"][0].reshape(32), x["gdn_dt_bias"][0].reshape(32)])
    a["gdn_rows"] = np.ascontiguousarray(np.broadcast_to(rows, (128, 64)))
    w = x["attn_w_in_2"][0]
    a["w_att_qk"], a["w_att_v"], a["w_att_z"] = blocks(w[:, :2560], 2), blocks(w[:, 2560:3072], 1, 256), blocks(w[:, 3072:], 2)
    a["w_att_out"], a["w_s5_out"] = blocks(x["w_out_2"][0], 1), blocks(x["w_out_2"][1], 1)
    w = x["s5_w_in_2"][0]
    a["w_s5_in"], a["w_s5_z"] = blocks(w[:, :2048], 2), blocks(w[:, 2048:], 2)
    a["w_s5_glu"] = blocks(x["s5_glu_w_2"][0], 1)
    st = lambda v: v.reshape(2, 16, 4, 128).transpose(3, 1, 0, 2).reshape(128, 128)
    step = np.repeat(x["s5_log_step_2"][0][:, :, None], 64, 2)
    a["s5_lam"] = np.concatenate([st(x["s5_lam_re_2"][0]), st(x["s5_lam_im_2"][0]), st(step)], 1)
    b = np.stack([x["s5_b_re_2"][0], x["s5_b_im_2"][0]]).reshape(2, 2, 16, 4, 2, 64, 16)
    bm = np.zeros((16, 4, 2, 16, 2, 2, 2, 64), np.float32)
    cm = np.zeros((16, 2, 64, 2, 4, 2, 2, 16), np.float32)
    cc = np.stack([x["s5_c_re_2"][0], x["s5_c_im_2"][0]]).reshape(2, 2, 16, 4, 2, 16, 64)
    for g in range(2):
        bm[:, :, g, :, :, :, g, :] = b[:, :, :, :, g].transpose(2, 3, 5, 1, 0, 4)
        cm[:, g, :, :, :, :, g, :] = cc[:, :, :, :, g].transpose(2, 5, 1, 3, 0, 4)
    a["s5_b"], a["s5_c"] = bm.reshape(16, 128, 512), cm.reshape(16, 128, 512)
    vec = {"sink": np.broadcast_to(x["attn_sink_2"][0], (128, 16)), "c": columns(x["c"][0]), "c_ctx": columns(x["c_ctx"]),
           "c_2": columns(x["c_2"][0]), "c_ctx_2": columns(x["c_ctx_2"]), "mla_q_norm": columns(x["mla_q_norm"][0]),
           "mla_kv_norm": columns(x["mla_kv_norm"][0]), "gdn_norm": columns(x["gdn_norm"][0]), "s5_d": columns(x["s5_d_2"][0]),
           "s5_glu_b": columns(x["s5_glu_b_2"][0])}
    for l in range(2):
        for n in ("b_mod", "ln1_g", "ln1_b", "ln2_g", "ln2_b", "ada_b_2", "ln_g_2", "ln_b_2"):
            vec[f"{n}{l}"] = columns(x[n][l])
    vec["gdn_taps"] = x["gdn_conv"][0].T.reshape(32, 128, 5).transpose(1, 0, 2).reshape(128, 160)
    a["vecs"] = np.concatenate([vec[n] for n, _ in VECS], 1)
    return {k: np.ascontiguousarray(v) for k, v in a.items()}


def kernel(**inputs):
    import concourse.bacc as bacc
    from concourse.bass_utils import run_bass_kernel_spmd
    names = [n for n, v in inputs.items() if v.size]
    arrays = layouts({n: np.asarray(inputs[n]) for n in names})
    nc = bacc.Bacc("TRN2", target_bir_lowering=False, num_devices=1)
    ins = {n: nc.dram_tensor("in_" + n, v.shape, F32, kind="ExternalInput").ap() for n, v in arrays.items()}
    out = nc.dram_tensor("out", (128, KD * LAT), F32, kind="ExternalOutput").ap()
    program(nc, ins, out)
    r = run_bass_kernel_spmd(nc, [{"in_" + n: v for n, v in arrays.items()}], core_ids=[0])
    y = r.results[0]["out"].reshape(128, KD, LAT)
    return np.ascontiguousarray(y.transpose(2, 1, 0)).reshape(1, LAT, D)
```
